# Optimizing a Trainium2 kernel written in Bass

```python
import jax, jax.numpy as jnp
from jax import lax
import numpy as np
import math

D_MODEL = 1024
BATCH = 1
SEQ = 256
DEPTH = 2

CHUNK = 64
N_A_LAYERS = DEPTH // 2
N_B_LAYERS = DEPTH - N_A_LAYERS
GMLP_BLOCK = 128
GMLP_WIDTH = D_MODEL
GMLP_GROUPS = 8
GMLP_GROUP_DIM = GMLP_WIDTH // GMLP_GROUPS
N_HEADS = 16
HEAD_DIM = D_MODEL // N_HEADS
LEFT_CHUNKS = 8
BAND = (LEFT_CHUNKS + 1) * CHUNK
PAD = LEFT_CHUNKS * CHUNK
REL_CLIP = 128
REL_SIZE = 2 * REL_CLIP + 1
D_FF = ((8 * D_MODEL // 3 + 127) // 128) * 128
CONV_WIDTH = 3
EPS = 1e-6
NEG_INF = -1e30


def rmsnorm(x, g):
    xf = x.astype(jnp.float32)
    y = xf * lax.rsqrt(jnp.mean(xf * xf, axis=-1, keepdims=True) + EPS)
    return (y * g.astype(jnp.float32)).astype(x.dtype)

def gmlp_mixer(h, w_in, v_norm_g, w_s, b_s, w_out):
    B, S, _ = h.shape
    z = jax.nn.gelu(h @ w_in)
    u, v = jnp.split(z, 2, axis=-1)
    v = rmsnorm(v, v_norm_g)
    pos_chunk = jnp.arange(GMLP_BLOCK) // CHUNK
    mask = pos_chunk[:, None] >= pos_chunk[None, :]
    w = jnp.where(mask[None], w_s, 0)
    v = v.reshape(B, S // GMLP_BLOCK, GMLP_BLOCK, GMLP_GROUPS, GMLP_GROUP_DIM)
    s = jnp.einsum('gij,bnjgc->bnigc', w, v) + b_s.T[None, None, :, :, None]
    out = u * s.reshape(B, S, GMLP_WIDTH)
    return out @ w_out

def chunk_attention(h, k, v, w_q, rel_bias, w_o):
    B, S, _ = h.shape
    nc = S // CHUNK
    scale = HEAD_DIM ** -0.5
    q = (h @ w_q).reshape(B, nc, CHUNK, N_HEADS, HEAD_DIM) * scale
    qc = jnp.moveaxis(q, 1, 0)
    kp = jnp.pad(k, ((0, 0), (PAD, 0), (0, 0), (0, 0)))
    vp = jnp.pad(v, ((0, 0), (PAD, 0), (0, 0), (0, 0)))
    qi = jnp.arange(CHUNK)[:, None]
    kj = jnp.arange(BAND)[None, :]
    rel_idx = jnp.clip(qi - kj + PAD, -REL_CLIP, REL_CLIP) + REL_CLIP
    bias = rel_bias[:, rel_idx].astype(jnp.float32)

    def one_chunk(args):
        c, qb = args
        start = c * CHUNK
        kb = lax.dynamic_slice_in_dim(kp, start, BAND, axis=1)
        vb = lax.dynamic_slice_in_dim(vp, start, BAND, axis=1)
        sc = jnp.einsum('bqhd,bkhd->bhqk', qb, kb).astype(jnp.float32) + bias
        valid = (start - PAD + jnp.arange(BAND)) >= 0
        sc = jnp.where(valid[None, None, None, :], sc, NEG_INF)
        p = jax.nn.softmax(sc, axis=-1).astype(vb.dtype)
        return jnp.einsum('bhqk,bkhd->bqhd', p, vb)

    o = lax.map(one_chunk, (jnp.arange(nc), qc))
    o = jnp.moveaxis(o, 0, 1).reshape(B, S, N_HEADS * HEAD_DIM)
    return o @ w_o

def conv_ffn(h, w_in, conv_w, conv_b, w_down):
    a = h @ w_in
    C = a.shape[-1]
    a = lax.conv_general_dilated(
        a, conv_w[:, None, :].astype(a.dtype), window_strides=(1,),
        padding=[(CONV_WIDTH - 1, 0)], dimension_numbers=('NWC', 'WIO', 'NWC'),
        feature_group_count=C) + conv_b
    up, gate = jnp.split(a, 2, axis=-1)
    return (jax.nn.silu(gate) * up) @ w_down

def first_inputs(seed: int = 0) -> dict:
    key = jax.random.key(seed)
    ks = jax.random.split(key, 20)
    nrm = lambda k, shape, s: jax.random.normal(k, shape, jnp.float32) * s
    gain = lambda k, shape: 1.0 + nrm(k, shape, 0.02)
    HD = N_HEADS * HEAD_DIM
    return {
        "x": nrm(ks[0], (BATCH, SEQ, D_MODEL), 1.0),
        "a_norm_g": gain(ks[1], (N_A_LAYERS, D_MODEL)),
        "a_w_in": nrm(ks[2], (N_A_LAYERS, D_MODEL, 2 * GMLP_WIDTH), D_MODEL ** -0.5),
        "a_v_norm_g": gain(ks[3], (N_A_LAYERS, GMLP_WIDTH)),
        "a_w_s": nrm(ks[4], (N_A_LAYERS, GMLP_GROUPS, GMLP_BLOCK, GMLP_BLOCK), GMLP_BLOCK ** -0.5),
        "a_b_s": 1.0 + nrm(ks[5], (N_A_LAYERS, GMLP_GROUPS, GMLP_BLOCK), 0.01),
        "a_w_out": nrm(ks[6], (N_A_LAYERS, GMLP_WIDTH, D_MODEL), GMLP_WIDTH ** -0.5),
        "kv_norm_g": gain(ks[7], (D_MODEL,)),
        "w_kv": nrm(ks[8], (D_MODEL, 2 * HD), D_MODEL ** -0.5),
        "b_norm_g": gain(ks[9], (N_B_LAYERS, D_MODEL)),
        "b_w_q": nrm(ks[10], (N_B_LAYERS, D_MODEL, HD), D_MODEL ** -0.5),
        "b_rel_bias": nrm(ks[11], (N_B_LAYERS, N_HEADS, REL_SIZE), 0.5),
        "b_w_o": nrm(ks[12], (N_B_LAYERS, HD, D_MODEL), HD ** -0.5),
        "f_norm_g": gain(ks[13], (DEPTH, D_MODEL)),
        "f_w_in": nrm(ks[14], (DEPTH, D_MODEL, 2 * D_FF), D_MODEL ** -0.5),
        "f_conv_w": nrm(ks[15], (DEPTH, CONV_WIDTH, 2 * D_FF), CONV_WIDTH ** -0.5),
        "f_conv_b": nrm(ks[16], (DEPTH, 2 * D_FF), 0.01),
        "f_w_down": nrm(ks[17], (DEPTH, D_FF, D_MODEL), D_FF ** -0.5),
        "final_norm_g": gain(ks[18], (D_MODEL,)),
    }

def first_block(x, a_norm_g, a_w_in, a_v_norm_g, a_w_s, a_b_s, a_w_out,
              kv_norm_g, w_kv, b_norm_g, b_w_q, b_rel_bias, b_w_o,
              f_norm_g, f_w_in, f_conv_w, f_conv_b, f_w_down, final_norm_g):
    B, S, _ = x.shape
    h = x
    k_shared = v_shared = None
    for l in range(DEPTH):
        if l < N_A_LAYERS:
            h = h + gmlp_mixer(rmsnorm(h, a_norm_g[l]), a_w_in[l], a_v_norm_g[l],
                               a_w_s[l], a_b_s[l], a_w_out[l])
        else:
            if l == N_A_LAYERS:
                kv = rmsnorm(h, kv_norm_g) @ w_kv
                k_shared, v_shared = jnp.split(kv, 2, axis=-1)
                k_shared = k_shared.reshape(B, S, N_HEADS, HEAD_DIM)
                v_shared = v_shared.reshape(B, S, N_HEADS, HEAD_DIM)
            j = l - N_A_LAYERS
            h = h + chunk_attention(rmsnorm(h, b_norm_g[j]), k_shared, v_shared,
                                    b_w_q[j], b_rel_bias[j], b_w_o[j])
        h = h + conv_ffn(rmsnorm(h, f_norm_g[l]), f_w_in[l], f_conv_w[l],
                         f_conv_b[l], f_w_down[l])
    return rmsnorm(h, final_norm_g)


PLE_DIM = 256
SB_HEADS = 8
SB_HEAD_DIM = 64
SB_WIDTH = SB_HEADS * SB_HEAD_DIM
RW_HEADS = 8
RW_HEAD_DIM = 64
RW_WIDTH = RW_HEADS * RW_HEAD_DIM
RW_DECAY_LORA = 64
RW_AAA_LORA = 64
RW_GATE_LORA = 160
RW_GN_EPS = 64e-5
RW_IN = 3 * RW_WIDTH + RW_DECAY_LORA + RW_AAA_LORA + RW_GATE_LORA
HYB_IN = 3 * SB_WIDTH + RW_IN
HYB_OUT = SB_WIDTH + RW_WIDTH
MLA_HEADS = 16
MLA_NOPE = 64
MLA_ROPE = 32
MLA_V = 64
MLA_Q_RANK = 384
MLA_KV_RANK = 256
MLA_DOWN = MLA_Q_RANK + MLA_KV_RANK + MLA_ROPE
ROPE_THETA = 10000.0
FFN_DIM = 2816
Q_BLOCK = 128
NORM_EPS = 1e-6
N_EVEN = (DEPTH + 1) // 2
N_ODD = DEPTH // 2


F32 = jnp.float32

def rmsnorm_2(x, g):
    xf = x.astype(F32)
    y = xf * lax.rsqrt(jnp.mean(xf * xf, axis=-1, keepdims=True) + NORM_EPS)
    return (y * g.astype(F32)).astype(x.dtype)

def shift_right(x, n):
    return jnp.pad(x, ((0, 0), (n, 0), (0, 0)))[:, : x.shape[1]]

def sweep_query_blocks(fn, q):
    b, s, h, e = q.shape
    nb = s // Q_BLOCK
    qb = q.reshape(b, nb, Q_BLOCK, h, e).transpose(1, 0, 2, 3, 4)
    starts = jnp.arange(nb, dtype=jnp.int32) * Q_BLOCK
    out = lax.map(lambda args: fn(args[0], args[1]), (qb, starts))
    return out.transpose(1, 0, 2, 3, 4).reshape(b, s, h, out.shape[-1])

def stick_breaking_attention(q, k, v):
    s_len = k.shape[1]
    scale = 1.0 / math.sqrt(q.shape[-1])
    key_pos = jnp.arange(s_len, dtype=jnp.int32)
    kf = k.astype(F32)
    vf = v.astype(F32)

    def block(qb, t0):
        z = jnp.einsum('bqhe,bshe->bhqs', qb.astype(F32), kf) * scale
        qpos = t0 + jnp.arange(Q_BLOCK, dtype=jnp.int32)
        mask = key_pos[None, :] < qpos[:, None]
        log_one_minus = jnp.where(mask, -jax.nn.softplus(z), 0.0)
        rev = lax.cumsum(log_one_minus, axis=3, reverse=True)
        after = jnp.concatenate([rev[..., 1:], jnp.zeros_like(rev[..., :1])], axis=3)
        w = jnp.where(mask, jnp.exp(jax.nn.log_sigmoid(z) + after), 0.0)
        return jnp.einsum('bhqs,bshe->bqhe', w, vf)

    return sweep_query_blocks(block, q).astype(v.dtype)

def causal_softmax_attention(q, k, v, scale):
    s_len = k.shape[1]
    key_pos = jnp.arange(s_len, dtype=jnp.int32)
    kf = k.astype(F32)
    vf = v.astype(F32)

    def block(qb, t0):
        sc = jnp.einsum('bqhe,bshe->bhqs', qb.astype(F32), kf) * scale
        qpos = t0 + jnp.arange(Q_BLOCK, dtype=jnp.int32)
        mask = key_pos[None, :] <= qpos[:, None]
        w = jax.nn.softmax(jnp.where(mask, sc, -jnp.inf), axis=-1)
        return jnp.einsum('bhqs,bshe->bqhe', w, vf)

    return sweep_query_blocks(block, q).astype(v.dtype)

def apply_rope(x, positions):
    half = x.shape[-1] // 2
    inv_freq = ROPE_THETA ** (-jnp.arange(half, dtype=F32) / half)
    ang = positions.astype(F32)[:, :, None, None] * inv_freq
    cos, sin = jnp.cos(ang), jnp.sin(ang)
    xf = x.astype(F32)
    x1, x2 = xf[..., :half], xf[..., half:]
    return jnp.concatenate([x1 * cos - x2 * sin, x1 * sin + x2 * cos], axis=-1).astype(x.dtype)

def rwkv7_time_mix(proj, mu, w0, w2, a0, a2, g2, k_k, k_a, r_k, ln_w, ln_b):
    b, s, _ = proj.shape
    pf = proj.astype(F32)
    xm = pf + (shift_right(pf, 1) - pf) * mu
    r, k, v, wl, al, gl = jnp.split(
        xm, [RW_WIDTH, 2 * RW_WIDTH, 3 * RW_WIDTH, 3 * RW_WIDTH + RW_DECAY_LORA,
             3 * RW_WIDTH + RW_DECAY_LORA + RW_AAA_LORA], axis=-1)
    w = -jax.nn.softplus(-(w0 + jnp.tanh(wl) @ w2)) - 0.5
    decay = jnp.exp(-jnp.exp(w))
    a = jax.nn.sigmoid(a0 + al @ a2)
    g = jax.nn.sigmoid(gl) @ g2

    hd = lambda t: t.reshape(b, s, RW_HEADS, RW_HEAD_DIM)
    ph = lambda t: t.astype(F32).reshape(RW_HEADS, RW_HEAD_DIM)
    r, k, v, decay, a = hd(r), hd(k), hd(v), hd(decay), hd(a)
    kk = k * ph(k_k)
    kk = kk * lax.rsqrt(jnp.maximum(jnp.sum(kk * kk, axis=-1, keepdims=True), 1e-24))
    k = k * (1.0 + (a - 1.0) * ph(k_a))

    def step(state, inp):
        r_t, w_t, k_t, v_t, kk_t, a_t = inp
        sa = jnp.einsum('bhij,bhj->bhi', state, -kk_t)
        state = (state * w_t[:, :, None, :] + sa[..., None] * (kk_t * a_t)[:, :, None, :]
                 + v_t[..., None] * k_t[:, :, None, :])
        return state, jnp.einsum('bhij,bhj->bhi', state, r_t)

    tm = lambda t: jnp.moveaxis(t, 1, 0)
    state0 = jnp.zeros((b, RW_HEADS, RW_HEAD_DIM, RW_HEAD_DIM), F32)
    _, y = lax.scan(step, state0, (tm(r), tm(decay), tm(k), tm(v), tm(kk), tm(a)))
    y = jnp.moveaxis(y, 0, 1)

    mean = jnp.mean(y, axis=-1, keepdims=True)
    var = jnp.mean(jnp.square(y - mean), axis=-1, keepdims=True)
    y = (y - mean) * lax.rsqrt(var + RW_GN_EPS)
    y = y * ph(ln_w) + ph(ln_b)
    y = y + jnp.sum(r * k * r_k.astype(F32), axis=-1, keepdims=True) * v
    return (y.reshape(b, s, RW_WIDTH) * g).astype(proj.dtype)

def sb_rwkv_mixer(hn, w_in, w_out, mu, w0, w2, a0, a2, g2, k_k, k_a, r_k, ln_w, ln_b):
    b, s, _ = hn.shape
    proj = hn @ w_in
    qa, ka, va, rw = jnp.split(proj, [SB_WIDTH, 2 * SB_WIDTH, 3 * SB_WIDTH], axis=-1)
    hd = lambda t: t.reshape(b, s, SB_HEADS, SB_HEAD_DIM)
    o_a = stick_breaking_attention(hd(qa), hd(ka), hd(va)).reshape(b, s, SB_WIDTH)
    o_b = rwkv7_time_mix(rw, mu, w0, w2, a0, a2, g2, k_k, k_a, r_k, ln_w, ln_b)
    return jnp.concatenate([o_a, o_b.astype(o_a.dtype)], axis=-1) @ w_out

def mla_mixer(hn, positions, w_down, q_norm, kv_norm, w_uq, w_ukv, w_o):
    b, s, _ = hn.shape
    c = hn @ w_down
    cq, ckv, kr = jnp.split(c, [MLA_Q_RANK, MLA_Q_RANK + MLA_KV_RANK], axis=-1)
    q = (rmsnorm_2(cq, q_norm) @ w_uq).reshape(b, s, MLA_HEADS, MLA_NOPE + MLA_ROPE)
    kv = (rmsnorm_2(ckv, kv_norm) @ w_ukv).reshape(b, s, MLA_HEADS, MLA_NOPE + MLA_V)
    q_nope, q_rope = jnp.split(q, [MLA_NOPE], axis=-1)
    k_nope, v = jnp.split(kv, [MLA_NOPE], axis=-1)
    q = jnp.concatenate([q_nope, apply_rope(q_rope, positions)], axis=-1)
    k_rope = jnp.broadcast_to(apply_rope(kr[:, :, None, :], positions), (b, s, MLA_HEADS, MLA_ROPE))
    k = jnp.concatenate([k_nope, k_rope], axis=-1)
    o = causal_softmax_attention(q, k, v, 1.0 / math.sqrt(MLA_NOPE + MLA_ROPE))
    return o.reshape(b, s, MLA_HEADS * MLA_V) @ w_o

def conv_glu(hn, w_in, conv_w, conv_b, w_out):
    u, gate_in = jnp.split(hn @ w_in, 2, axis=-1)
    c = (conv_w[0] * shift_right(gate_in, 2) + conv_w[1] * shift_right(gate_in, 1)
         + conv_w[2] * gate_in + conv_b)
    return (jax.nn.gelu(c, approximate=False) * u) @ w_out

def second_inputs(seed: int = 0) -> dict:
    key = jax.random.key(seed)
    keys = jax.random.split(key, 48)
    counter = [0]

    def nk():
        kk = keys[counter[0]]
        counter[0] += 1
        return kk

    def nrm(shape, scale):
        return jax.random.normal(nk(), shape, F32) * scale

    def gain(shape):
        return 1.0 + nrm(shape, 0.05)

    x = nrm((BATCH, SEQ, D_MODEL), 1.0)
    p = nrm((DEPTH, BATCH, SEQ, PLE_DIM), 1.0)
    offset = jax.random.randint(nk(), (BATCH, 1), 0, 4096, dtype=jnp.int32)
    positions = offset + jnp.arange(SEQ, dtype=jnp.int32)[None, :]
    return {
        "x": x,
        "p": p,
        "positions": positions,
        "attn_norm": gain((DEPTH, D_MODEL)),
        "ffn_norm": gain((DEPTH, D_MODEL)),
        "ffn_w_in": nrm((DEPTH, D_MODEL, 2 * FFN_DIM), D_MODEL ** -0.5),
        "ffn_conv_w": nrm((DEPTH, CONV_WIDTH, FFN_DIM), CONV_WIDTH ** -0.5),
        "ffn_conv_b": nrm((DEPTH, FFN_DIM), 0.01),
        "ffn_w_out": nrm((DEPTH, FFN_DIM, D_MODEL), FFN_DIM ** -0.5),
        "ple_w_proj": nrm((DEPTH, PLE_DIM, D_MODEL), PLE_DIM ** -0.5),
        "ple_norm": gain((DEPTH, D_MODEL)),
        "ple_gate_norm": gain((DEPTH, D_MODEL)),
        "ple_w_gate": nrm((DEPTH, D_MODEL, D_MODEL), D_MODEL ** -0.5),
        "hyb_w_in": nrm((N_EVEN, D_MODEL, HYB_IN), D_MODEL ** -0.5),
        "hyb_w_out": nrm((N_EVEN, HYB_OUT, D_MODEL), HYB_OUT ** -0.5),
        "rw_mu": jax.random.uniform(nk(), (N_EVEN, RW_IN), F32),
        "rw_w0": jax.random.uniform(nk(), (N_EVEN, RW_WIDTH), F32, -6.0, 1.0),
        "rw_w2": nrm((N_EVEN, RW_DECAY_LORA, RW_WIDTH), RW_DECAY_LORA ** -0.5),
        "rw_a0": nrm((N_EVEN, RW_WIDTH), 0.1),
        "rw_a2": nrm((N_EVEN, RW_AAA_LORA, RW_WIDTH), RW_AAA_LORA ** -0.5),
        "rw_g2": nrm((N_EVEN, RW_GATE_LORA, RW_WIDTH), RW_GATE_LORA ** -0.5),
        "rw_k_k": 0.85 + nrm((N_EVEN, RW_WIDTH), 0.05),
        "rw_k_a": gain((N_EVEN, RW_WIDTH)),
        "rw_r_k": nrm((N_EVEN, RW_HEADS, RW_HEAD_DIM), 0.1),
        "rw_ln_w": gain((N_EVEN, RW_WIDTH)),
        "rw_ln_b": nrm((N_EVEN, RW_WIDTH), 0.01),
        "mla_w_down": nrm((N_ODD, D_MODEL, MLA_DOWN), D_MODEL ** -0.5),
        "mla_q_norm": gain((N_ODD, MLA_Q_RANK)),
        "mla_kv_norm": gain((N_ODD, MLA_KV_RANK)),
        "mla_w_uq": nrm((N_ODD, MLA_Q_RANK, MLA_HEADS * (MLA_NOPE + MLA_ROPE)), MLA_Q_RANK ** -0.5),
        "mla_w_ukv": nrm((N_ODD, MLA_KV_RANK, MLA_HEADS * (MLA_NOPE + MLA_V)), MLA_KV_RANK ** -0.5),
        "mla_w_o": nrm((N_ODD, MLA_HEADS * MLA_V, D_MODEL), (MLA_HEADS * MLA_V) ** -0.5),
        "final_norm": gain((D_MODEL,)),
    }

def second_block(x, p, positions, attn_norm, ffn_norm, ffn_w_in, ffn_conv_w, ffn_conv_b, ffn_w_out,
              ple_w_proj, ple_norm, ple_gate_norm, ple_w_gate,
              hyb_w_in, hyb_w_out, rw_mu, rw_w0, rw_w2, rw_a0, rw_a2, rw_g2, rw_k_k, rw_k_a,
              rw_r_k, rw_ln_w, rw_ln_b,
              mla_w_down, mla_q_norm, mla_kv_norm, mla_w_uq, mla_w_ukv, mla_w_o, final_norm):
    h = x
    for i in range(DEPTH):
        j = i // 2
        hn = rmsnorm_2(h, attn_norm[i])
        if i % 2 == 0:
            mix = sb_rwkv_mixer(hn, hyb_w_in[j], hyb_w_out[j], rw_mu[j], rw_w0[j], rw_w2[j],
                                rw_a0[j], rw_a2[j], rw_g2[j], rw_k_k[j], rw_k_a[j], rw_r_k[j],
                                rw_ln_w[j], rw_ln_b[j])
        else:
            mix = mla_mixer(hn, positions, mla_w_down[j], mla_q_norm[j], mla_kv_norm[j],
                            mla_w_uq[j], mla_w_ukv[j], mla_w_o[j])
        h = h + mix
        h = h + conv_glu(rmsnorm_2(h, ffn_norm[i]), ffn_w_in[i], ffn_conv_w[i], ffn_conv_b[i], ffn_w_out[i])
        e = rmsnorm_2(p[i] @ ple_w_proj[i], ple_norm[i])
        gate = jax.nn.sigmoid(rmsnorm_2(h, ple_gate_norm[i]) @ ple_w_gate[i])
        h = h + gate * e
    return rmsnorm_2(h, final_norm)


def setup_inputs(seed=0):
    out = dict(first_inputs(seed))
    for name, value in second_inputs(seed + 1).items():
        if name != "x":
            out[name + "_2"] = value
    return out


def reference(
    x, a_norm_g, a_w_in, a_v_norm_g, a_w_s, a_b_s, a_w_out, kv_norm_g, w_kv, b_norm_g, b_w_q,
    b_rel_bias, b_w_o, f_norm_g, f_w_in, f_conv_w, f_conv_b, f_w_down, final_norm_g, p_2,
    positions_2, attn_norm_2, ffn_norm_2, ffn_w_in_2, ffn_conv_w_2, ffn_conv_b_2, ffn_w_out_2,
    ple_w_proj_2, ple_norm_2, ple_gate_norm_2, ple_w_gate_2, hyb_w_in_2, hyb_w_out_2, rw_mu_2,
    rw_w0_2, rw_w2_2, rw_a0_2, rw_a2_2, rw_g2_2, rw_k_k_2, rw_k_a_2, rw_r_k_2, rw_ln_w_2,
    rw_ln_b_2, mla_w_down_2, mla_q_norm_2, mla_kv_norm_2, mla_w_uq_2, mla_w_ukv_2, mla_w_o_2,
    final_norm_2,
):
    x = first_block(
        x, a_norm_g, a_w_in, a_v_norm_g, a_w_s, a_b_s, a_w_out, kv_norm_g, w_kv, b_norm_g,
        b_w_q, b_rel_bias, b_w_o, f_norm_g, f_w_in, f_conv_w, f_conv_b, f_w_down, final_norm_g,
    )
    return second_block(
        x, p_2, positions_2, attn_norm_2, ffn_norm_2, ffn_w_in_2, ffn_conv_w_2, ffn_conv_b_2,
        ffn_w_out_2, ple_w_proj_2, ple_norm_2, ple_gate_norm_2, ple_w_gate_2, hyb_w_in_2,
        hyb_w_out_2, rw_mu_2, rw_w0_2, rw_w2_2, rw_a0_2, rw_a2_2, rw_g2_2, rw_k_k_2, rw_k_a_2,
        rw_r_k_2, rw_ln_w_2, rw_ln_b_2, mla_w_down_2, mla_q_norm_2, mla_kv_norm_2, mla_w_uq_2,
        mla_w_ukv_2, mla_w_o_2, final_norm_2,
    )


_drawn_inputs = setup_inputs


def setup_inputs(seed=0):
    import zlib

    import numpy as np

    out = dict(_drawn_inputs(seed))
    spreads = {}
    factors = {'a_v_norm_g': 5.007,
     'a_b_s': 7.592,
     'kv_norm_g': 8.0,
     'b_norm_g': 8.0,
     'f_conv_b': 5.26,
     'ffn_conv_b_2': 8.0,
     'ple_gate_norm_2': 5.866,
     'rw_a0_2': 4.227,
     'rw_k_k_2': 2.999,
     'rw_ln_w_2': 3.168,
     'rw_ln_b_2': 8.0,
     'mla_q_norm_2': 8.0,
     'mla_kv_norm_2': 5.198}
    for name, (base, spread) in spreads.items():
        noise = np.random.default_rng([zlib.crc32(name.encode()), seed]).standard_normal(out[name].shape)
        drawn = base * np.exp(spread * noise) if base else spread * noise
        out[name] = __import__('jax').numpy.asarray(drawn.astype(out[name].dtype))
    for name, factor in factors.items():
        out[name] = (out[name] * factor).astype(out[name].dtype)
    return out
```

```python
from contextlib import ExitStack

import numpy as np

import concourse.bass as bass
from concourse import mybir

F32 = mybir.dt.float32
F32R = mybir.dt.float32r
I32 = mybir.dt.int32
ALU = mybir.AluOpType
ACT = mybir.ActivationFunctionType
AX_X = mybir.AxisListType.X

P = 128
T = 256
D = 1024
KD = D // P
FF = 2816
KF = FF // P
PAIRS = KF // 2
CHUNK = 16 * P
RING = 4
AHEAD = 3
EPS = 1e-6
GN_EPS = 64e-5
NEG = -1e30
HCON = 6 * 128 + 6 * 64
HEADS = 16
SB_HEADS = 8
RBLK = 4
RCH = 64
NRCH = T // RCH
MLA_SCALE = 96 ** -0.5
DECAY = -float(np.exp(np.float64(-0.5)))

_PLAN = [("gm_v", 4), ("gm_u", 4), ("gm_o", 4), ("up0", 22), ("dn0", 11),
         ("at_k", 4), ("at_v", 4), ("at_q", 4), ("at_o", 4), ("up1", 22), ("dn1", 11),
         ("hy", 14), ("hy_o", 4), ("up2", 22), ("dn2", 11), ("pl_p0", 1), ("pl_g0", 4),
         ("ml_d", 3), ("ml_q", 3), ("ml_k", 2), ("ml_v", 1), ("ml_o", 4),
         ("up3", 22), ("dn3", 11), ("pl_p1", 1), ("pl_g1", 4)]
C0, NCH = {}, 0
for _name, _n in _PLAN:
    C0[_name] = NCH
    NCH += _n

_VECS = [("a_norm", 8), ("a_vnorm", 8), ("kv_norm", 8), ("b_norm", 8), ("f_norm0", 8), ("f_norm1", 8),
         ("cw0", 132), ("cw1", 132), ("cb0", 44), ("cb1", 44), ("fin1", 8),
         ("at_norm0", 8), ("at_norm1", 8), ("ff_norm0", 8), ("ff_norm1", 8),
         ("cw2", 66), ("cw3", 66), ("cb2", 22), ("cb3", 22),
         ("pl_norm0", 8), ("pl_norm1", 8), ("pl_gnorm0", 8), ("pl_gnorm1", 8),
         ("rw_mu", 15), ("rw_a0", 4), ("rw_kk", 4), ("rw_ka", 4), ("rw_rk", 4), ("rw_lnw", 4), ("rw_lnb", 4),
         ("q_norm", 3), ("c_norm", 2), ("fin2", 8),
         ("eps", 1), ("gn_eps", 1), ("freq", 1), ("turn", 1), ("phase", 1), ("ln256", 1)]
VC, NV = {}, 0
for _name, _n in _VECS:
    VC[_name] = NV
    NV += _n

OUT_GM, OUT_GATED, OUT_FF0, OUT_KV, OUT_Q, OUT_FF1, OUT_HY, OUT_FF2, OUT_PL0, OUT_ML, OUT_FF3, OUT_PL1 = range(12)
N_GM, N_FF0, N_AT, N_FF1, N_FIN1, N_HY, N_FF2, N_PL0, N_ML, N_FF3, N_PL1, N_FIN2 = range(12)

FINAL_XT = 8 * 13
EVACS = {4: 2, 8: 2, 14: 2, 16: 2}


def build(nc, stream, x_t, vecs, wst, bsp, rel, hyc, w0, lora, mlc, pos, p_t, out):
    with ExitStack() as ctx:
        def sem(name):
            return ctx.enter_context(nc.semaphore(name))

        def sb(name, shape, dt=F32, where=ctx):
            return where.enter_context(nc.sbuf_tensor(name, shape, dt))

        raw = [sb(f"raw{i}", [P, CHUNK]) for i in range(RING)]
        w_hi = [sb(f"w_hi{i}", [P, CHUNK], F32R) for i in range(RING)]
        w_lo = [sb(f"w_lo{i}", [P, CHUNK], F32R) for i in range(RING)]
        hT = sb("hT", [P, KD, T])
        vec = sb("vec", [P, NV])
        eye_ones = sb("eye_ones", [P, 2 * P])
        rs = sb("rs", [P, T])
        std = sb("std", [P, T])
        xB = sb("xB", [P, KD, 2, T], F32R)
        with ExitStack() as ph:
            xt = sb("xt", [P, KD, T], where=ph)
            xA = sb("xA", [P, KD, 2, T], F32R, ph)
            with ExitStack() as f:
                hid = sb("hid", [P, KF, 2, T], F32R, f)
                up_acc = [sb(f"up_acc{i}", [P, 2, T], where=f) for i in range(2)]
                gate_acc = [sb(f"gate_acc{i}", [P, 2, T], where=f) for i in range(2)]
            with ExitStack() as f:
                uT = sb("uT", [P, KD, T], where=f)
                vnat = sb("vnat", [P, 2, D], where=f)
                wsT = sb("wsT", [P, KD, P], where=f)
                bsb = sb("bsb", [P, KD, P], where=f)
                gm_junk = sb("gm_junk", [P, T], where=f)
                gm_sum = sb("gm_sum", [P, 8], where=f)
                gm_rs = sb("gm_rs", [P, 4], where=f)
            with ExitStack() as f:
                at_qT = sb("at_qT", [P, KD, T], where=f)
                at_k = sb("at_k", [P, HEADS, T], where=f)
                at_v = sb("at_v", [P, 2, D], where=f)
                at_bias = sb("at_bias", [P, HEADS, T], where=f)
                at_pr = [sb(f"at_pr{i}", [P, 384], where=f) for i in range(2)]
                at_pt = [sb(f"at_pt{i}", [P, 384], where=f) for i in range(2)]
                at_st = sb("at_st", [P, 4, 2 * HEADS], where=f)
            with ExitStack() as f:
                ml_q = sb("ml_q", [P, HEADS, T], where=f)
                ml_k = sb("ml_k", [P, HEADS, T], where=f)
                ml_v = sb("ml_v", [P, 2, D], where=f)
                ml_c = sb("ml_c", [P, 5, T], where=f)
                ml_rs = sb("ml_rs", [P, 2, T], where=f)
                ml_pr = [sb(f"ml_pr{i}", [P, 384], where=f) for i in range(2)]
                ml_pt = [sb(f"ml_pt{i}", [P, 384], where=f) for i in range(2)]
                ml_st = sb("ml_st", [P, 4, 2 * HEADS], where=f)
                ml_con = sb("ml_con", [P, 384], where=f)
                ml_cs = sb("ml_cs", [P, T], where=f)
                ml_pos = sb("ml_pos", [P, T], I32, f)
                ml_kr = sb("ml_kr", [P, T], where=f)
            ml_bias, ml_fold = ml_con[:, 0:256], ml_con[:, 256:384]
            ml_ang, ml_n = ml_pr[0][:, 0:T], ml_pr[1][:, 0:T]
            with ExitStack() as f:
                pl_in = sb("pl_in", [P, 2, T], where=f)
                pl_x = sb("pl_x", [P, 2, 2, T], F32R, f)
                pl_e = sb("pl_e", [P, KD, T], where=f)
                pl_sq = sb("pl_sq", [P, KD, T], where=f)
                pl_rs = sb("pl_rs", [P, T], where=f)
                pl_sg = [sb(f"pl_sg{i}", [P, 2, T], where=f) for i in range(2)]
            with ExitStack() as f:
                hcon = sb("hcon", [P, HCON], where=f)
                w0b = sb("w0b", [P, 512], where=f)
                wlal = sb("wlal", [P, T], where=f)
                gl = sb("gl", [P, 2, T], where=f)
                pend = sb("pend", [P, RBLK, NRCH], where=f)
                om_mu = sb("om_mu", [P, 15], where=f)
                slot = [sb(f"slot{i}", [P, RBLK, T], where=f) for i in range(3)]
                with ExitStack() as g:
                    sb_q = sb("sb_q", [P, RBLK, T], where=g)
                    sb_k = sb("sb_k", [P, SB_HEADS, T], where=g)
                    sb_v = sb("sb_v", [P, 2, 512], where=g)
                    sb_l = [sb(f"sb_l{i}", [P, 2, 384], where=g) for i in range(2)]
                    sb_ls = [sb(f"sb_ls{i}", [P, 2, 384], where=g) for i in range(2)]
                    sb_lm = sb("sb_lm", [P, 2, 384], where=g)
                slot += [sb(f"slot{i}", [P, RBLK, T], where=f) for i in range(3, 12)]
        with ExitStack() as f:
            lora_w = sb("lora_w", [P, 4, 512], where=f)
            slot += [sb(f"slot{i}", [P, RBLK, T], where=f) for i in range(12, 16)]
        h_after, h_tri, h_sum, h_mean = [hcon[:, P * i:P * i + P] for i in range(4)]
        h_cum = hcon[:, 4 * P:6 * P]
        m_d, m_dt, m_ot, m_strict, m_incl = [hcon[:, 6 * P + 64 * i:6 * P + 64 * i + 64] for i in range(5)]
        ps = ctx.enter_context(nc.psum_tensor("ps", [P, 8, 512], F32))

        eye, ones = eye_ones[:, 0:P], eye_ones[:, P:2 * P]

        def half(bank, h):
            return ps[:, bank, T * h:T * h + T]

        def col(name, j=0, n=1):
            return vec[:, VC[name] + j:VC[name] + j + n]

        def dcol(name, j, off):
            if isinstance(j, int):
                return col(name, off + j)
            return vec[:, bass.ds(j + (VC[name] + off), 1)]

        def rows(tile, k, n, part):
            if isinstance(k, int):
                return tile[:, k:k + n, part, :]
            return tile[:, bass.ds(k, n), part, :]

        raw_landed = [sem(f"raw_landed{i}") for i in range(RING)]
        hi_made = sem("hi_made")
        lo_made = sem("lo_made")
        chunk_used = sem("chunk_used")
        x_landed = sem("x_landed")
        vec_landed = sem("vec_landed")
        gm_landed = sem("gm_landed")
        h_updated = sem("h_updated")
        sq_made = sem("sq_made")
        ss_summed = sem("ss_summed")
        std_made = sem("std_made")
        rs_made = sem("rs_made")
        xt_made = sem("xt_made")
        x_hi_made = sem("x_hi_made")
        x_lo_made = sem("x_lo_made")
        dve_own = sem("dve_own")
        act_own = sem("act_own")
        up_lin, gate_lin = sem("up_lin"), sem("gate_lin")
        tap_done = sem("tap_done")
        up_conv, gate_conv = sem("up_conv"), sem("gate_conv")
        gate_on = sem("gate_on")
        prod_made = sem("prod_made")
        hid_hi, hid_lo = sem("hid_hi"), sem("hid_lo")
        down_bank = sem("down_bank")
        gm_evac, gm_sums, gm_std, gm_scaled, gm_mixed, gm_masked = [
            sem(n) for n in ("gm_evac", "gm_sums", "gm_std", "gm_scaled", "gm_mixed", "gm_masked")]
        qkv_evac, k_zeroed, bias_ready = sem("qkv_evac"), sem("k_zeroed"), sem("bias_ready")
        bias_landed = sem("bias_landed")
        scored, max_made, exp_made, prob_made, prob_turned, turned_copied, mixed = [
            sem(n) for n in ("scored", "max_made", "exp_made", "prob_made", "prob_turned", "turned_copied", "mixed")]
        o_hi, o_lo = sem("o_hi"), sem("o_lo")
        hy_landed, lora_landed, sbk_zeroed = sem("hy_landed"), sem("lora_landed"), sem("sbk_zeroed")
        hy_evac, hy_lin, hy_mixed = sem("hy_evac"), sem("hy_lin"), sem("hy_mixed")
        z_made, log_made, stick_made, after_made, arg_made, w_made, w_masked, sb_mixed, sb_hi, sb_lo = [
            sem(n) for n in ("z_made", "log_made", "stick_made", "after_made", "arg_made", "w_made", "w_masked",
                             "sb_mixed", "sb_hi", "sb_lo")]
        (mu_ready, lora_in, w_proj, a_proj, w_arg, w_sig, a_sig, cum_made, decay_made, kk_made, kk_sq, kk_ss, kk_max,
         kk_rn, rk_made, rk_sum, factors, imdt_made, bonus_made) = [sem(n) for n in (
             "mu_ready", "lora_in", "w_proj", "a_proj", "w_arg", "w_sig", "a_sig", "cum_made", "decay_made", "kk_made",
             "kk_sq", "kk_ss", "kk_max", "kk_rn", "rk_made", "rk_sum", "factors", "imdt_made", "bonus_made")]
        mat_done = sem("mat_done")
        mat = [sem(f"mat{i}") for i in range(22)]
        ch_x, ch_xs, ch_u, ch_us, ch_s, ch_st, ch_y = [
            sem(n) for n in ("ch_x", "ch_xs", "ch_u", "ch_us", "ch_s", "ch_st", "ch_y")]
        y_made, y_mean, yc_made, y_sq, y_var, y_rstd, g_proj, ro_made, ro_hi, ro_lo = [
            sem(n) for n in ("y_made", "y_mean", "yc_made", "y_sq", "y_var", "y_rstd", "g_proj", "ro_made", "ro_hi",
                             "ro_lo")]
        p_landed, p_hi, p_lo, e_done, e_evac, e_sq, e_ss, e_std, e_made, g_on = [
            sem(n) for n in ("p_landed", "p_hi", "p_lo", "e_done", "e_evac", "e_sq", "e_ss", "e_std", "e_made", "g_on")]
        ml_landed, cs_arg, cs_made, c_evac, kr_made, c_sq, c_ss, c_std, c_made, c_hi, c_lo = [
            sem(n) for n in ("ml_landed", "cs_arg", "cs_made", "c_evac", "kr_made", "c_sq", "c_ss", "c_std", "c_made",
                             "c_hi", "c_lo")]
        up_done, ml_evac, ml_rope, fold_done, kr_spread = [
            sem(n) for n in ("up_done", "ml_evac", "ml_rope", "fold_done", "kr_spread")]
        stored = sem("stored")

        block = ctx.enter_context(nc.Block())

        def at_least(eng, s, value):
            if not isinstance(value, int) or value > 0:
                eng.wait_ge(s, value)

        def mixed_block(j):
            if j < 12:
                return slot[j // 4][:, j % 4, :]
            return wlal[:] if j == 12 else gl[:, j - 13, :]

        def flat(i):
            return slot[i][:].rearrange("p b t -> p (b t)")

        class Own:

            def __init__(self, eng, s):
                self.eng, self.s, self.n = eng, s, 0

            def mark(self, ins):
                ins.then_inc(self.s, 1)
                self.n += 1
                return self.n

            def wait(self, n=None):
                self.eng.wait_ge(self.s, self.n if n is None else n)

        class Chunk:

            def __init__(self, first, it=None):
                self.first, self.it, self.slot = first, it, first % RING

            def count(self, more):
                return self.first + more if self.it is None else self.it * RING + (self.first + more)

            def landed(self):
                n = 16 * (self.first // RING + 1)
                return n if self.it is None else self.it * 16 + n

            def ahead(self):
                if self.it is None and self.first + AHEAD >= NCH:
                    return None
                return Chunk(self.first + AHEAD, self.it)

        ends_chunk = {7: C0["ml_q"] + 2, 11: C0["ml_k"], 15: C0["ml_k"] + 1, 19: C0["ml_v"]}

        def wait_up(eng, g):
            if g in ends_chunk:
                eng.wait_ge(chunk_used, ends_chunk[g] + 1)
            else:
                eng.wait_ge(up_done, g + 1 - sum(e < g for e in ends_chunk))

        @block.sync
        def _(sp):
            for c in range(RING):
                sp.dma_start(raw[c][:], stream[c]).then_inc(raw_landed[c], 16)
            with sp.Fori(1, NCH // RING) as it:
                for s in range(RING):
                    sp.wait_ge(lo_made, it * RING + (s + 1 - RING))
                    src = stream[bass.ds(it * RING + s, 1)].rearrange("a p n -> p (a n)")
                    sp.dma_start(raw[s][:], src).then_inc(raw_landed[s], 16)
            for c in range(NCH // RING * RING, NCH):
                sp.wait_ge(lo_made, c + 1 - RING)
                sp.dma_start(raw[c % RING][:], stream[c]).then_inc(raw_landed[c % RING], 16)
            sp.wait_ge(xt_made, FINAL_XT)
            sp.dma_start(out, xt[:]).then_inc(stored, 16)
            sp.wait_ge(stored, 16)

        @block.gpsimd
        def _(pool):
            pool.wait_ge(gm_landed, 32)
            nc.gpsimd.memset(wsT[64:128, :, 0:64], 0.0).then_inc(gm_masked, 1)
            pool.wait_ge(h_updated, 8)
            nc.gpsimd.memset(at_k[64:128, 0:HEADS:2, :], 0.0).then_inc(k_zeroed, 1)
            nc.gpsimd.memset(at_k[0:64, 1:HEADS:2, :], 0.0).then_inc(k_zeroed, 1)
            pool.dma_start(at_bias[:], rel).then_inc(bias_landed, 16)
            pool.wait_ge(bias_landed, 16)
            nc.gpsimd.memset(at_bias[0:64, :, 192:256], NEG).then_inc(bias_ready, 1)
            pool.wait_ge(h_updated, 16)
            pool.dma_start(hcon[:], hyc[:, 2 * P:]).then_inc(hy_landed, 16)
            pool.dma_start(w0b[:], bass.AP(w0.tensor, 0, [[0, P], [1, 512]])).then_inc(hy_landed, 16)
            nc.gpsimd.memset(sb_k[64:128, 0:SB_HEADS:2, :], 0.0).then_inc(sbk_zeroed, 1)
            nc.gpsimd.memset(sb_k[0:64, 1:SB_HEADS:2, :], 0.0).then_inc(sbk_zeroed, 1)
            pool.wait_ge(x_lo_made, 4 * (OUT_HY + 1))
            pool.dma_start(lora_w[:], lora).then_inc(lora_landed, 16)
            pool.wait_ge(h_updated, 28)
            pool.dma_start(pl_in[:], p_t[0]).then_inc(p_landed, 16)
            pool.wait_ge(h_updated, 32)
            pool.dma_start(ml_con[:], mlc).then_inc(ml_landed, 16)
            pool.dma_start(ml_pos[:], bass.AP(pos.tensor, 0, [[0, P], [1, T]])).then_inc(ml_landed, 16)
            pool.wait_ge(h_updated, 40)
            pool.dma_start(pl_in[:], p_t[1]).then_inc(p_landed, 16)

        @block.scalar
        def _(act):
            own = Own(act, act_own)

            def split_hi(c):
                if c is None:
                    return
                act.wait_ge(raw_landed[c.slot], c.landed())
                at_least(act, chunk_used, c.count(1 - RING))
                nc.scalar.activation(w_hi[c.slot][:], raw[c.slot][:], ACT.Copy).then_inc(hi_made, 1)

            def square_norm(n):
                for b in range(4):
                    if n == 0:
                        act.wait_ge(x_landed, 16)
                    else:
                        act.wait_ge(h_updated, 4 * (n - 1) + b + 1)
                    nc.scalar.activation(xt[:, 2 * b:2 * b + 2, :], hT[:, 2 * b:2 * b + 2, :],
                                         ACT.Square).then_inc(sq_made, 1)
                nc.scalar.preload_act_table(ACT.Sqrt)
                act.wait_ge(ss_summed, n + 1)
                nc.scalar.activation(std[:], half(4, 0), ACT.Sqrt, bias=col("eps"),
                                     scale=1.0 / D).then_inc(std_made, 1)

            def round_x(o, dst):
                for b in range(4):
                    act.wait_ge(xt_made, 8 * o + 2 * b + 2)
                    nc.scalar.activation(dst[:, 2 * b:2 * b + 2, 0, :], xt[:, 2 * b:2 * b + 2, :],
                                         ACT.Copy).then_inc(x_hi_made, 1)

            def only_split(name, n, start=0):
                for j in range(start, n):
                    split_hi(Chunk(C0[name] + j).ahead())

            def ffn(f):
                c0, base, both = C0[f"up{f}"], PAIRS * f, f < 2
                goff = KF if both else 0

                def linear(acc, bank, q, off):
                    for b in range(2):
                        j = 2 * q + b if isinstance(q, int) else q * 2 + b
                        last = nc.scalar.activation(acc[:, b, :], half(bank, b), ACT.Identity,
                                                    bias=dcol(f"cb{f}", j, off),
                                                    scale=dcol(f"cw{f}", j, off + 2 * (goff + KF)))
                    return last

                def gate(q, par):
                    act.wait_ge(gate_conv, q + (base + 1))
                    nc.scalar.activation(gate_acc[par][:], gate_acc[par][:],
                                         ACT.Silu if both else ACT.Gelu).then_inc(gate_on, 1)

                def round_hid(q, par):
                    act.wait_ge(prod_made, q + (base + 1))
                    nc.scalar.activation(rows(hid, q * 2, 2, 0), up_acc[par][:], ACT.Copy).then_inc(hid_hi, 1)

                def pair(q, par, cu, cg, first=False, second=False):
                    split_hi(cu.ahead())
                    if not first:
                        gate(q - 1, 1 - par)
                    if both:
                        act.wait_ge(chunk_used, cu.count(1))
                        if not (first or second):
                            act.wait_ge(hid_lo, q + (base - 1))
                        linear(up_acc[par], 2 * par, q, 0).then_inc(up_lin, 1)
                    split_hi(cg.ahead())
                    if not first:
                        round_hid(q - 1, 1 - par)
                    act.wait_ge(chunk_used, cg.count(1))
                    if not (first or second):
                        act.wait_ge(prod_made, q + (base - 1))
                    linear(gate_acc[par], 2 * par + 1, q, goff).then_inc(gate_lin, 1)

                pair(0, 0, Chunk(c0), Chunk(c0 + 1), first=True)
                pair(1, 1, Chunk(c0 + 2), Chunk(c0 + 3), second=True)
                pair(2, 0, Chunk(c0 + 4), Chunk(c0 + 5))
                with act.Fori(0, (PAIRS - 3) // 2) as it:
                    for j in range(2):
                        pair(it * 2 + (3 + j), (3 + j) % 2, Chunk(c0 + 6 + 2 * j, it), Chunk(c0 + 7 + 2 * j, it))
                gate(PAIRS - 1, (PAIRS - 1) % 2)
                round_hid(PAIRS - 1, (PAIRS - 1) % 2)
                d0 = C0[f"dn{f}"]
                with act.Fori(0, 2) as it:
                    for s in range(RING):
                        split_hi(Chunk(d0 + s, it).ahead())
                for s in range(8, PAIRS):
                    split_hi(Chunk(d0 + s).ahead())

            def attention(a, pr, pt, st):
                h0, m0 = HEADS * a, KD * a

                def exponent(h):
                    act.wait_ge(max_made, h0 + h + 1)
                    for t, (lo, hi) in enumerate(((0, P), (P, 384))):
                        last = nc.scalar.activation(pr[h % 2][:, lo:hi], pr[h % 2][:, lo:hi], ACT.Exp,
                                                    bias=st[:, 1, 2 * h + t:2 * h + t + 1],
                                                    accum_out=st[:, 2, 2 * h + t:2 * h + t + 1])
                    last.then_inc(exp_made, 1)

                def copy_turned(h):
                    act.wait_ge(prob_turned, h0 + h + 1)
                    if h >= 2:
                        act.wait_ge(mixed, h0 + h - 1)
                    nc.scalar.activation(pt[h % 2][:], ps[:, 2 + h % 2, 0:384], ACT.Copy).then_inc(turned_copied, 1)

                def round_o(m):
                    act.wait_ge(mixed, h0 + 2 * m + 2)
                    nc.scalar.activation(xB[:, m, 0, :], half(4 + m % 4, 0), ACT.Copy).then_inc(o_hi, 1)

                for i in range(HEADS + 3):
                    if i < HEADS:
                        exponent(i)
                    if 1 <= i <= HEADS:
                        copy_turned(i - 1)
                    if i >= 4 and i % 2 == 0:
                        round_o(i // 2 - 2)

            act.dma_start(hT[:], x_t).then_inc(x_landed, 16)
            act.dma_start(vec[:], vecs).then_inc(vec_landed, 16)
            act.dma_start(eye_ones[:], hyc[:, 0:2 * P]).then_inc(vec_landed, 16)
            act.dma_start(wsT[:], wst).then_inc(gm_landed, 16)
            act.dma_start(bsb[:], bass.AP(bsp.tensor, 0, [[0, P], [P, KD], [1, P]])).then_inc(gm_landed, 16)
            act.wait_ge(vec_landed, 32)

            square_norm(N_GM)
            for c in range(AHEAD):
                split_hi(Chunk(c))
            round_x(OUT_GM, xA)
            for g in range(8):
                split_hi(Chunk(g).ahead())
                act.wait_ge(chunk_used, g + 1)
                if g < 4:
                    dst = vnat[:, :, T * g:T * g + T]
                else:
                    dst = uT[:, 2 * (g - 4):2 * (g - 4) + 2, :]
                nc.scalar.activation(dst, ps[:, g % 4, :].rearrange("p (b t) -> p b t", b=2),
                                     ACT.Gelu_apprx_tanh).then_inc(gm_evac, 1)
                if g == 4:
                    act.wait_ge(gm_sums, 1)
                    nc.scalar.activation(gm_rs[:, 0:2], gm_rs[:, 2:4], ACT.Sqrt, bias=col("eps"),
                                         scale=1.0 / D).then_inc(gm_std, 1)
            round_x(OUT_GATED, xB)
            only_split("gm_o", 4)
            square_norm(N_FF0)
            round_x(OUT_FF0, xA)
            ffn(0)
            square_norm(N_AT)
            round_x(OUT_KV, xB)
            round_x(OUT_Q, xA)
            for g in range(12):
                split_hi(Chunk(C0["at_k"] + g).ahead())
                act.wait_ge(chunk_used, C0["at_k"] + g + 1)
                two = ps[:, g % 4, :].rearrange("p (b t) -> p b t", b=2)
                if g < 4:
                    if g == 0:
                        act.wait_ge(k_zeroed, 2)
                    nc.scalar.activation(at_k[0:64, 4 * g:4 * g + 4:2, :], two[0:64], ACT.Copy)
                    ins = nc.scalar.activation(at_k[64:128, 4 * g + 1:4 * g + 4:2, :], two[64:128], ACT.Copy)
                elif g < 8:
                    ins = nc.scalar.activation(at_v[:, :, T * (g - 4):T * (g - 3)], two, ACT.Copy)
                else:
                    ins = nc.scalar.activation(at_qT[:, 2 * (g - 8):2 * (g - 8) + 2, :], two, ACT.Copy, scale=0.125)
                ins.then_inc(qkv_evac, 1)
            attention(0, at_pr, at_pt, at_st)
            only_split("at_o", 4)
            square_norm(N_FF1)
            round_x(OUT_FF1, xA)
            ffn(1)
            square_norm(N_FIN1)
            square_norm(N_HY)
            round_x(OUT_HY, xA)
            c0 = C0["hy"]

            def log_parts(u):
                act.wait_ge(z_made, u + 1)
                if u >= 2:
                    act.wait_ge(log_made, u - 1)
                buf, z = sb_l[u % 2][:], ps[:, 4 + 2 * (u % 2):6 + 2 * (u % 2), 0:384]
                own.mark(nc.scalar.activation(buf, z, ACT.Abs))
                own.wait()
                own.mark(nc.scalar.activation(buf, buf, ACT.Exp, scale=-1.0))
                own.wait()
                nc.scalar.activation(buf, buf, ACT.Ln, bias=1.0).then_inc(stick_made, 1)

            def weights(u):
                act.wait_ge(arg_made, u + 1)
                nc.scalar.activation(sb_ls[u % 2][:], sb_ls[u % 2][:], ACT.Exp).then_inc(w_made, 1)

            def round_sb(u):
                act.wait_ge(sb_mixed, u + 1)
                nc.scalar.activation(xB[:, u, 0, :], half(3, u % 2), ACT.Copy).then_inc(sb_hi, 1)

            act.wait_ge(sbk_zeroed, 2)
            act.wait_ge(mu_ready, 1)
            for g in range(14):
                split_hi(Chunk(c0 + g).ahead())
                act.wait_ge(chunk_used, c0 + g + 1)
                two = ps[:, g % 3, :].rearrange("p (b t) -> p b t", b=2)
                if g < 2:
                    nc.scalar.activation(sb_q[:, 2 * g:2 * g + 2, :], two, ACT.Copy, scale=0.125).then_inc(hy_evac, 1)
                elif g < 4:
                    j = 4 * (g - 2)
                    nc.scalar.activation(sb_k[0:64, j:j + 4:2, :], two[0:64], ACT.Copy)
                    nc.scalar.activation(sb_k[64:128, j + 1:j + 4:2, :], two[64:128], ACT.Copy).then_inc(hy_evac, 1)
                elif g < 6:
                    nc.scalar.activation(sb_v[:, :, T * (g - 4):T * (g - 3)], two, ACT.Copy).then_inc(hy_evac, 1)
                else:
                    j = g - 6
                    if 3 <= j <= 6:
                        round_sb(j - 3)
                    for b in range(2 if g < 13 else 1):
                        last = nc.scalar.activation(mixed_block(2 * j + b), half(g % 3, b), ACT.Copy,
                                                    scale=om_mu[:, 2 * j + b:2 * j + b + 1])
                    last.then_inc(hy_lin, 1)
                    if j < 4:
                        if j == 0:
                            nc.scalar.preload_act_table_set("natural_log_exp_and_others")
                        log_parts(j)
                    if 1 <= j <= 4:
                        weights(j - 1)
            act.wait_ge(hy_mixed, 7)
            nc.scalar.activation(wlal[0:64, :], wlal[0:64, :], ACT.Tanh).then_inc(lora_in, 1)
            act.wait_ge(hy_mixed, 8)
            nc.scalar.activation(gl[:], gl[:], ACT.Sigmoid).then_inc(lora_in, 1)
            for t in range(2):
                act.wait_ge(w_arg, t + 1)
                nc.scalar.activation(flat(3)[:, 512 * t:512 * t + 512], flat(3)[:, 512 * t:512 * t + 512],
                                     ACT.Sigmoid).then_inc(w_sig, 1)
            act.wait_ge(a_proj, 2)
            for b in range(RBLK):
                last = nc.scalar.activation(slot[4][:, b, :], half(6 + b // 2, b % 2), ACT.Sigmoid,
                                            bias=col("rw_a0", b))
            last.then_inc(a_sig, 1)
            act.wait_ge(kk_made, 1)
            nc.scalar.activation(slot[9][:], slot[8][:], ACT.Square).then_inc(kk_sq, 1)
            nc.scalar.preload_act_table_set("natural_log_exp_and_others")
            act.wait_ge(cum_made, 1)
            cums = ps[:, 0:4, :].rearrange("p b (t i n) -> p b t i n", t=2, i=2)
            for dst, i, sign in ((5, 0, 1.0), (6, 0, -1.0), (7, 1, 1.0)):
                nc.scalar.activation(slot[dst][:].rearrange("p b (t n) -> p b t n", t=2), cums[:, :, :, i, :], ACT.Exp,
                                     scale=sign).then_inc(decay_made, 1)
            act.wait_ge(kk_max, 2)
            own.mark(nc.scalar.activation(slot[9][:], slot[9][:], ACT.Ln, scale=65536.0))
            own.wait()
            nc.scalar.activation(slot[9][:], slot[9][:], ACT.Exp, scale=-0.5, bias=col("ln256")).then_inc(kk_rn, 1)

            def copy_product(i, dst):
                for b in range(2):
                    act.wait_ge(mat_done, 2 * i + b + 1)
                    nc.scalar.activation(slot[dst][:, 2 * b:2 * b + 2, :],
                                         ps[:, 2 * (i % 4) + b, :].rearrange("p (b t) -> p b t", b=2),
                                         ACT.Copy).then_inc(mat[i], 1)

            for i, dst in ((0, 3), (1, 5), (2, 6), (9, 4), (11, 10), (12, 1), (13, 2), (15, 10), (17, 2), (19, 10),
                           (20, 7), (21, 1)):
                if i == 0:
                    act.wait_ge(factors, 5)
                copy_product(i, dst)
            act.wait_ge(ch_y, 1)
            for b in range(2):
                nc.scalar.activation(slot[12][:, 2 * b:2 * b + 2, :],
                                     ps[:, 4 + b, :].rearrange("p (b t) -> p b t", b=2), ACT.Copy).then_inc(y_made, 1)
            for b in range(2):
                act.wait_ge(yc_made, b + 1)
                nc.scalar.activation(slot[13][:, 2 * b:2 * b + 2, :], slot[12][:, 2 * b:2 * b + 2, :],
                                     ACT.Square).then_inc(y_sq, 1)
            for b in range(2):
                act.wait_ge(y_var, b + 1)
                own.mark(nc.scalar.activation(slot[14][:, 2 * b:2 * b + 2, :],
                                              ps[:, b, :].rearrange("p (b t) -> p b t", b=2), ACT.Ln,
                                              bias=col("gn_eps")))
                own.wait()
                nc.scalar.activation(slot[14][:, 2 * b:2 * b + 2, :], slot[14][:, 2 * b:2 * b + 2, :], ACT.Exp,
                                     scale=-0.5).then_inc(y_rstd, 1)
            for b in range(2):
                act.wait_ge(ro_made, b + 1)
                nc.scalar.activation(xB[:, 4 + 2 * b:6 + 2 * b, 0, :], slot[15][:, 2 * b:2 * b + 2, :],
                                     ACT.Copy).then_inc(ro_hi, 1)
            only_split("hy_o", 4)
            square_norm(N_FF2)
            round_x(OUT_FF2, xA)
            ffn(2)
            def ple(i):
                n, o = (N_PL0, OUT_PL0) if i == 0 else (N_PL1, OUT_PL1)
                c0 = C0[f"pl_p{i}"]
                act.wait_ge(p_landed, 16 * (i + 1))
                nc.scalar.activation(pl_x[:, :, 0, :], pl_in[:], ACT.Copy).then_inc(p_hi, 1)
                square_norm(n)
                round_x(o, xA)
                split_hi(Chunk(c0).ahead())
                for b in range(4):
                    if b < 3:
                        act.wait_ge(e_done, 3 * i + b + 1)
                    else:
                        act.wait_ge(chunk_used, c0 + 1)
                    two = ps[:, b, :].rearrange("p (b t) -> p b t", b=2)
                    nc.scalar.activation(pl_e[:, 2 * b:2 * b + 2, :], two, ACT.Copy)
                    nc.scalar.activation(pl_sq[:, 2 * b:2 * b + 2, :], two, ACT.Square).then_inc(e_evac, 1)
                act.wait_ge(e_ss, i + 1)
                nc.scalar.activation(pl_rs[:], half(5, 0), ACT.Sqrt, bias=col("eps"), scale=1.0 / D).then_inc(e_std, 1)
                for g in range(4):
                    c = Chunk(c0 + 1 + g)
                    split_hi(c.ahead())
                    act.wait_ge(chunk_used, c.count(1))
                    if g >= 2:
                        act.wait_ge(h_updated, 4 * (n if i == 0 else n) + g - 1)
                    nc.scalar.activation(pl_sg[g % 2][:], ps[:, g, :].rearrange("p (b t) -> p b t", b=2),
                                         ACT.Sigmoid).then_inc(g_on, 1)

            ple(0)
            square_norm(N_ML)
            round_x(OUT_ML, xA)
            act.wait_ge(cs_arg, 1)
            nc.scalar.activation(ml_cs[:], ml_ang, ACT.Sin).then_inc(cs_made, 1)
            c0 = C0["ml_d"]
            for g in range(3):
                split_hi(Chunk(c0 + g).ahead())
                act.wait_ge(chunk_used, c0 + g + 1)
                n = 2 if g < 2 else 1
                two = ps[:, g, 0:n * T].rearrange("p (b t) -> p b t", b=n)
                nc.scalar.activation(ml_c[:, 2 * g:2 * g + n, :], two, ACT.Copy)
                nc.scalar.activation(xt[:, 2 * g:2 * g + n, :], two, ACT.Square).then_inc(c_evac, 1)
            nc.scalar.preload_act_table(ACT.Sqrt)
            for j, width in enumerate((384, 256)):
                act.wait_ge(c_ss, j + 1)
                nc.scalar.activation(ml_rs[:, j, :], half(4 + j, 0), ACT.Sqrt, bias=col("eps"),
                                     scale=1.0 / width).then_inc(c_std, 1)
            for k in range(5):
                act.wait_ge(c_made, k + 1)
                nc.scalar.activation(xB[:, k, 0, :], xt[:, k, :], ACT.Copy).then_inc(c_hi, 1)
            act.wait_ge(fold_done, 1)
            src = ps[64:128, 6, 0:T].unsqueeze(1).broadcast_to([64, HEADS // 2, T])
            nc.scalar.activation(ml_k[64:128, 0:HEADS // 2, :], src, ACT.Copy).then_inc(kr_spread, 1)
            for g in range(20):
                if g in (0, 2, 5, 8, 12, 16):
                    split_hi(Chunk(C0["ml_q"] + (0, 2, 5, 8, 12, 16).index(g)).ahead())
                wait_up(act, g)
                two = ps[:, g % 4, :].rearrange("p (b t) -> p b t", b=2)
                if g < 8:
                    ins = nc.scalar.activation(ml_q[0:64, 2 * g:2 * g + 2, :], two[0:64], ACT.Copy, scale=MLA_SCALE)
                elif g < 16:
                    ins = nc.scalar.activation(ml_k[0:64, 2 * (g - 8):2 * (g - 8) + 2, :], two[0:64], ACT.Copy)
                else:
                    t, n = divmod(g - 16, 2)
                    ins = nc.scalar.activation(ml_v[:, t, 512 * n:512 * n + 512], ps[:, g % 4, :], ACT.Copy)
                ins.then_inc(ml_evac, 1)
            attention(1, ml_pr, ml_pt, ml_st)
            only_split("ml_o", 4)
            square_norm(N_FF3)
            round_x(OUT_FF3, xA)
            ffn(3)
            ple(1)
            square_norm(N_FIN2)

        @block.vector
        def _(dve):
            own = Own(dve, dve_own)

            def link(ins):
                own.mark(ins)
                own.wait()

            def split_lo(c):
                if c is None:
                    return
                dve.wait_ge(hi_made, c.count(1))
                nc.vector.tensor_tensor(w_lo[c.slot][:], raw[c.slot][:], w_hi[c.slot][:].bitcast(F32),
                                        ALU.subtract).then_inc(lo_made, 1)

            def only_split(name, n):
                for j in range(n):
                    split_lo(Chunk(C0[name] + j).ahead())

            def root(n):
                dve.wait_ge(std_made, n + 1)
                nc.vector.reciprocal(rs[:], std[:]).then_inc(rs_made, 1)
                dve.wait_ge(rs_made, n + 1)

            def rest_x(o, dst, b):
                dve.wait_ge(x_hi_made, 4 * o + b + 1)
                nc.vector.tensor_tensor(dst[:, 2 * b:2 * b + 2, 1, :], xt[:, 2 * b:2 * b + 2, :],
                                        dst[:, 2 * b:2 * b + 2, 0, :].bitcast(F32), ALU.subtract).then_inc(x_lo_made, 1)

            def scale_x(o, dst, gain):
                for k in range(KD):
                    nc.vector.scalar_tensor_tensor(out=xt[:, k, :], in0=hT[:, k, :], scalar=col(gain, k), in1=rs[:],
                                                   op0=ALU.mult, op1=ALU.mult).then_inc(xt_made, 1)
                    if k >= 3 and k % 2:
                        rest_x(o, dst, (k - 3) // 2)
                rest_x(o, dst, 3)

            def add_quarter(b, bank):
                nc.vector.tensor_tensor(hT[:, 2 * b:2 * b + 2, :], hT[:, 2 * b:2 * b + 2, :],
                                        ps[:, bank, :].rearrange("p (b t) -> p b t", b=2),
                                        ALU.add).then_inc(h_updated, 1)

            def add_projection(name):
                for g in range(4):
                    split_lo(Chunk(C0[name] + g).ahead())
                    dve.wait_ge(chunk_used, C0[name] + g + 1)
                    add_quarter(g, 4 + g)

            def ffn(f):
                c0, base, both = C0[f"up{f}"], PAIRS * f, f < 2
                goff = KF if both else 0
                nblk = 2 * KF if both else KF
                taps = 4 if both else 2
                tap0 = 4 * PAIRS * min(f, 2) + 2 * PAIRS * max(f - 2, 0)

                def convolve(acc, bank, q, off, nth):
                    for b in range(2):
                        j = q * 2 + b
                        nc.vector.scalar_tensor_tensor(out=acc[:, b, 2:T], in0=half(bank, b)[:, 0:T - 2],
                                                       scalar=dcol(f"cw{f}", j, off), in1=acc[:, b, 2:T],
                                                       op0=ALU.mult, op1=ALU.add).then_inc(tap_done, 1)
                    for b in range(2):
                        j = q * 2 + b
                        dve.wait_ge(tap_done, q * taps + (tap0 + nth + b + 1))
                        last = nc.vector.scalar_tensor_tensor(out=acc[:, b, 1:T], in0=half(bank, b)[:, 0:T - 1],
                                                              scalar=dcol(f"cw{f}", j, off + nblk),
                                                              in1=acc[:, b, 1:T], op0=ALU.mult, op1=ALU.add)
                    return last

                def product(q, par):
                    dve.wait_ge(gate_on, q + (base + 1))
                    if both:
                        dve.wait_ge(up_conv, q + (base + 1))
                        up = up_acc[par][:]
                    else:
                        up = ps[:, 2 * par, :].rearrange("p (b t) -> p b t", b=2)
                        if not isinstance(q, int) or q >= 2:
                            dve.wait_ge(hid_lo, q + (base - 1))
                    nc.vector.tensor_tensor(up_acc[par][:], up, gate_acc[par][:], ALU.mult).then_inc(prod_made, 1)

                def rest_hid(q, par):
                    dve.wait_ge(hid_hi, q + (base + 1))
                    nc.vector.tensor_tensor(rows(hid, q * 2, 2, 1), up_acc[par][:], rows(hid, q * 2, 2, 0).bitcast(F32),
                                            ALU.subtract).then_inc(hid_lo, 1)

                def pair(q, par, cu, cg, first=False):
                    split_lo(cu.ahead())
                    if both:
                        dve.wait_ge(up_lin, q + (base + 1))
                        convolve(up_acc[par], 2 * par, q, 0, 0).then_inc(up_conv, 1)
                    if not first:
                        product(q - 1, 1 - par)
                    split_lo(cg.ahead())
                    dve.wait_ge(gate_lin, q + (base + 1))
                    convolve(gate_acc[par], 2 * par + 1, q, goff, taps - 2).then_inc(gate_conv, 1)
                    if not first:
                        rest_hid(q - 1, 1 - par)

                pair(0, 0, Chunk(c0), Chunk(c0 + 1), first=True)
                pair(1, 1, Chunk(c0 + 2), Chunk(c0 + 3))
                pair(2, 0, Chunk(c0 + 4), Chunk(c0 + 5))
                with dve.Fori(0, (PAIRS - 3) // 2) as it:
                    for j in range(2):
                        pair(it * 2 + (3 + j), (3 + j) % 2, Chunk(c0 + 6 + 2 * j, it), Chunk(c0 + 7 + 2 * j, it))
                product(PAIRS - 1, (PAIRS - 1) % 2)
                rest_hid(PAIRS - 1, (PAIRS - 1) % 2)
                d0 = C0[f"dn{f}"]
                with dve.Fori(0, 2) as it:
                    for s in range(RING):
                        split_lo(Chunk(d0 + s, it).ahead())
                for s in range(8, PAIRS):
                    split_lo(Chunk(d0 + s).ahead())
                for b in range(4):
                    if b < 3:
                        dve.wait_ge(down_bank, 3 * f + b + 1)
                    else:
                        dve.wait_ge(chunk_used, d0 + PAIRS)
                    add_quarter(b, 4 + b)

            def attention(a, pr, st, bias):
                h0, m0 = HEADS * a, KD * a

                def biased_max(h):
                    dve.wait_ge(scored, h0 + h + 1)
                    if h >= 2:
                        dve.wait_ge(prob_turned, h0 + h - 1)
                    for t, (lo, hi) in enumerate(((0, P), (P, 384))):
                        own.mark(nc.vector.tensor_tensor_reduce(
                            pr[h % 2][:, lo:hi], ps[:, h % 2, lo:hi], bias(h, t), 1.0, -3e38, ALU.add, ALU.max,
                            st[:, 0, 2 * h + t:2 * h + t + 1]))
                    own.wait()
                    nc.vector.tensor_scalar(st[:, 1, 2 * h:2 * h + 2], st[:, 0, 2 * h:2 * h + 2], -1.0, None,
                                            ALU.mult).then_inc(max_made, 1)

                def normalise(h):
                    dve.wait_ge(exp_made, h0 + h + 1)
                    link(nc.vector.reciprocal(st[:, 3, 2 * h:2 * h + 2], st[:, 2, 2 * h:2 * h + 2]))
                    for t, (lo, hi) in enumerate(((0, P), (P, 384))):
                        last = nc.vector.tensor_scalar(pr[h % 2][:, lo:hi], pr[h % 2][:, lo:hi],
                                                       st[:, 3, 2 * h + t:2 * h + t + 1], None, ALU.mult)
                    last.then_inc(prob_made, 1)

                def rest_o(m):
                    dve.wait_ge(o_hi, m0 + m + 1)
                    nc.vector.tensor_tensor(xB[:, m, 1, :], half(4 + m % 4, 0), xB[:, m, 0, :].bitcast(F32),
                                            ALU.subtract).then_inc(o_lo, 1)

                for i in range(HEADS + 3):
                    if i < HEADS:
                        biased_max(i)
                    if 1 <= i <= HEADS:
                        normalise(i - 1)
                    if i >= 5 and i % 2:
                        rest_o((i - 5) // 2)
                rest_o(KD - 1)

            dve.wait_ge(vec_landed, 32)
            for c in range(AHEAD):
                split_lo(Chunk(c))
            dve.wait_ge(x_landed, 16)
            root(N_GM)
            scale_x(OUT_GM, xA, "a_norm")
            for g in range(8):
                split_lo(Chunk(g).ahead())
                if g < 4:
                    dve.wait_ge(gm_evac, g + 1)
                    for t in range(2):
                        own.mark(nc.vector.tensor_tensor_reduce(
                            gm_junk[:], vnat[:, t, T * g:T * g + T], vnat[:, t, T * g:T * g + T], 1.0, 0.0, ALU.mult,
                            ALU.add, gm_sum[:, 4 * t + g:4 * t + g + 1]))
                        own.wait()
                if g == 3:
                    nc.vector.tensor_reduce(gm_rs[:, 2:4], gm_sum[:].rearrange("p (t g) -> p t g", t=2), AX_X,
                                            ALU.add).then_inc(gm_sums, 1)
            dve.wait_ge(gm_std, 1)
            link(nc.vector.reciprocal(gm_rs[:, 2:4], gm_rs[:, 0:2]))
            for t in range(2):
                nc.vector.tensor_scalar(vnat[:, t, :], vnat[:, t, :], gm_rs[:, 2 + t:3 + t], None,
                                        ALU.mult).then_inc(gm_scaled, 1)
            dve.wait_ge(gm_evac, 8)
            for k in range(KD):
                dve.wait_ge(gm_mixed, k // 2 + 1)
                if k == 0:
                    dve.wait_ge(gm_landed, 32)
                xk = xt[:, k, :].rearrange("p (n i) -> p n i", n=2)
                link(nc.vector.scalar_tensor_tensor(
                    out=xk, in0=half(4 + k // 2, k % 2).rearrange("p (n i) -> p n i", n=2), scalar=col("a_vnorm", k),
                    in1=bsb[:, k:k + 1, :].broadcast_to([P, 2, P]), op0=ALU.mult, op1=ALU.add))
                nc.vector.tensor_tensor(xt[:, k, :], xt[:, k, :], uT[:, k, :], ALU.mult).then_inc(xt_made, 1)
                if k >= 3 and k % 2:
                    rest_x(OUT_GATED, xB, (k - 3) // 2)
            rest_x(OUT_GATED, xB, 3)
            add_projection("gm_o")
            root(N_FF0)
            scale_x(OUT_FF0, xA, "f_norm0")
            ffn(0)
            root(N_AT)
            scale_x(OUT_KV, xB, "kv_norm")
            dve.wait_ge(x_lo_made, 4 * OUT_Q)
            scale_x(OUT_Q, xA, "b_norm")
            for g in range(12):
                split_lo(Chunk(C0["at_k"] + g).ahead())
            dve.wait_ge(bias_ready, 1)
            attention(0, at_pr, at_st, lambda h, t: at_bias[:, h, P:T] if t == 0 else at_bias[:, h, :])
            add_projection("at_o")
            root(N_FF1)
            scale_x(OUT_FF1, xA, "f_norm1")
            ffn(1)
            root(N_FIN1)
            for k in range(KD):
                ins = nc.vector.scalar_tensor_tensor(out=hT[:, k, :], in0=hT[:, k, :], scalar=col("fin1", k), in1=rs[:],
                                                     op0=ALU.mult, op1=ALU.mult)
                if k % 2:
                    ins.then_inc(h_updated, 1)
            nc.vector.tensor_scalar(om_mu[:], col("rw_mu", 0, 15), -1.0, 1.0, ALU.mult, ALU.add).then_inc(mu_ready, 1)
            root(N_HY)
            dve.wait_ge(h_updated, 20)
            scale_x(OUT_HY, xA, "at_norm0")
            c0 = C0["hy"]

            def diagonal(tile):
                return tile[:].rearrange("p h (b q) -> p h b q", b=3)[:, :, 0:3:2, :]

            tri = h_tri.unsqueeze(1).unsqueeze(1).broadcast_to([P, 2, 2, P])

            def logs(u):
                dve.wait_ge(stick_made, u + 1)
                z = ps[:, 4 + 2 * (u % 2):6 + 2 * (u % 2), 0:384]
                if u >= 2:
                    dve.wait_ge(sb_mixed, u - 1)
                link(nc.vector.scalar_tensor_tensor(out=sb_ls[u % 2][:], in0=z, scalar=0.0, in1=sb_l[u % 2][:],
                                                    op0=ALU.min, op1=ALU.subtract))
                if u >= 1:
                    dve.wait_ge(after_made, u)
                link(nc.vector.tensor_tensor(sb_lm[:], sb_ls[u % 2][:], z, ALU.subtract))
                nc.vector.tensor_tensor(diagonal(sb_lm), diagonal(sb_lm), tri, ALU.mult).then_inc(log_made, 1)

            def arguments(u):
                dve.wait_ge(after_made, u + 1)
                nc.vector.tensor_tensor(sb_ls[u % 2][:], sb_ls[u % 2][:],
                                        ps[:, 4 + 2 * (u % 2):6 + 2 * (u % 2), 0:384], ALU.add).then_inc(arg_made, 1)
                dve.wait_ge(w_made, u + 1)
                nc.vector.tensor_tensor(diagonal(sb_ls[u % 2]), diagonal(sb_ls[u % 2]), tri, ALU.mult).then_inc(w_masked, 1)

            def rest_sb(u):
                dve.wait_ge(sb_hi, u + 1)
                nc.vector.tensor_tensor(xB[:, u, 1, :], half(3, u % 2), xB[:, u, 0, :].bitcast(F32),
                                        ALU.subtract).then_inc(sb_lo, 1)

            dve.wait_ge(hy_landed, 32)
            for g in range(14):
                split_lo(Chunk(c0 + g).ahead())
                if g < 6:
                    continue
                j = g - 6
                if 3 <= j <= 6:
                    rest_sb(j - 3)
                dve.wait_ge(hy_lin, j + 1)
                for b in range(2 if g < 13 else 1):
                    dst = mixed_block(2 * j + b)
                    last = nc.vector.scalar_tensor_tensor(out=dst[:, 1:T], in0=half(g % 3, b)[:, 0:T - 1],
                                                          scalar=col("rw_mu", 2 * j + b), in1=dst[:, 1:T],
                                                          op0=ALU.mult, op1=ALU.add)
                last.then_inc(hy_mixed, 1)
                if j < 4:
                    logs(j)
                if 1 <= j <= 4:
                    arguments(j - 1)
            dve.wait_ge(sb_mixed, 4)
            dve.wait_ge(hy_mixed, 8)
            for b in range(RBLK):
                last = nc.vector.tensor_scalar(slot[8][:, b, :], slot[1][:, b, :], col("rw_kk", b), None, ALU.mult)
            last.then_inc(kk_made, 1)
            for t in range(2):
                dve.wait_ge(w_proj, t + 1)
                nc.vector.tensor_tensor(flat(3)[:, 512 * t:512 * t + 512], ps[:, 4 + t, :], w0b[:], ALU.add).then_inc(w_arg, 1)
            for b in range(2):
                dve.wait_ge(kk_ss, b + 1)
                nc.vector.tensor_scalar(slot[9][:, 2 * b:2 * b + 2, :], ps[:, 4 + b, :].rearrange("p (b t) -> p b t", b=2),
                                        1e-24, None, ALU.max).then_inc(kk_max, 1)
            dve.wait_ge(kk_rn, 1)
            link(nc.vector.tensor_tensor(slot[8][:], slot[8][:], slot[9][:], ALU.mult))
            dve.wait_ge(a_sig, 1)
            for b in range(RBLK):
                own.mark(nc.vector.tensor_scalar(slot[9][:, b, :], slot[4][:, b, :], -1.0, col("rw_ka", b), ALU.add, ALU.mult))
            own.wait()
            link(nc.vector.scalar_tensor_tensor(out=slot[1][:], in0=slot[9][:], scalar=1.0, in1=slot[1][:], op0=ALU.add,
                                                op1=ALU.mult))
            for b in range(RBLK):
                last = nc.vector.scalar_tensor_tensor(out=slot[9][:, b, :], in0=slot[0][:, b, :], scalar=col("rw_rk", b),
                                                      in1=slot[1][:, b, :], op0=ALU.mult, op1=ALU.mult)
                if b % 2:
                    last.then_inc(rk_made, 1)
            link(nc.vector.tensor_tensor(slot[4][:], slot[4][:], slot[8][:], ALU.mult))
            dve.wait_ge(rk_made, 2)
            dve.wait_ge(decay_made, 3)
            for dst, by in ((8, 7), (4, 6), (1, 6), (0, 5)):
                nc.vector.tensor_tensor(slot[dst][:], slot[dst][:], slot[by][:], ALU.mult).then_inc(factors, 1)
            nc.vector.tensor_copy(pend[:], slot[5][:].rearrange("p b (c t) -> p b c t", c=NRCH)[:, :, :, RCH - 1]).then_inc(factors, 1)
            for b in range(2):
                dve.wait_ge(rk_sum, b + 1)
                nc.vector.tensor_tensor(slot[9][:, 2 * b:2 * b + 2, :], ps[:, 6 + b, :].rearrange("p (b t) -> p b t", b=2),
                                        slot[2][:, 2 * b:2 * b + 2, :], ALU.mult).then_inc(bonus_made, 1)

            def halves(i, b):
                return ps[:, 2 * (i % 4) + b, :].rearrange("p (m s) -> p m s", s=64)

            def part(d, b):
                return slot[d][:, 2 * b:2 * b + 2, :].rearrange("p b (c s) -> p (b c) s", s=64)

            def wide(mask):
                return mask.unsqueeze(1).broadcast_to([P, 8, 64])

            eye64 = hcon[:, HCON - 64:HCON]

            def masked(i, dsts):
                for b in range(2):
                    dve.wait_ge(mat_done, 2 * i + b + 1)
                    for dst, mask in dsts:
                        nc.vector.tensor_tensor(part(dst, b), halves(i, b), wide(mask), ALU.mult).then_inc(mat[i], 1)

            def with_eye(i, dsts):
                for b in range(2):
                    dve.wait_ge(mat_done, 2 * i + b + 1)
                    for dst, how in dsts:
                        if how == 0:
                            ins = nc.vector.tensor_copy(part(dst, b), halves(i, b))
                        else:
                            ins = nc.vector.scalar_tensor_tensor(out=part(dst, b), in0=halves(i, b), scalar=float(how),
                                                                 in1=wide(eye64), op0=ALU.mult, op1=ALU.add)
                        ins.then_inc(mat[i], 1)

            masked(3, ((7, m_d),))
            masked(4, ((10, m_dt), (11, m_ot)))
            masked(5, ((12, m_strict),))
            masked(6, ((13, m_incl),))
            masked(7, ((14, m_incl),))
            dve.wait_ge(mat[4], 4)
            for b in range(2):
                nc.vector.scalar_tensor_tensor(out=part(15, b), in0=part(10, b), scalar=-1.0, in1=wide(eye64),
                                               op0=ALU.mult, op1=ALU.add).then_inc(imdt_made, 1)
            with_eye(8, ((1, 0), (2, 1)))
            with_eye(10, ((7, 1),))
            with_eye(14, ((4, 0), (7, -1)))
            with_eye(16, ((11, 0), (15, 1)))
            with_eye(18, ((4, 1),))
            states = [flat(10)[:, 256 * i:256 * i + 256].rearrange("p (b i) -> p b i", b=RBLK) for i in range(3)]
            small = lambda bank: ps[:, bank, 0:256].rearrange("p (b i) -> p b i", b=RBLK)
            uall = slot[11][:].rearrange("p c (b i) -> p c b i", b=RBLK)
            for c in range(NRCH):
                dve.wait_ge(ch_x, c + 1)
                if c == 0:
                    dve.wait_ge(mat[20], 2)
                nc.vector.tensor_copy(states[2], small(0)).then_inc(ch_xs, 1)
                dve.wait_ge(ch_u, c + 1)
                nc.vector.tensor_scalar(uall[:, c], small(1), -1.0, None, ALU.mult).then_inc(ch_us, 1)
                if c == NRCH - 1:
                    break
                dve.wait_ge(ch_s, c + 1)
                fade = pend[:, :, c:c + 1].broadcast_to([P, RBLK, 64])
                if c == 0:
                    nc.vector.tensor_tensor(states[0], small(2), fade, ALU.mult).then_inc(ch_st, 1)
                else:
                    link(nc.vector.tensor_tensor(states[c % 2], states[(c - 1) % 2], small(2), ALU.add))
                    nc.vector.tensor_tensor(states[c % 2], states[c % 2], fade, ALU.mult).then_inc(ch_st, 1)
            for b in range(2):
                dve.wait_ge(y_mean, b + 1)
                y = slot[12][:, 2 * b:2 * b + 2, :]
                nc.vector.tensor_tensor(y, y, ps[:, 6 + b, :].rearrange("p (b t) -> p b t", b=2), ALU.subtract).then_inc(yc_made, 1)
            for b in range(2):
                dve.wait_ge(y_rstd, b + 1)
                for k in (2 * b, 2 * b + 1):
                    own.mark(nc.vector.scalar_tensor_tensor(out=slot[15][:, k, :], in0=slot[12][:, k, :],
                                                            scalar=col("rw_lnw", k), in1=slot[14][:, k, :], op0=ALU.mult,
                                                            op1=ALU.mult))
                own.wait()
                for k in (2 * b, 2 * b + 1):
                    own.mark(nc.vector.scalar_tensor_tensor(out=slot[15][:, k, :], in0=slot[15][:, k, :],
                                                            scalar=col("rw_lnb", k), in1=slot[9][:, k, :], op0=ALU.add,
                                                            op1=ALU.add))
                own.wait()
                dve.wait_ge(g_proj, b + 1)
                nc.vector.tensor_tensor(slot[15][:, 2 * b:2 * b + 2, :], slot[15][:, 2 * b:2 * b + 2, :],
                                        ps[:, 2 + b, :].rearrange("p (b t) -> p b t", b=2), ALU.mult).then_inc(ro_made, 1)
            for b in range(2):
                dve.wait_ge(ro_hi, b + 1)
                nc.vector.tensor_tensor(xB[:, 4 + 2 * b:6 + 2 * b, 1, :], slot[15][:, 2 * b:2 * b + 2, :],
                                        xB[:, 4 + 2 * b:6 + 2 * b, 0, :].bitcast(F32), ALU.subtract).then_inc(ro_lo, 1)
            add_projection("hy_o")
            root(N_FF2)
            scale_x(OUT_FF2, xA, "ff_norm0")
            ffn(2)

            def ple(i):
                n, o = (N_PL0, OUT_PL0) if i == 0 else (N_PL1, OUT_PL1)
                c0 = C0[f"pl_p{i}"]
                dve.wait_ge(p_hi, i + 1)
                nc.vector.tensor_tensor(pl_x[:, :, 1, :], pl_in[:], pl_x[:, :, 0, :].bitcast(F32),
                                        ALU.subtract).then_inc(p_lo, 1)
                root(n)
                scale_x(o, xA, f"pl_gnorm{i}")
                split_lo(Chunk(c0).ahead())
                dve.wait_ge(e_std, i + 1)
                link(nc.vector.reciprocal(pl_rs[:], pl_rs[:]))
                for k in range(KD):
                    own.mark(nc.vector.scalar_tensor_tensor(out=pl_e[:, k, :], in0=pl_e[:, k, :],
                                                            scalar=col(f"pl_norm{i}", k), in1=pl_rs[:], op0=ALU.mult,
                                                            op1=ALU.mult))
                own.wait()
                for g in range(4):
                    c = Chunk(c0 + 1 + g)
                    split_lo(c.ahead())
                    dve.wait_ge(g_on, 4 * i + g + 1)
                    link(nc.vector.tensor_tensor(pl_sg[g % 2][:], pl_sg[g % 2][:], pl_e[:, 2 * g:2 * g + 2, :], ALU.mult))
                    nc.vector.tensor_tensor(hT[:, 2 * g:2 * g + 2, :], hT[:, 2 * g:2 * g + 2, :], pl_sg[g % 2][:],
                                            ALU.add).then_inc(h_updated, 1)

            ple(0)
            root(N_ML)
            scale_x(OUT_ML, xA, "at_norm1")
            dve.wait_ge(ml_landed, 32)
            two_pi = 2 * np.pi
            c1 = 6.28125
            c2 = float(np.float32(np.round((two_pi - c1) * 2 ** 20) / 2 ** 20))
            c3 = float(np.float32(two_pi - c1 - c2))
            magic = 1.5 * 2.0 ** 23
            link(nc.vector.tensor_copy(ml_ang, ml_pos[:]))
            link(nc.vector.tensor_scalar(ml_ang, ml_ang, col("freq"), None, ALU.mult))
            link(nc.vector.tensor_scalar(ml_n, ml_ang, 1.0 / two_pi, col("turn"), ALU.mult, ALU.add))
            link(nc.vector.tensor_scalar(ml_n, ml_n, magic, None, ALU.add))
            link(nc.vector.tensor_scalar(ml_n, ml_n, magic, None, ALU.subtract))
            for c in (c1, c2, c3):
                link(nc.vector.scalar_tensor_tensor(out=ml_ang, in0=ml_n, scalar=-c, in1=ml_ang, op0=ALU.mult, op1=ALU.add))
            link(nc.vector.tensor_scalar(ml_ang, ml_ang, col("phase"), None, ALU.add))
            lim = 3.1415925
            nc.vector.tensor_scalar(ml_ang, ml_ang, lim, -lim, ALU.min, ALU.max).then_inc(cs_arg, 1)
            for g in range(3):
                split_lo(Chunk(C0["ml_d"] + g).ahead())
            dve.wait_ge(c_evac, 3)
            dve.wait_ge(cs_made, 1)
            nc.vector.tensor_tensor(ml_kr[64:128, :], half(2, 1)[64:128], ml_cs[64:128, :], ALU.mult).then_inc(kr_made, 1)
            for j in range(2):
                dve.wait_ge(c_std, j + 1)
                link(nc.vector.reciprocal(ml_rs[:, j, :], ml_rs[:, j, :]))
                for k in ((0, 1, 2), (3, 4))[j]:
                    gain = col("q_norm", k) if j == 0 else col("c_norm", k - 3)
                    nc.vector.scalar_tensor_tensor(out=xt[:, k, :], in0=ml_c[:, k, :], scalar=gain, in1=ml_rs[:, j, :],
                                                   op0=ALU.mult, op1=ALU.mult).then_inc(c_made, 1)
                for k in ((0, 1, 2), (3, 4))[j]:
                    dve.wait_ge(c_hi, k + 1)
                    nc.vector.tensor_tensor(xB[:, k, 1, :], xt[:, k, :], xB[:, k, 0, :].bitcast(F32),
                                            ALU.subtract).then_inc(c_lo, 1)
            dve.wait_ge(fold_done, 2)
            src = ps[64:128, 7, 0:T].unsqueeze(1).broadcast_to([64, HEADS // 2, T])
            nc.vector.tensor_copy(ml_k[64:128, HEADS // 2:HEADS, :], src).then_inc(kr_spread, 1)
            for g in range(20):
                if g in (0, 2, 5, 8, 12, 16):
                    split_lo(Chunk(C0["ml_q"] + (0, 2, 5, 8, 12, 16).index(g)).ahead())
                if g < 8:
                    wait_up(dve, g)
                    nc.vector.scalar_tensor_tensor(
                        out=ml_q[64:128, 2 * g:2 * g + 2, :], in0=ps[64:128, g % 4, :].rearrange("p (b t) -> p b t", b=2),
                        scalar=MLA_SCALE, in1=ml_cs[64:128, :].unsqueeze(1).broadcast_to([64, 2, T]), op0=ALU.mult,
                        op1=ALU.mult).then_inc(ml_rope, 1)
            attention(1, ml_pr, ml_st, lambda h, t: ml_bias[:, P:T] if t == 0 else ml_bias[:, 0:T])
            add_projection("ml_o")
            root(N_FF3)
            scale_x(OUT_FF3, xA, "ff_norm1")
            ffn(3)
            ple(1)
            root(N_FIN2)
            for k in range(KD):
                nc.vector.scalar_tensor_tensor(out=xt[:, k, :], in0=hT[:, k, :], scalar=col("fin2", k), in1=rs[:],
                                               op0=ALU.mult, op1=ALU.mult).then_inc(xt_made, 1)

        @block.tensor
        def _(pe):
            def three(out, wh, wl, xh, xl, start, stop):
                nc.tensor.matmul(out, wh, xh, start=start, stop=False, skip_group_check=True)
                nc.tensor.matmul(out, wh, xl, start=False, stop=False, skip_group_check=True)
                return nc.tensor.matmul(out, wl, xh, start=False, stop=stop, skip_group_check=True)

            def three_natural(out, xh, xl, wh, wl, start, stop):
                nc.tensor.matmul(out, xh, wh, start=start, stop=False, skip_group_check=True)
                nc.tensor.matmul(out, xh, wl, start=False, stop=False, skip_group_check=True)
                return nc.tensor.matmul(out, xl, wh, start=False, stop=stop, skip_group_check=True)

            def plain(out, lhsT, rhs, start=True, stop=True):
                return nc.tensor.matmul(out, lhsT, rhs, start=start, stop=stop, skip_group_check=True)

            def weight(c, i, n=1):
                return w_hi[c.slot][:, P * i:P * (i + n)], w_lo[c.slot][:, P * i:P * (i + n)]

            def sum_squares(n):
                for b in range(4):
                    pe.wait_ge(sq_made, 4 * n + b + 1)
                    for k in (2 * b, 2 * b + 1):
                        last = plain(half(4, 0), ones, xt[:, k, :], start=k == 0, stop=k == KD - 1)
                last.then_inc(ss_summed, 1)

            def wide_chunk(c, bank, x, ready=None):
                pe.wait_ge(lo_made, c.count(1))
                for k in range(KD):
                    if ready is not None:
                        ready(k)
                    for b in range(2):
                        last = three(half(bank, b), *weight(c, 2 * k + b), x[:, k, 0, :], x[:, k, 1, :],
                                     k == 0 and b == 0, k == KD - 1)
                last.then_inc(chunk_used, 1)

            def natural_chunk(c, bank, x, ready=None):
                pe.wait_ge(lo_made, c.count(1))
                for k in range(KD):
                    if ready is not None:
                        ready(k)
                    for t in range(2):
                        last = three_natural(half(bank, t), x[:, k, 0, P * t:P * t + P], x[:, k, 1, P * t:P * t + P],
                                             *weight(c, 2 * k, 2), k == 0 and t == 0, k == KD - 1)
                last.then_inc(chunk_used, 1)

            def x_ready(o):
                def ready(k):
                    if k % 2 == 0:
                        pe.wait_ge(x_lo_made, 4 * o + k // 2 + 1)
                return ready

            def ffn(f, n, o):
                c0, base, both = C0[f"up{f}"], PAIRS * f, f < 2
                up_used = up_conv if both else prod_made

                def pair(q, par, cu, cg, ready=None, first=False):
                    if not first:
                        pe.wait_ge(up_used, q + (base - 1))
                    wide_chunk(cu, 2 * par, xA, ready)
                    if not first:
                        pe.wait_ge(gate_conv, q + (base - 1))
                    wide_chunk(cg, 2 * par + 1, xA)

                def down(d, c, start=False, stop=False):
                    pe.wait_ge(lo_made, c.count(1))
                    pe.wait_ge(hid_lo, d + (base + 1))
                    for b in range(KD):
                        for k in range(2):
                            if isinstance(d, int):
                                xh, xl = hid[:, 2 * d + k, 0, :], hid[:, 2 * d + k, 1, :]
                            else:
                                xh, xl = [rows(hid, d * 2 + k, 1, i).rearrange("p a t -> p (a t)") for i in range(2)]
                            last = three(half(4 + b // 2, b % 2), *weight(c, KD * k + b), xh, xl,
                                         start and k == 0 and b % 2 == 0, stop and k == 1)
                        if stop and b % 2 and b < KD - 1:
                            last.then_inc(down_bank, 1)
                    last.then_inc(chunk_used, 1)

                sum_squares(n)
                pair(0, 0, Chunk(c0), Chunk(c0 + 1), x_ready(o), True)
                pair(1, 1, Chunk(c0 + 2), Chunk(c0 + 3), None, True)
                pair(2, 0, Chunk(c0 + 4), Chunk(c0 + 5))
                with pe.Fori(0, (PAIRS - 3) // 2) as it:
                    for j in range(2):
                        pair(it * 2 + (3 + j), (3 + j) % 2, Chunk(c0 + 6 + 2 * j, it), Chunk(c0 + 7 + 2 * j, it))
                d0 = C0[f"dn{f}"]
                down(0, Chunk(d0), start=True)
                with pe.Fori(0, 2) as it:
                    for s in range(RING):
                        down(it * RING + (1 + s), Chunk(d0 + 1 + s, it))
                down(9, Chunk(d0 + 9))
                down(10, Chunk(d0 + 10), stop=True)

            def attention(a, q, k, v, pr, pt):
                h0, m0 = HEADS * a, KD * a

                def scores(h):
                    if h >= 2:
                        pe.wait_ge(max_made, h0 + h - 1)
                    plain(ps[:, h % 2, 0:P], q(h)[:, 0:P], k(h)[:, 0:P])
                    plain(ps[:, h % 2, P:384], q(h)[:, P:T], k(h)).then_inc(scored, 1)

                def turn(h):
                    pe.wait_ge(prob_made, h0 + h + 1)
                    if h >= 2:
                        pe.wait_ge(turned_copied, h0 + h - 1)
                    for i in range(3):
                        last = nc.tensor.transpose(ps[:, 2 + h % 2, P * i:P * i + P], pr[h % 2][:, P * i:P * i + P], eye)
                    last.then_inc(prob_turned, 1)

                def mix(h):
                    pe.wait_ge(turned_copied, h0 + h + 1)
                    m, r = h // 2, 64 * (h % 2)
                    if m >= 4 and h % 2 == 0:
                        pe.wait_ge(o_lo, m0 + m - 3)
                    out = half(4 + m % 4, 0)[r:r + 64]
                    plain(out, v[:, 0, 64 * h:64 * h + 64], pt[h % 2][:, 0:T], stop=False)
                    plain(out[:, P:T], v[:, 1, 64 * h:64 * h + 64], pt[h % 2][:, T:384], start=False).then_inc(mixed, 1)

                for i in range(HEADS + 2):
                    if i < HEADS:
                        scores(i)
                    if 1 <= i <= HEADS:
                        turn(i - 1)
                    if i >= 2:
                        mix(i - 2)

            def project(name, x, ready):
                for g in range(4):
                    wide_chunk(Chunk(C0[name] + g), 4 + g, x, ready if g == 0 else None)

            pe.wait_ge(vec_landed, 32)
            sum_squares(N_GM)
            for g in range(4):
                natural_chunk(Chunk(g), g, xA, x_ready(OUT_GM) if g == 0 else None)
            for g in range(4, 8):
                pe.wait_ge(gm_evac, g - 3)
                wide_chunk(Chunk(g), g % 4, xA)
            pe.wait_ge(gm_masked, 1)
            pe.wait_ge(gm_scaled, 2)
            for k in range(KD):
                for t in range(2):
                    last = plain(half(4 + k // 2, k % 2)[:, P * t:P * t + P], vnat[:, t, P * k:P * k + P], wsT[:, k, :])
                if k % 2:
                    last.then_inc(gm_mixed, 1)
            project("gm_o", xB, x_ready(OUT_GATED))
            ffn(0, N_FF0, OUT_FF0)
            sum_squares(N_AT)
            for g in range(12):
                if g >= 4:
                    pe.wait_ge(qkv_evac, g - 3)
                x, o = (xB, OUT_KV) if g < 8 else (xA, OUT_Q)
                (natural_chunk if 4 <= g < 8 else wide_chunk)(Chunk(C0["at_k"] + g), g % 4, x,
                                                              x_ready(o) if g in (0, 8) else None)
            pe.wait_ge(qkv_evac, 12)
            attention(0, lambda h: at_qT[:, h // 2, :], lambda h: at_k[:, h, :], at_v, at_pr, at_pt)
            pe.wait_ge(o_lo, 8)
            project("at_o", xB, None)
            ffn(1, N_FF1, OUT_FF1)
            sum_squares(N_FIN1)
            sum_squares(N_HY)

            def stick_scores(u):
                if u >= 2:
                    pe.wait_ge(arg_made, u - 1)
                for i in range(2):
                    h, bank = 2 * u + i, 4 + 2 * (u % 2) + i
                    plain(ps[:, bank, 0:T], sb_k[:, h, 0:P], sb_q[:, u, :])
                    last = plain(ps[:, bank, T:384], sb_k[:, h, P:T], sb_q[:, u, P:T])
                last.then_inc(z_made, 1)

            def stick_after(u):
                pe.wait_ge(log_made, u + 1)
                for i in range(2):
                    bank = 4 + 2 * (u % 2) + i
                    plain(ps[:, bank, 0:384], h_after, sb_lm[:, i, :], stop=False)
                    last = plain(ps[:, bank, P:T], ones, sb_lm[:, i, T:384], start=False)
                last.then_inc(after_made, 1)

            def stick_mix(u):
                pe.wait_ge(w_masked, u + 1)
                if u >= 1:
                    pe.wait_ge(sb_lo, u)
                for i in range(2):
                    h, out = 2 * u + i, half(3, u % 2)[64 * i:64 * i + 64]
                    plain(out, sb_v[:, 0, 64 * h:64 * h + 64], sb_ls[u % 2][:, i, 0:T], stop=False)
                    last = plain(out[:, P:T], sb_v[:, 1, 64 * h:64 * h + 64], sb_ls[u % 2][:, i, T:384], start=False)
                last.then_inc(sb_mixed, 1)

            c0 = C0["hy"]
            for g in range(14):
                if 3 <= g < 9:
                    pe.wait_ge(hy_evac, g - 2)
                elif g >= 9:
                    pe.wait_ge(hy_mixed, g - 8)
                if g in (4, 5):
                    natural_chunk(Chunk(c0 + g), g % 3, xA)
                else:
                    wide_chunk(Chunk(c0 + g), g % 3, xA, x_ready(OUT_HY) if g == 0 else None)
                j = g - 6
                if j == 0:
                    pe.wait_ge(hy_evac, 6)
                    pe.wait_ge(hy_landed, 32)
                if 0 <= j < 4:
                    stick_scores(j)
                if 1 <= j <= 4:
                    stick_after(j - 1)
                if 2 <= j <= 5:
                    stick_mix(j - 2)
            pe.wait_ge(lora_landed, 16)
            pe.wait_ge(lora_in, 1)
            for t in range(2):
                plain(ps[:, 4 + t, :], wlal[:, P * t:P * t + P], lora_w[:, 0, :]).then_inc(w_proj, 1)
            for b in range(RBLK):
                last = plain(half(6 + b // 2, b % 2), lora_w[:, 1, P * b:P * b + P], wlal[:])
                if b % 2:
                    last.then_inc(a_proj, 1)
            pe.wait_ge(w_sig, 2)
            pe.wait_ge(sb_lo, 4)
            pe.wait_ge(lora_in, 2)
            for t in range(2):
                for b in range(RBLK):
                    last = plain(half(b, t), flat(3)[:, 512 * t + P * b:512 * t + P * b + P], h_cum)
            last.then_inc(cum_made, 1)

            def head_sums(bank, src, mat_, signal, ready):
                for b in range(RBLK):
                    ready(b)
                    last = plain(half(bank + b // 2, b % 2), mat_, slot[src][:, b, :])
                    if b % 2:
                        last.then_inc(signal, 1)

            pe.wait_ge(kk_sq, 1)
            pe.wait_ge(w_arg, 2)
            head_sums(4, 9, h_sum, kk_ss, lambda b: None)
            pe.wait_ge(a_sig, 1)
            head_sums(6, 9, h_sum, rk_sum, lambda b: pe.wait_ge(rk_made, b // 2 + 1) if b % 2 == 0 else None)

            def tile(d, hf, p, c):
                return slot[d][64 * hf:64 * hf + 64, p, RCH * c:RCH * c + RCH]

            def product(i, lhs, rhs, needs, used=None):
                for b in range(2):
                    for j, n in needs:
                        pe.wait_ge(mat[j], n * (b + 1))
                    if i >= 4:
                        pe.wait_ge(mat[i - 4], EVACS.get(i - 4, 1) * (b + 1))
                    for p in (2 * b, 2 * b + 1):
                        for c in range(NRCH):
                            at = ((p % 2) * NRCH + c) * RCH
                            for hf in range(2):
                                out = ps[64 * hf:64 * hf + 64, 2 * (i % 4) + b, at:at + RCH]
                                right = eye[64 * hf:64 * hf + 64, 64 * hf:64 * hf + 64] if rhs is None else tile(rhs, hf, p, c)
                                last = plain(out, tile(lhs, hf, p, c), right)
                    last.then_inc(mat_done, 1)

            pe.wait_ge(factors, 5)
            product(0, 4, None, ())
            product(1, 1, None, ())
            product(2, 2, None, ())
            pe.wait_ge(bonus_made, 2)
            product(3, 8, 4, ())
            product(4, 4, 8, ())
            product(5, 1, 8, ())
            product(6, 4, 0, ())
            product(7, 1, 0, ())
            product(8, 10, 7, ((3, 1), (4, 2)))
            product(9, 7, 10, ((3, 1), (4, 2)))
            product(10, 4, 1, ((8, 2), (9, 1)))
            pe.wait_ge(imdt_made, 2)
            product(11, 2, 15, ((8, 2),))
            product(12, 7, 10, ((10, 1), (11, 1)))
            product(13, 1, None, ((12, 1),))
            product(14, 11, 2, ((13, 1),))
            product(15, 2, 11, ((13, 1),))
            product(16, 10, 4, ((14, 2), (15, 1)))
            product(17, 4, 10, ((14, 2), (15, 1)))
            product(18, 2, 11, ((16, 2), (17, 1)))
            product(19, 7, 1, ((14, 2), (12, 1)))
            product(20, 15, 10, ((16, 2), (19, 1)))
            product(21, 4, 7, ((18, 1), (20, 1)))
            for i in range(18, 22):
                pe.wait_ge(mat[i], 2)
            pe.wait_ge(mat[2], 2)

            def each():
                for p in range(RBLK):
                    for hf in range(2):
                        yield p, slice(64 * hf, 64 * hf + 64), hf

            def state(i, p, s):
                return flat(10)[s, 256 * i + 64 * p:256 * i + 64 * p + 64]

            for c in range(NRCH):
                if c:
                    pe.wait_ge(ch_st, c)
                for p, s, hf in each():
                    last = plain(ps[s, 0, 64 * p:64 * p + 64], tile(12, hf, p, c), tile(6, hf, p, c), stop=c == 0)
                    if c:
                        last = plain(ps[s, 0, 64 * p:64 * p + 64], tile(8, hf, p, c), state((c - 1) % 2, p, s), start=False)
                last.then_inc(ch_x, 1)
                pe.wait_ge(ch_xs, c + 1)
                for p, s, hf in each():
                    last = plain(ps[s, 1, 64 * p:64 * p + 64], tile(1, hf, p, c), state(2, p, s))
                last.then_inc(ch_u, 1)
                pe.wait_ge(ch_us, c + 1)

                def u(p, s):
                    return slot[11][s, c, 64 * p:64 * p + 64]

                if c < NRCH - 1:
                    for p, s, hf in each():
                        plain(ps[s, 2, 64 * p:64 * p + 64], tile(3, hf, p, c), u(p, s), stop=False)
                        last = plain(ps[s, 2, 64 * p:64 * p + 64], tile(5, hf, p, c), tile(6, hf, p, c), start=False)
                    last.then_inc(ch_s, 1)
                for p, s, hf in each():
                    out = ps[s, 4 + p // 2, T * (p % 2) + RCH * c:T * (p % 2) + RCH * c + RCH]
                    if c:
                        plain(out, state((c - 1) % 2, p, s), tile(0, hf, p, c), stop=False)
                    plain(out, u(p, s), tile(13, hf, p, c), start=c == 0, stop=False)
                    last = plain(out, tile(6, hf, p, c), tile(14, hf, p, c), start=False)
            last.then_inc(ch_y, 1)
            for b in range(RBLK):
                for k in range(2):
                    last = plain(half(2 + b // 2, b % 2), lora_w[:, 2 + k, P * b:P * b + P], gl[:, k, :], k == 0, k == 1)
                if b % 2:
                    last.then_inc(g_proj, 1)
            head_sums(6, 12, h_mean, y_mean, lambda b: pe.wait_ge(y_made, b // 2 + 1) if b % 2 == 0 else None)
            head_sums(0, 13, h_mean, y_var, lambda b: pe.wait_ge(y_sq, b // 2 + 1) if b % 2 == 0 else None)
            pe.wait_ge(ro_lo, 2)
            project("hy_o", xB, None)
            ffn(2, N_FF2, OUT_FF2)

            def ple(i):
                n, o = (N_PL0, OUT_PL0) if i == 0 else (N_PL1, OUT_PL1)
                c = Chunk(C0[f"pl_p{i}"])
                sum_squares(n)
                pe.wait_ge(p_lo, i + 1)
                pe.wait_ge(lo_made, c.count(1))
                for b in range(KD):
                    for k in range(2):
                        last = three(half(b // 2, b % 2), *weight(c, KD * k + b), pl_x[:, k, 0, :], pl_x[:, k, 1, :],
                                     k == 0, k == 1)
                    if b % 2 and b < KD - 1:
                        last.then_inc(e_done, 1)
                last.then_inc(chunk_used, 1)
                for b in range(4):
                    pe.wait_ge(e_evac, 4 * i + b + 1)
                    for k in (2 * b, 2 * b + 1):
                        last = plain(half(5, 0), ones, pl_sq[:, k, :], k == 0, k == KD - 1)
                last.then_inc(e_ss, 1)
                for g in range(4):
                    wide_chunk(Chunk(C0[f"pl_g{i}"] + g), g, xA, x_ready(o) if g == 0 else None)

            ple(0)
            sum_squares(N_ML)
            for g in range(3):
                wide_chunk(Chunk(C0["ml_d"] + g), g, xA, x_ready(OUT_ML) if g == 0 else None)
            for j, ks in enumerate(((0, 1, 2), (3, 4))):
                for k in ks:
                    pe.wait_ge(c_evac, k // 2 + 1)
                    last = plain(half(4 + j, 0), ones, xt[:, k, :], k == ks[0], k == ks[-1])
                last.then_inc(c_ss, 1)
            pe.wait_ge(kr_made, 1)
            for bank in (6, 7):
                plain(ps[:, bank, 0:T], ml_fold[64:128, :], ml_kr[64:128, :]).then_inc(fold_done, 1)
            group = 0
            pe.wait_ge(c_evac, 3)
            for kn, name, k0 in ((3, "ml_q", 0), (2, "ml_k", 3)):
                for i in range(HEADS * kn):
                    h, k = divmod(i, kn)
                    c = Chunk(C0[name] + i // 16)
                    if i % 16 == 0:
                        pe.wait_ge(lo_made, c.count(1))
                    if h % 2 == 0 and k == 0:
                        g = h // 2 + (8 if kn == 2 else 0)
                        if g >= 4:
                            pe.wait_ge(ml_evac, g - 3)
                            if g < 12:
                                pe.wait_ge(ml_rope, g - 3)
                    if i < kn:
                        pe.wait_ge(c_lo, k0 + k + 1)
                    last = three(half(g % 4, h % 2), *weight(c, i % 16), xB[:, k0 + k, 0, :], xB[:, k0 + k, 1, :],
                                 k == 0, k == kn - 1)
                    if i % 16 == 15:
                        last.then_inc(chunk_used, 1)
                    elif h % 2 and k == kn - 1:
                        last.then_inc(up_done, 1)
            c = Chunk(C0["ml_v"])
            pe.wait_ge(lo_made, c.count(1))
            for i in range(4):
                t, n = divmod(i, 2)
                pe.wait_ge(ml_evac, 16 + i - 3)
                for k in range(2):
                    last = three_natural(ps[:, (16 + i) % 4, :], xB[:, 3 + k, 0, P * t:P * t + P], xB[:, 3 + k, 1, P * t:P * t + P],
                                         *weight(c, KD * k + 4 * n, 4), k == 0, k == 1)
                last.then_inc(chunk_used if i == 3 else up_done, 1)
            pe.wait_ge(ml_evac, 20)
            pe.wait_ge(ml_rope, 8)
            pe.wait_ge(kr_spread, 2)
            attention(1, lambda h: ml_q[:, h, :], lambda h: ml_k[:, h, :], ml_v, ml_pr, ml_pt)
            pe.wait_ge(o_lo, 16)
            project("ml_o", xB, None)
            ffn(3, N_FF3, OUT_FF3)
            ple(1)
            sum_squares(N_FIN2)


def _cols(v):
    v = np.asarray(v).reshape(-1)
    return v.reshape(-1, P).T


def _chunks(blocks):
    return blocks.transpose(0, 2, 1, 3).reshape(-1, P, CHUNK)


def _by_columns(w):
    n = w.shape[1] // 256
    return w.reshape(KD, P, n, 256).transpose(2, 1, 0, 3).reshape(n, P, CHUNK)


def _by_rows(w):
    n = w.shape[0] // 256
    return w.reshape(n, 2, P, D).transpose(0, 2, 1, 3).reshape(n, P, CHUNK)


def _paired(w):
    up, gate = _by_columns(w[:, :FF]), _by_columns(w[:, FF:])
    return np.stack([up, gate], 1).reshape(-1, P, CHUNK)


def _by_heads(w):
    k, h = w.shape[0] // P, w.shape[1] // P
    return _chunks(w.reshape(k, P, h, P).transpose(2, 0, 1, 3).reshape(-1, 16, P, P))


def _constants():
    i = np.arange(P)
    s = np.arange(64)
    eye, ones = np.eye(P), np.ones((P, P))
    after = (i[:, None] > i[None, :])
    tri = (i[:, None] < i[None, :])
    head = (i[:, None] // 64 == i[None, :] // 64)
    cum = head * (i[:, None] <= i[None, :]) * DECAY
    cum_x = head * (i[:, None] < i[None, :]) * DECAY
    d = (s[:, None] > s[None, :]) & (s[:, None] // 8 == s[None, :] // 8)
    dt = d.T
    ot = (s[:, None] < s[None, :]) & ~dt
    strict, incl = s[:, None] < s[None, :], s[:, None] <= s[None, :]
    small = [np.concatenate([m, m], 0) for m in (d, dt, ot, strict, incl, np.eye(64))]
    hyc = np.concatenate([eye, ones, after, tri, head, head / 64.0, cum, cum_x] + small, 1)
    causal = np.where(i[None, :] <= i[:, None], 0.0, NEG)
    fold = (i[:, None] >= 64) & (i[:, None] % 32 == i[None, :] % 32)
    mlc = np.concatenate([np.zeros((P, P)), causal, fold], 1)
    return np.ascontiguousarray(hyc, np.float32), np.ascontiguousarray(mlc, np.float32)


def kernel(**inputs):
    import concourse.bacc as bacc
    from concourse.bass_utils import run_bass_kernel_spmd

    a = {k: np.asarray(v) for k, v in inputs.items()}
    f32 = np.float32

    def zeros(*shape):
        return np.zeros(shape, f32)

    hyb = np.concatenate([a["hyb_w_in_2"][0], zeros(D, 14 * 256 - a["hyb_w_in_2"].shape[2])], 1)
    down = a["mla_w_down_2"][0]
    kr = down[:, 640:672]
    kr_swap = np.concatenate([kr[:, 16:], kr[:, :16]], 1)
    down = np.concatenate([down[:, :640], zeros(D, 64), kr, kr_swap], 1)
    uq = a["mla_w_uq_2"][0].reshape(384, HEADS, 96)
    uq = np.concatenate([uq, uq[:, :, 80:96], uq[:, :, 64:80]], 2).reshape(384, HEADS * P)
    ukv = a["mla_w_ukv_2"][0].reshape(256, HEADS, P)
    uk = np.concatenate([ukv[:, :, :64], zeros(256, HEADS, 64)], 2).reshape(256, HEADS * P)
    uv = np.ascontiguousarray(ukv[:, :, 64:]).reshape(256, HEADS * 64)
    a_in, kv = a["a_w_in"][0], a["w_kv"]
    parts = [_by_columns(a_in[:, D:]), _by_columns(a_in[:, :D]), _by_columns(a["a_w_out"][0]),
             _paired(a["f_w_in"][0]), _by_rows(a["f_w_down"][0]),
             _by_columns(kv[:, :D]), _by_columns(kv[:, D:]), _by_columns(a["b_w_q"][0]), _by_columns(a["b_w_o"][0]),
             _paired(a["f_w_in"][1]), _by_rows(a["f_w_down"][1]),
             _by_columns(hyb), _by_columns(a["hyb_w_out_2"][0]),
             _paired(a["ffn_w_in_2"][0]), _by_rows(a["ffn_w_out_2"][0]),
             _by_rows(a["ple_w_proj_2"][0]), _by_columns(a["ple_w_gate_2"][0]),
             _by_columns(down), _by_heads(uq), _by_heads(uk), _by_rows(uv), _by_columns(a["mla_w_o_2"][0]),
             _paired(a["ffn_w_in_2"][1]), _by_rows(a["ffn_w_out_2"][1]),
             _by_rows(a["ple_w_proj_2"][1]), _by_columns(a["ple_w_gate_2"][1])]
    stream = np.concatenate(parts, 0)

    half_freq = (f32(10000.0) ** (-np.arange(16, dtype=f32) / f32(16))).astype(f32)
    freq, phase = zeros(P), zeros(P)
    freq[64:128] = np.tile(half_freq, 4)
    phase[64:96], phase[96:112] = np.pi / 2, np.pi
    vecs = {
        "a_norm": a["a_norm_g"][0], "a_vnorm": a["a_v_norm_g"][0], "kv_norm": a["kv_norm_g"], "b_norm": a["b_norm_g"][0],
        "f_norm0": a["f_norm_g"][0], "f_norm1": a["f_norm_g"][1], "cw0": a["f_conv_w"][0], "cw1": a["f_conv_w"][1],
        "cb0": a["f_conv_b"][0], "cb1": a["f_conv_b"][1], "fin1": a["final_norm_g"],
        "at_norm0": a["attn_norm_2"][0], "at_norm1": a["attn_norm_2"][1], "ff_norm0": a["ffn_norm_2"][0],
        "ff_norm1": a["ffn_norm_2"][1], "cw2": a["ffn_conv_w_2"][0], "cw3": a["ffn_conv_w_2"][1],
        "cb2": a["ffn_conv_b_2"][0], "cb3": a["ffn_conv_b_2"][1], "pl_norm0": a["ple_norm_2"][0],
        "pl_norm1": a["ple_norm_2"][1], "pl_gnorm0": a["ple_gate_norm_2"][0], "pl_gnorm1": a["ple_gate_norm_2"][1],
        "rw_mu": np.concatenate([a["rw_mu_2"][0], zeros(96)]), "rw_a0": a["rw_a0_2"][0], "rw_kk": a["rw_k_k_2"][0],
        "rw_ka": a["rw_k_a_2"][0], "rw_rk": a["rw_r_k_2"][0], "rw_lnw": a["rw_ln_w_2"][0], "rw_lnb": a["rw_ln_b_2"][0],
        "q_norm": a["mla_q_norm_2"][0], "c_norm": a["mla_kv_norm_2"][0], "fin2": a["final_norm_2"],
        "eps": zeros(P) + f32(EPS), "gn_eps": zeros(P) + f32(GN_EPS), "freq": freq, "turn": phase / f32(2 * np.pi),
        "phase": phase, "ln256": zeros(P) + f32(8 * np.log(2.0)),
    }
    packed = np.concatenate([_cols(vecs[name]) for name, _ in _VECS], 1).astype(f32)
    hyc, mlc = _constants()
    rel = a["b_rel_bias"][0][:, ::-1]
    ext = np.concatenate([np.repeat(rel[:, :1], P, 1), rel[:, :256]], 1)
    rel = np.lib.stride_tricks.sliding_window_view(ext, T, 1)[:, P:0:-1].transpose(1, 0, 2)
    lora = np.concatenate([a["rw_w2_2"][0], zeros(64, 512), zeros(64, 512), a["rw_a2_2"][0], a["rw_g2_2"][0],
                           zeros(96, 512)], 0).reshape(4, P, 512).transpose(1, 0, 2)
    arrays = {
        "stream": stream,
        "x_t": a["x"][0].T.reshape(KD, P, T).transpose(1, 0, 2),
        "vecs": packed,
        "wst": a["a_w_s"][0].transpose(2, 0, 1),
        "bsp": a["a_b_s"][0],
        "rel": rel, "hyc": hyc, "w0": a["rw_w0_2"], "lora": lora, "mlc": mlc, "pos": a["positions_2"],
        "p_t": a["p_2"][:, 0].transpose(0, 2, 1).reshape(2, 2, P, T).transpose(0, 2, 1, 3),
    }
    nc = bacc.Bacc("TRN2", target_bir_lowering=False, num_devices=1)
    args = []
    for name in arrays:
        arrays[name] = np.ascontiguousarray(arrays[name])
        args.append(nc.dram_tensor(name, arrays[name].shape, mybir.dt.from_np(arrays[name].dtype),
                                   kind="ExternalInput").ap())
    args.append(nc.dram_tensor("out_t", (P, KD, T), F32, kind="ExternalOutput").ap())
    build(nc, *args)
    r = run_bass_kernel_spmd(nc, [arrays], core_ids=[0])
    got = r.results[0]["out_t"]
    return np.ascontiguousarray(got.transpose(2, 1, 0).reshape(1, T, D))
```

```python
from contextlib import ExitStack

import numpy as np

import concourse.bass as bass
from concourse import mybir

F32 = mybir.dt.float32
F32R = mybir.dt.float32r
I32 = mybir.dt.int32
ALU = mybir.AluOpType
ACT = mybir.ActivationFunctionType
AX_X = mybir.AxisListType.X

P = 128
T = 256
D = 1024
KD = D // P
FF = 2816
KF = FF // P
PAIRS = KF // 2
CHUNK = 16 * P
RING = 4
AHEAD = 3
EPS = 1e-6
GN_EPS = 64e-5
NEG = -1e30
HCON = 6 * 128 + 6 * 64
HEADS = 16
SB_HEADS = 8
RBLK = 4
RCH = 64
NRCH = T // RCH
MLA_SCALE = 96 ** -0.5
DECAY = -float(np.exp(np.float64(-0.5)))

_PLAN = [("gm_v", 4), ("gm_u", 4), ("gm_o", 4), ("up0", 22), ("dn0", 11),
         ("at_k", 4), ("at_v", 4), ("at_q", 4), ("at_o", 4), ("up1", 22), ("dn1", 11),
         ("hy", 14), ("hy_o", 4), ("up2", 22), ("dn2", 11), ("pl_p0", 1), ("pl_g0", 4),
         ("ml_d", 3), ("ml_q", 3), ("ml_k", 2), ("ml_v", 1), ("ml_o", 4),
         ("up3", 22), ("dn3", 11), ("pl_p1", 1), ("pl_g1", 4)]
C0, NCH = {}, 0
for _name, _n in _PLAN:
    C0[_name] = NCH
    NCH += _n

_VECS = [("a_norm", 8), ("a_vnorm", 8), ("kv_norm", 8), ("b_norm", 8), ("f_norm0", 8), ("f_norm1", 8),
         ("cw0", 132), ("cw1", 132), ("cb0", 44), ("cb1", 44), ("fin1", 8),
         ("at_norm0", 8), ("at_norm1", 8), ("ff_norm0", 8), ("ff_norm1", 8),
         ("cw2", 66), ("cw3", 66), ("cb2", 22), ("cb3", 22),
         ("pl_norm0", 8), ("pl_norm1", 8), ("pl_gnorm0", 8), ("pl_gnorm1", 8),
         ("rw_mu", 15), ("rw_a0", 4), ("rw_kk", 4), ("rw_ka", 4), ("rw_rk", 4), ("rw_lnw", 4), ("rw_lnb", 4),
         ("q_norm", 3), ("c_norm", 2), ("fin2", 8),
         ("eps", 1), ("gn_eps", 1), ("freq", 1), ("turn", 1), ("phase", 1), ("ln256", 1)]
VC, NV = {}, 0
for _name, _n in _VECS:
    VC[_name] = NV
    NV += _n

OUT_GM, OUT_GATED, OUT_FF0, OUT_KV, OUT_Q, OUT_FF1, OUT_HY, OUT_FF2, OUT_PL0, OUT_ML, OUT_FF3, OUT_PL1 = range(12)
N_GM, N_FF0, N_AT, N_FF1, N_FIN1, N_HY, N_FF2, N_PL0, N_ML, N_FF3, N_PL1, N_FIN2 = range(12)

FINAL_XT = 8 * 12
FILL = (3, 9)
GATE_BANK = (4, 6, 7, 5)
UNITS = ((0, 1), (1, 2), (2, 4), (4, 6), (6, 8))
EVACS = {4: 2, 8: 2, 14: 2, 16: 2}


def build(nc, stream, x_t, vecs, wst, bsp, rel, hyc, w0, lora, mlc, pos, p_t, out):
    with ExitStack() as ctx:
        def sem(name):
            return ctx.enter_context(nc.semaphore(name))

        def sb(name, shape, dt=F32, where=ctx):
            return where.enter_context(nc.sbuf_tensor(name, shape, dt))

        raw = [sb(f"raw{i}", [P, CHUNK]) for i in range(RING)]
        w_hi = [sb(f"w_hi{i}", [P, CHUNK], F32R) for i in range(RING)]
        w_lo = [sb(f"w_lo{i}", [P, CHUNK], F32R) for i in range(RING)]
        hT = sb("hT", [P, KD, T])
        vec = sb("vec", [P, NV])
        eye_ones = sb("eye_ones", [P, 2 * P])
        rs = sb("rs", [P, T])
        xB = sb("xB", [P, KD, 2, T], F32R)
        with ExitStack() as ph:
            xt = sb("xt", [P, KD, T], where=ph)
            xA = sb("xA", [P, KD, 2, T], F32R, ph)
            with ExitStack() as f:
                hid = sb("hid", [P, KF, 2, T], F32R, f)
                up_acc = [sb(f"up_acc{i}", [P, 2, T], where=f) for i in range(2)]
                gate_acc = [sb(f"gate_acc{i}", [P, 2, T], where=f) for i in range(2)]
                pl_in = sb("pl_in", [P, 2, T], where=f)
                pl_x = sb("pl_x", [P, 2, 2, T], F32R, f)
            with ExitStack() as f:
                uT = sb("uT", [P, KD, T], where=f)
                vnat = sb("vnat", [P, 2, D], where=f)
                wsT = sb("wsT", [P, KD, P], where=f)
                bsb = sb("bsb", [P, KD, P], where=f)
                gm_junk = sb("gm_junk", [P, T], where=f)
                gm_sum = sb("gm_sum", [P, 8], where=f)
                gm_rs = sb("gm_rs", [P, 4], where=f)
            with ExitStack() as f:
                at_qT = sb("at_qT", [P, KD, T], where=f)
                at_k = sb("at_k", [P, KD, T], where=f)
                at_v = sb("at_v", [P, 2, D], where=f)
                at_bias = sb("at_bias", [P, HEADS, T], where=f)
                at_pr = [sb(f"at_pr{i}", [P, 384], where=f) for i in range(3)]
                at_pt = [sb(f"at_pt{i}", [P, 384], where=f) for i in range(2)]
                at_st = sb("at_st", [P, 3, 2 * HEADS], where=f)
            with ExitStack() as f:
                ml_q = sb("ml_q", [P, HEADS, T], where=f)
                ml_k = sb("ml_k", [P, HEADS, T], where=f)
                ml_v = sb("ml_v", [P, 2, D], where=f)
                ml_c = sb("ml_c", [P, 5, T], where=f)
                ml_pr = [sb(f"ml_pr{i}", [P, 384], where=f) for i in range(3)]
                ml_pt = [sb(f"ml_pt{i}", [P, 384], where=f) for i in range(2)]
                ml_st = sb("ml_st", [P, 3, 2 * HEADS], where=f)
                ml_con = sb("ml_con", [P, 384], where=f)
                ml_cs = sb("ml_cs", [P, T], where=f)
                ml_pos = sb("ml_pos", [P, T], I32, f)
                ml_kr = sb("ml_kr", [P, T], where=f)
            ml_bias, ml_fold = ml_con[:, 0:256], ml_con[:, 256:384]
            ml_rs = [t[:, 0:T] for t in ml_pt]
            ml_ang, ml_n = ml_pr[0][:, 0:T], ml_pr[1][:, 0:T]
            with ExitStack() as f:
                pl_e = sb("pl_e", [P, KD, T], where=f)
                pl_sq = sb("pl_sq", [P, KD, T], where=f)
                pl_rb = sb("pl_rb", [P, T], where=f)
                pl_sg = [sb(f"pl_sg{i}", [P, 2, T], where=f) for i in range(2)]
            with ExitStack() as f:
                hcon = sb("hcon", [P, HCON], where=f)
                w0b = sb("w0b", [P, 512], where=f)
                wlal = sb("wlal", [P, T], where=f)
                gl = sb("gl", [P, 2, T], where=f)
                pend = sb("pend", [P, RBLK, NRCH], where=f)
                om_mu = sb("om_mu", [P, 15], where=f)
                slot = [sb(f"slot{i}", [P, RBLK, T], where=f) for i in range(12)]
        with ExitStack() as f:
            lora_w = sb("lora_w", [P, 4, 512], where=f)
            with ExitStack() as g:
                sb_l = [sb(f"sb_l{i}", [P, 2, 384], where=g) for i in range(2)]
                sb_ls = [sb(f"sb_ls{i}", [P, 2, 384], where=g) for i in range(2)]
            slot += [sb(f"slot{i}", [P, RBLK, T], where=f) for i in range(12, 16)]
        sb_q, sb_k, sb_v = slot[7], slot[10], slot[11][:].rearrange("p b t -> p (b t)").rearrange("p (a n) -> p a n", a=2)
        h_after, h_tri, h_sum, h_mean = [hcon[:, P * i:P * i + P] for i in range(4)]
        h_cum = hcon[:, 4 * P:6 * P]
        m_d, m_dt, m_ot, m_strict, m_incl = [hcon[:, 6 * P + 64 * i:6 * P + 64 * i + 64] for i in range(5)]
        ps = ctx.enter_context(nc.psum_tensor("ps", [P, 8, 512], F32))

        eye, ones = eye_ones[:, 0:P], eye_ones[:, P:2 * P]

        def half(bank, h):
            return ps[:, bank, T * h:T * h + T]

        def col(name, j=0, n=1):
            return vec[:, VC[name] + j:VC[name] + j + n]

        def dcol(name, j, off):
            if isinstance(j, int):
                return col(name, off + j)
            return vec[:, bass.ds(j + (VC[name] + off), 1)]

        def rows(tile, k, n, part):
            if isinstance(k, int):
                return tile[:, k:k + n, part, :]
            return tile[:, bass.ds(k, n), part, :]

        raw_landed = [sem(f"raw_landed{i}") for i in range(RING)]
        hi_made = sem("hi_made")
        lo_made = sem("lo_made")
        chunk_used = sem("chunk_used")
        x_landed = [sem(f"x_landed{b}") for b in range(4)]
        vec_landed, eye_landed = sem("vec_landed"), sem("eye_landed")
        gm_landed = sem("gm_landed")
        h_updated = sem("h_updated")
        sq_made = sem("sq_made")
        ss_summed = sem("ss_summed")
        sq_added = sem("sq_added")
        rs_made = sem("rs_made")
        xt_made = sem("xt_made")
        x_hi_made = sem("x_hi_made")
        x_lo_made = sem("x_lo_made")
        dve_own = sem("dve_own")
        act_own = sem("act_own")
        up_lin, gate_lin = sem("up_lin"), sem("gate_lin")
        tap_done = sem("tap_done")
        up_conv, gate_conv = sem("up_conv"), sem("gate_conv")
        gate_on = sem("gate_on")
        prod_made = sem("prod_made")
        hid_hi, hid_lo = sem("hid_hi"), sem("hid_lo")
        down_bank = sem("down_bank")
        gm_evac, gm_sums, gm_std, gm_scaled, gm_mixed, gm_masked = [
            sem(n) for n in ("gm_evac", "gm_sums", "gm_std", "gm_scaled", "gm_mixed", "gm_masked")]
        qkv_evac, bias_ready = sem("qkv_evac"), sem("bias_ready")
        bias_landed, bias_negated = sem("bias_landed"), sem("bias_negated")
        scored, max_made, exp_made, prob_made, prob_turned, turned_copied, mixed = [
            sem(n) for n in ("scored", "max_made", "exp_made", "prob_made", "prob_turned", "turned_copied", "mixed")]
        o_hi, o_lo = sem("o_hi"), sem("o_lo")
        hy_landed, lora_landed = sem("hy_landed"), sem("lora_landed")
        hy_evac, hy_lin, hy_mixed = sem("hy_evac"), sem("hy_lin"), sem("hy_mixed")
        z_made, log_made, stick_made, after_made, arg_made, w_made, w_masked, sb_mixed, sb_hi, sb_lo = [
            sem(n) for n in ("z_made", "log_made", "stick_made", "after_made", "arg_made", "w_made", "w_masked",
                             "sb_mixed", "sb_hi", "sb_lo")]
        (mu_ready, lora_in, w_proj, a_proj, w_arg, w_sig, a_sig, cum_made, decay_made, kk_made, kk_sq, kk_ss, kk_max,
         kk_rn, rk_made, rk_sum, factors, imdt_made, bonus_made) = [sem(n) for n in (
             "mu_ready", "lora_in", "w_proj", "a_proj", "w_arg", "w_sig", "a_sig", "cum_made", "decay_made", "kk_made",
             "kk_sq", "kk_ss", "kk_max", "kk_rn", "rk_made", "rk_sum", "factors", "imdt_made", "bonus_made")]
        mat_done = sem("mat_done")
        mat = [sem(f"mat{i}") for i in range(22)]
        ch_x, ch_xs, ch_u, ch_us, ch_s, ch_st, ch_y = [
            sem(n) for n in ("ch_x", "ch_xs", "ch_u", "ch_us", "ch_s", "ch_st", "ch_y")]
        y_made, y_mean, yc_made, y_sq, y_var, y_rstd, g_proj, ro_made, ro_hi, ro_lo = [
            sem(n) for n in ("y_made", "y_mean", "yc_made", "y_sq", "y_var", "y_rstd", "g_proj", "ro_made", "ro_hi",
                             "ro_lo")]
        p_landed, p_hi, p_lo, e_done, e_evac, e_ss, e_rs, g_on = [
            sem(n) for n in ("p_landed", "p_hi", "p_lo", "e_done", "e_evac", "e_ss", "e_rs", "g_on")]
        ml_landed, cs_arg, cs_made, c_evac, kr_made, c_ss, c_rs, c_made, c_hi, c_lo = [
            sem(n) for n in ("ml_landed", "cs_arg", "cs_made", "c_evac", "kr_made", "c_ss", "c_rs", "c_made", "c_hi",
                             "c_lo")]
        up_done, ml_evac, ml_rope, fold_done, kr_spread = [
            sem(n) for n in ("up_done", "ml_evac", "ml_rope", "fold_done", "kr_spread")]
        stored = sem("stored")

        block = ctx.enter_context(nc.Block())

        def at_least(eng, s, value):
            if not isinstance(value, int) or value > 0:
                eng.wait_ge(s, value)

        def mixed_block(j):
            if j < 3:
                return gl[:, j - 1, :] if j else wlal[:]
            i, b = divmod(j - 3, 4)
            return slot[(1, 0, 2)[i]][:, b, :]

        def product_bank(i, b):
            return (2 * i + b) % 3 if i < 3 else 2 * (i % 4) + b

        def flat(i):
            return slot[i][:].rearrange("p b t -> p (b t)")

        class Own:

            def __init__(self, eng, s):
                self.eng, self.s, self.n = eng, s, 0

            def mark(self, ins):
                ins.then_inc(self.s, 1)
                self.n += 1
                return self.n

            def wait(self, n=None):
                self.eng.wait_ge(self.s, self.n if n is None else n)

        class Chunk:

            def __init__(self, first, it=None):
                self.first, self.it, self.slot = first, it, first % RING

            def count(self, more):
                return self.first + more if self.it is None else self.it * RING + (self.first + more)

            def landed(self):
                n = 16 * (self.first // RING + 1)
                return n if self.it is None else self.it * 16 + n

            def ahead(self):
                if self.it is None and self.first + AHEAD >= NCH:
                    return None
                return Chunk(self.first + AHEAD, self.it)

        ends_chunk = {7: C0["ml_q"] + 2, 11: C0["ml_k"], 15: C0["ml_k"] + 1, 19: C0["ml_v"]}

        def wait_up(eng, g):
            if g in ends_chunk:
                eng.wait_ge(chunk_used, ends_chunk[g] + 1)
            else:
                eng.wait_ge(up_done, g + 1 - sum(e < g for e in ends_chunk))

        @block.sync
        def _(sp):
            sp.dma_start(raw[0][:], stream[0]).then_inc(raw_landed[0], 16)
            sp.dma_start(eye_ones[:], hyc[:, 0:2 * P]).then_inc(eye_landed, 16)
            for b in range(4):
                sp.dma_start(hT[:, 2 * b:2 * b + 2], x_t[:, 2 * b:2 * b + 2]).then_inc(x_landed[b], 16)
            sp.dma_start(vec[:], vecs).then_inc(vec_landed, 16)
            for c in range(1, RING):
                sp.dma_start(raw[c][:], stream[c]).then_inc(raw_landed[c], 16)
            with sp.Fori(1, NCH // RING) as it:
                for s in range(RING):
                    sp.wait_ge(lo_made, it * RING + (s + 1 - RING))
                    src = stream[bass.ds(it * RING + s, 1)].rearrange("a p n -> p (a n)")
                    sp.dma_start(raw[s][:], src).then_inc(raw_landed[s], 16)
            for c in range(NCH // RING * RING, NCH):
                sp.wait_ge(lo_made, c + 1 - RING)
                sp.dma_start(raw[c % RING][:], stream[c]).then_inc(raw_landed[c % RING], 16)
            for b in range(4):
                sp.wait_ge(xt_made, FINAL_XT + 2 * b + 2)
                sp.dma_start(out[:, 2 * b:2 * b + 2], xt[:, 2 * b:2 * b + 2]).then_inc(stored, 16)
            sp.wait_ge(stored, 64)

        @block.gpsimd
        def _(pool):
            def add_squares(n):
                pool.wait_ge(sq_made, 4 * n + 2)
                nc.gpsimd.tensor_tensor(xt[:, 0:2, :], xt[:, 0:2, :], xt[:, 2:4, :], ALU.add).then_inc(sq_added, 1)

            add_squares(N_GM)
            pool.wait_ge(sq_added, N_GM + 1)
            pool.wait_ge(gm_landed, 32)
            nc.gpsimd.memset(wsT[64:128, :, 0:64], 0.0).then_inc(gm_masked, 1)
            add_squares(N_FF0)
            add_squares(N_AT)
            pool.wait_ge(h_updated, 8)
            pool.dma_start(at_bias[:], rel).then_inc(bias_landed, 16)
            pool.wait_ge(sq_added, N_AT + 1)
            pool.wait_ge(bias_landed, 16)
            nc.gpsimd.tensor_scalar(at_bias[:], at_bias[:], -1.0, None, ALU.mult).then_inc(bias_negated, 1)
            pool.wait_ge(bias_negated, 1)
            nc.gpsimd.memset(at_bias[0:64, :, 192:256], -NEG).then_inc(bias_ready, 1)
            add_squares(N_FF1)
            add_squares(N_FIN1)
            pool.wait_ge(h_updated, 16)
            pool.dma_start(hcon[:], hyc[:, 2 * P:]).then_inc(hy_landed, 16)
            pool.dma_start(w0b[:], bass.AP(w0.tensor, 0, [[0, P], [1, 512]])).then_inc(hy_landed, 16)
            add_squares(N_HY)
            pool.wait_ge(x_lo_made, 5 * (OUT_HY + 1))
            pool.dma_start(lora_w[:], lora).then_inc(lora_landed, 16)
            add_squares(N_FF2)
            pool.wait_ge(h_updated, 24)
            pool.dma_start(pl_in[:], p_t[0]).then_inc(p_landed, 16)
            add_squares(N_PL0)
            add_squares(N_ML)
            pool.wait_ge(h_updated, 32)
            pool.dma_start(ml_con[:], mlc).then_inc(ml_landed, 16)
            pool.dma_start(ml_pos[:], bass.AP(pos.tensor, 0, [[0, P], [1, T]])).then_inc(ml_landed, 16)
            add_squares(N_FF3)
            pool.wait_ge(h_updated, 36)
            pool.dma_start(pl_in[:], p_t[1]).then_inc(p_landed, 16)
            add_squares(N_PL1)
            add_squares(N_FIN2)

        @block.scalar
        def _(act):
            own = Own(act, act_own)

            def split_hi(c):
                if c is None:
                    return
                act.wait_ge(raw_landed[c.slot], c.landed())
                at_least(act, chunk_used, c.count(1 - RING))
                nc.scalar.activation(w_hi[c.slot][:], raw[c.slot][:], ACT.Copy).then_inc(hi_made, 1)

            def inverse_root(dst, sums, width, made):
                own.mark(nc.scalar.activation(dst, sums, ACT.Ln, bias=col("eps"), scale=1.0 / width))
                own.wait()
                nc.scalar.activation(dst, dst, ACT.Exp, scale=-0.5).then_inc(made, 1)

            def square(n, b):
                if n == 0:
                    act.wait_ge(x_landed[b], 16)
                else:
                    act.wait_ge(h_updated, 4 * (n - 1) + b + 1)
                if b == 2:
                    nc.scalar.preload_act_table_set("natural_log_exp_and_others")
                nc.scalar.activation(xt[:, 2 * b:2 * b + 2, :], hT[:, 2 * b:2 * b + 2, :],
                                     ACT.Square).then_inc(sq_made, 1)

            def square_norm(n):
                for b in range(4):
                    square(n, b)
                root_norm(n)

            def root_norm(n):
                act.wait_ge(ss_summed, n + 1)
                inverse_root(rs[:], half(4, 0), D, rs_made)

            def round_x(o, dst, ahead=()):
                for u, (lo, hi) in enumerate(UNITS):
                    act.wait_ge(xt_made, 8 * o + hi)
                    nc.scalar.activation(dst[:, lo:hi, 0, :], xt[:, lo:hi, :], ACT.Copy).then_inc(x_hi_made, 1)
                    if u == 2:
                        for c in ahead:
                            split_hi(Chunk(c))

            def split_and_square(name, n, first=0):
                for g in range(4):
                    if g >= first:
                        split_hi(Chunk(C0[name] + g).ahead())
                    if g:
                        square(n, g - 1)
                square(n, 3)
                root_norm(n)

            def ffn(f):
                c0, base, both = C0[f"up{f}"], PAIRS * f, f < 2
                goff = KF if both else 0

                def linear(acc, bank, q, off):
                    for b in range(2):
                        j = 2 * q + b if isinstance(q, int) else q * 2 + b
                        last = nc.scalar.activation(acc[:, b, :], half(bank, b), ACT.Identity,
                                                    bias=dcol(f"cb{f}", j, off),
                                                    scale=dcol(f"cw{f}", j, off + 2 * (goff + KF)))
                    return last

                def gate(q, par):
                    act.wait_ge(gate_conv, q + (base + 1))
                    nc.scalar.activation(gate_acc[par][:], gate_acc[par][:],
                                         ACT.Silu if both else ACT.Gelu).then_inc(gate_on, 1)

                def round_hid(q, par):
                    act.wait_ge(prod_made, q + (base + 1))
                    nc.scalar.activation(rows(hid, q * 2, 2, 0), up_acc[par][:], ACT.Copy).then_inc(hid_hi, 1)

                def pair(q, par, cu, cg, first=False, second=False):
                    split_hi(cu.ahead())
                    if not first:
                        gate(q - 1, 1 - par)
                    if both:
                        act.wait_ge(chunk_used, cu.count(1))
                        if not (first or second):
                            act.wait_ge(hid_lo, q + (base - 1))
                        linear(up_acc[par], 2 * par, q, 0).then_inc(up_lin, 1)
                    split_hi(cg.ahead())
                    if not first:
                        round_hid(q - 1, 1 - par)
                    act.wait_ge(chunk_used, cg.count(1))
                    if not (first or second):
                        act.wait_ge(prod_made, q + (base - 1))
                    linear(gate_acc[par], 2 * par + 1, q, goff).then_inc(gate_lin, 1)

                pair(0, 0, Chunk(c0), Chunk(c0 + 1), first=True)
                pair(1, 1, Chunk(c0 + 2), Chunk(c0 + 3), second=True)
                pair(2, 0, Chunk(c0 + 4), Chunk(c0 + 5))
                with act.Fori(0, (PAIRS - 3) // 2) as it:
                    for j in range(2):
                        pair(it * 2 + (3 + j), (3 + j) % 2, Chunk(c0 + 6 + 2 * j, it), Chunk(c0 + 7 + 2 * j, it))
                gate(PAIRS - 1, (PAIRS - 1) % 2)
                round_hid(PAIRS - 1, (PAIRS - 1) % 2)
                d0 = C0[f"dn{f}"]
                with act.Fori(0, 2) as it:
                    for s in range(RING):
                        split_hi(Chunk(d0 + s, it).ahead())
                if f >= 2:
                    act.wait_ge(p_landed, 16 * (f - 1))
                    nc.scalar.activation(pl_x[:, :, 0, :], pl_in[:], ACT.Copy).then_inc(p_hi, 1)
                for s in range(8, PAIRS):
                    split_hi(Chunk(d0 + s).ahead())

            def attention(a, pr, pt, st):
                h0, m0 = HEADS * a, KD * a

                def exponent(h):
                    act.wait_ge(max_made, h0 + h + 1)
                    for t, (lo, hi) in enumerate(((0, P), (P, 384))):
                        last = nc.scalar.activation(pr[h % 3][:, lo:hi], pr[h % 3][:, lo:hi], ACT.Exp, scale=-1.0,
                                                    bias=st[:, 0, 2 * h + t:2 * h + t + 1],
                                                    accum_out=st[:, 1, 2 * h + t:2 * h + t + 1])
                    last.then_inc(exp_made, 1)

                def copy_turned(h):
                    act.wait_ge(prob_turned, h0 + h + 1)
                    if h >= 2:
                        act.wait_ge(mixed, h0 + h - 1)
                    nc.scalar.activation(pt[h % 2][:], ps[:, 2 + h % 2, 0:384], ACT.Copy).then_inc(turned_copied, 1)

                def round_o(m):
                    act.wait_ge(mixed, h0 + 2 * m + 2)
                    nc.scalar.activation(xB[:, m, 0, :], half(4 + m % 4, 0), ACT.Copy).then_inc(o_hi, 1)

                for i in range(HEADS + 4):
                    if i < HEADS:
                        exponent(i)
                    if 2 <= i <= HEADS + 1:
                        copy_turned(i - 2)
                    if i >= 5 and i % 2:
                        round_o((i - 5) // 2)

            split_hi(Chunk(0))
            for b in range(4):
                square(N_GM, b)
            act.wait_ge(vec_landed, 16)
            root_norm(N_GM)
            act.dma_start(wsT[:], wst).then_inc(gm_landed, 16)
            act.dma_start(bsb[:], bass.AP(bsp.tensor, 0, [[0, P], [P, KD], [1, P]])).then_inc(gm_landed, 16)
            round_x(OUT_GM, xA, ahead=range(1, AHEAD))
            for g in range(8):
                split_hi(Chunk(g).ahead())
                act.wait_ge(chunk_used, g + 1)
                if g < 4:
                    dst = vnat[:, :, T * g:T * g + T]
                else:
                    dst = uT[:, 2 * (g - 4):2 * (g - 4) + 2, :]
                nc.scalar.activation(dst, ps[:, g % 4, :].rearrange("p (b t) -> p b t", b=2),
                                     ACT.Gelu_apprx_tanh).then_inc(gm_evac, 1)
                if g == 4:
                    act.wait_ge(gm_sums, 1)
                    inverse_root(gm_rs[:, 0:2], gm_rs[:, 2:4], D, gm_std)
            round_x(OUT_GATED, xB)
            split_and_square("gm_o", N_FF0)
            round_x(OUT_FF0, xA)
            ffn(0)
            square_norm(N_AT)
            round_x(OUT_KV, xB)
            round_x(OUT_Q, xA)
            for g in range(12):
                split_hi(Chunk(C0["at_k"] + g).ahead())
                act.wait_ge(chunk_used, C0["at_k"] + g + 1)
                two = ps[:, g % 4, :].rearrange("p (b t) -> p b t", b=2)
                if g < 4:
                    ins = nc.scalar.activation(at_k[:, 2 * g:2 * g + 2, :], two, ACT.Copy)
                elif g < 8:
                    ins = nc.scalar.activation(at_v[:, :, T * (g - 4):T * (g - 3)], two, ACT.Copy)
                else:
                    ins = nc.scalar.activation(at_qT[:, 2 * (g - 8):2 * (g - 8) + 2, :], two, ACT.Copy, scale=-0.125)
                ins.then_inc(qkv_evac, 1)
            attention(0, at_pr, at_pt, at_st)
            split_and_square("at_o", N_FF1)
            round_x(OUT_FF1, xA)
            ffn(1)
            square_norm(N_FIN1)
            square_norm(N_HY)
            round_x(OUT_HY, xA)
            c0 = C0["hy"]

            def log_parts(u):
                act.wait_ge(z_made, u + 1)
                if u >= 2:
                    act.wait_ge(after_made, u - 1)
                buf, z = sb_l[u % 2][:], ps[:, 4 + 2 * (u % 2):6 + 2 * (u % 2), 0:384]
                own.mark(nc.scalar.activation(buf, z, ACT.Abs))
                own.wait()
                own.mark(nc.scalar.activation(buf, buf, ACT.Exp, scale=-1.0))
                own.wait()
                nc.scalar.activation(buf, buf, ACT.Ln, bias=1.0).then_inc(stick_made, 1)

            def weights(u):
                act.wait_ge(arg_made, u + 1)
                nc.scalar.activation(sb_ls[u % 2][:], sb_ls[u % 2][:], ACT.Exp).then_inc(w_made, 1)

            def round_sb(u):
                act.wait_ge(sb_mixed, u + 1)
                nc.scalar.activation(xB[:, u, 0, :], half(3, u % 2), ACT.Copy).then_inc(sb_hi, 1)

            def decay(dst, i, sign):
                cums = ps[:, 2:6, :].rearrange("p b (t i n) -> p b t i n", t=2, i=2)
                nc.scalar.activation(slot[dst][:].rearrange("p b (t n) -> p b t n", t=2), cums[:, :, :, i, :], ACT.Exp,
                                     scale=sign).then_inc(decay_made, 1)

            act.wait_ge(mu_ready, 1)
            for g in range(14):
                split_hi(Chunk(c0 + g).ahead())
                if g == 2:
                    act.wait_ge(hy_mixed, 1)
                    nc.scalar.activation(wlal[0:64, :], wlal[0:64, :], ACT.Tanh).then_inc(lora_in, 1)
                elif g == 3:
                    act.wait_ge(hy_mixed, 2)
                    nc.scalar.activation(gl[:], gl[:], ACT.Sigmoid).then_inc(lora_in, 1)
                elif g == 4:
                    act.wait_ge(kk_made, 1)
                    nc.scalar.activation(slot[9][:], slot[8][:], ACT.Square).then_inc(kk_sq, 1)
                elif g == 5:
                    for t in range(2):
                        act.wait_ge(w_arg, t + 1)
                        nc.scalar.activation(flat(3)[:, 512 * t:512 * t + 512], flat(3)[:, 512 * t:512 * t + 512],
                                             ACT.Sigmoid).then_inc(w_sig, 1)
                    act.wait_ge(a_proj, 2)
                    for b in range(RBLK):
                        last = nc.scalar.activation(slot[4][:, b, :], half(4 + b // 2, b % 2), ACT.Sigmoid,
                                                    bias=col("rw_a0", b))
                    last.then_inc(a_sig, 1)
                elif g == 6:
                    nc.scalar.preload_act_table_set("natural_log_exp_and_others")
                    act.wait_ge(kk_max, 2)
                    own.mark(nc.scalar.activation(slot[9][:], slot[9][:], ACT.Ln, scale=65536.0))
                    own.wait()
                    nc.scalar.activation(slot[9][:], slot[9][:], ACT.Exp, scale=-0.5, bias=col("ln256")).then_inc(kk_rn, 1)
                elif g == 7:
                    act.wait_ge(cum_made, 1)
                    decay(5, 1, 1.0)
                    decay(6, 0, -1.0)
                elif g == 9:
                    act.wait_ge(factors, 1)
                    decay(5, 0, 1.0)
                act.wait_ge(chunk_used, c0 + g + 1)
                two = ps[:, g % 2, :].rearrange("p (b t) -> p b t", b=2)
                if g < 8:
                    for b in range(2 if g < 7 else 1):
                        last = nc.scalar.activation(mixed_block(2 * g + b), half(g % 2, b), ACT.Copy,
                                                    scale=om_mu[:, 2 * g + b:2 * g + b + 1])
                    last.then_inc(hy_lin, 1)
                elif g < 10:
                    nc.scalar.activation(sb_q[:, 2 * g - 16:2 * g - 14, :], two, ACT.Copy, scale=0.125).then_inc(hy_evac, 1)
                elif g < 12:
                    nc.scalar.activation(sb_k[:, 2 * g - 20:2 * g - 18, :], two, ACT.Copy).then_inc(hy_evac, 1)
                else:
                    nc.scalar.activation(sb_v[:, :, T * (g - 12):T * (g - 11)], two, ACT.Copy).then_inc(hy_evac, 1)

            def copy_product(i, dst):
                for b in range(2):
                    act.wait_ge(mat_done, 2 * i + b + 1)
                    nc.scalar.activation(slot[dst][:, 2 * b:2 * b + 2, :],
                                         ps[:, product_bank(i, b), :].rearrange("p (b t) -> p b t", b=2),
                                         ACT.Copy).then_inc(mat[i], 1)

            log_parts(0)
            log_parts(1)
            act.wait_ge(factors, 5)
            copy_product(0, 3)
            weights(0)
            copy_product(1, 5)
            weights(1)
            log_parts(2)
            round_sb(0)
            copy_product(2, 6)
            log_parts(3)
            round_sb(1)
            weights(2)
            weights(3)
            round_sb(2)
            round_sb(3)
            split_hi(Chunk(C0["hy_o"]).ahead())
            for i, dst in ((9, 4), (11, 10), (12, 1), (13, 2), (15, 10), (17, 2), (19, 10), (20, 7), (21, 1)):
                copy_product(i, dst)
            act.wait_ge(ch_y, 1)
            for b in range(2):
                nc.scalar.activation(slot[12][:, 2 * b:2 * b + 2, :],
                                     ps[:, 4 + b, :].rearrange("p (b t) -> p b t", b=2), ACT.Copy).then_inc(y_made, 1)
            for b in range(2):
                act.wait_ge(yc_made, b + 1)
                nc.scalar.activation(slot[13][:, 2 * b:2 * b + 2, :], slot[12][:, 2 * b:2 * b + 2, :],
                                     ACT.Square).then_inc(y_sq, 1)
            for b in range(2):
                act.wait_ge(y_var, b + 1)
                own.mark(nc.scalar.activation(slot[14][:, 2 * b:2 * b + 2, :],
                                              ps[:, b, :].rearrange("p (b t) -> p b t", b=2), ACT.Ln,
                                              bias=col("gn_eps")))
                own.wait()
                nc.scalar.activation(slot[14][:, 2 * b:2 * b + 2, :], slot[14][:, 2 * b:2 * b + 2, :], ACT.Exp,
                                     scale=-0.5).then_inc(y_rstd, 1)
            for b in range(2):
                act.wait_ge(ro_made, b + 1)
                nc.scalar.activation(xB[:, 4 + 2 * b:6 + 2 * b, 0, :], slot[15][:, 2 * b:2 * b + 2, :],
                                     ACT.Copy).then_inc(ro_hi, 1)
            split_and_square("hy_o", N_FF2, 1)
            round_x(OUT_FF2, xA)
            ffn(2)
            def ple(i):
                n, o = (N_PL0, OUT_PL0) if i == 0 else (N_PL1, OUT_PL1)
                c0 = C0[f"pl_p{i}"]
                square_norm(n)
                round_x(o, xA)
                split_hi(Chunk(c0).ahead())
                for b in range(4):
                    if b < 3:
                        act.wait_ge(e_done, 3 * i + b + 1)
                    else:
                        act.wait_ge(chunk_used, c0 + 1)
                    nc.scalar.activation(pl_sq[:, 2 * b:2 * b + 2, :], ps[:, b, :].rearrange("p (b t) -> p b t", b=2),
                                         ACT.Square).then_inc(e_evac, 1)
                act.wait_ge(e_ss, i + 1)
                inverse_root(pl_rb[:], half(5, 1), D, e_rs)
                for g in range(4):
                    c = Chunk(c0 + 1 + g)
                    split_hi(c.ahead())
                    act.wait_ge(chunk_used, c.count(1))
                    if g >= 2:
                        act.wait_ge(h_updated, 4 * (n if i == 0 else n) + g - 1)
                    nc.scalar.activation(pl_sg[g % 2][:], ps[:, GATE_BANK[g], :].rearrange("p (b t) -> p b t", b=2),
                                         ACT.Sigmoid).then_inc(g_on, 1)
                    for b in ((), (0,), (1, 2), (3,))[g]:
                        square(n + 1, b)
                root_norm(n + 1)

            ple(0)
            round_x(OUT_ML, xA)
            act.wait_ge(cs_arg, 1)
            nc.scalar.activation(ml_cs[:], ml_ang, ACT.Sin).then_inc(cs_made, 1)
            c0 = C0["ml_d"]
            for g in range(3):
                split_hi(Chunk(c0 + g).ahead())
                act.wait_ge(chunk_used, c0 + g + 1)
                n = 2 if g < 2 else 1
                two = ps[:, g, 0:n * T].rearrange("p (b t) -> p b t", b=n)
                nc.scalar.activation(ml_c[:, 2 * g:2 * g + n, :], two, ACT.Copy)
                nc.scalar.activation(xt[:, 2 * g:2 * g + n, :], two, ACT.Square).then_inc(c_evac, 1)
            nc.scalar.preload_act_table_set("natural_log_exp_and_others")
            for j, width in enumerate((384, 256)):
                act.wait_ge(c_ss, j + 1)
                inverse_root(ml_rs[j], half(4 + j, 0), width, c_rs)
            for k in range(5):
                act.wait_ge(c_made, k + 1)
                nc.scalar.activation(xB[:, k, 0, :], xt[:, k, :], ACT.Copy).then_inc(c_hi, 1)
            act.wait_ge(fold_done, 1)
            src = ps[64:128, 6, 0:T].unsqueeze(1).broadcast_to([64, HEADS // 2, T])
            nc.scalar.activation(ml_k[64:128, 0:HEADS // 2, :], src, ACT.Copy).then_inc(kr_spread, 1)
            for g in range(20):
                if g in (0, 2, 5, 8, 12, 16):
                    split_hi(Chunk(C0["ml_q"] + (0, 2, 5, 8, 12, 16).index(g)).ahead())
                wait_up(act, g)
                two = ps[:, g % 4, :].rearrange("p (b t) -> p b t", b=2)
                if g < 8:
                    ins = nc.scalar.activation(ml_q[0:64, 2 * g:2 * g + 2, :], two[0:64], ACT.Copy, scale=-MLA_SCALE)
                elif g < 16:
                    ins = nc.scalar.activation(ml_k[0:64, 2 * (g - 8):2 * (g - 8) + 2, :], two[0:64], ACT.Copy)
                else:
                    t, n = divmod(g - 16, 2)
                    ins = nc.scalar.activation(ml_v[:, t, 512 * n:512 * n + 512], ps[:, g % 4, :], ACT.Copy)
                ins.then_inc(ml_evac, 1)
            attention(1, ml_pr, ml_pt, ml_st)
            split_and_square("ml_o", N_FF3)
            round_x(OUT_FF3, xA)
            ffn(3)
            ple(1)

        @block.vector
        def _(dve):
            own = Own(dve, dve_own)

            def link(ins):
                own.mark(ins)
                own.wait()

            def split_lo(c):
                if c is None:
                    return
                dve.wait_ge(hi_made, c.count(1))
                nc.vector.tensor_tensor(w_lo[c.slot][:], raw[c.slot][:], w_hi[c.slot][:].bitcast(F32),
                                        ALU.subtract).then_inc(lo_made, 1)

            def only_split(name, n):
                for j in range(n):
                    split_lo(Chunk(C0[name] + j).ahead())

            def root(n):
                dve.wait_ge(rs_made, n + 1)

            def refine(y, sums, width, tmp):
                link(nc.vector.tensor_tensor(tmp, y, y, ALU.mult))
                link(nc.vector.scalar_tensor_tensor(out=tmp, in0=sums, scalar=EPS * width, in1=tmp, op0=ALU.add, op1=ALU.mult))
                link(nc.vector.tensor_scalar(tmp, tmp, -0.5 / width, 1.5, ALU.mult, ALU.add))
                link(nc.vector.tensor_tensor(y, y, tmp, ALU.mult))

            def rest_x(o, dst, u):
                lo, hi = UNITS[u]
                dve.wait_ge(x_hi_made, 5 * o + u + 1)
                nc.vector.tensor_tensor(dst[:, lo:hi, 1, :], xt[:, lo:hi, :], dst[:, lo:hi, 0, :].bitcast(F32),
                                        ALU.subtract).then_inc(x_lo_made, 1)

            rest_after = {2: 0, 3: 1, 5: 2, 7: 3}

            def scale_x(o, dst, gain, ahead=()):
                for k in range(KD):
                    nc.vector.scalar_tensor_tensor(out=xt[:, k, :], in0=hT[:, k, :], scalar=col(gain, k), in1=rs[:],
                                                   op0=ALU.mult, op1=ALU.mult).then_inc(xt_made, 1)
                    if k in rest_after:
                        rest_x(o, dst, rest_after[k])
                rest_x(o, dst, 4)
                for c in ahead:
                    split_lo(Chunk(c))

            def add_quarter(b, bank):
                nc.vector.tensor_tensor(hT[:, 2 * b:2 * b + 2, :], hT[:, 2 * b:2 * b + 2, :],
                                        ps[:, bank, :].rearrange("p (b t) -> p b t", b=2),
                                        ALU.add).then_inc(h_updated, 1)

            def add_projection(name, first=0):
                for g in range(4):
                    if g >= first:
                        split_lo(Chunk(C0[name] + g).ahead())
                    dve.wait_ge(chunk_used, C0[name] + g + 1)
                    add_quarter(g, 4 + g)

            def ffn(f):
                c0, base, both = C0[f"up{f}"], PAIRS * f, f < 2
                goff = KF if both else 0
                nblk = 2 * KF if both else KF
                taps = 4 if both else 2
                tap0 = 4 * PAIRS * min(f, 2) + 2 * PAIRS * max(f - 2, 0)

                def convolve(acc, bank, q, off, nth):
                    for b in range(2):
                        j = q * 2 + b
                        nc.vector.scalar_tensor_tensor(out=acc[:, b, 2:T], in0=half(bank, b)[:, 0:T - 2],
                                                       scalar=dcol(f"cw{f}", j, off), in1=acc[:, b, 2:T],
                                                       op0=ALU.mult, op1=ALU.add).then_inc(tap_done, 1)
                    for b in range(2):
                        j = q * 2 + b
                        dve.wait_ge(tap_done, q * taps + (tap0 + nth + b + 1))
                        last = nc.vector.scalar_tensor_tensor(out=acc[:, b, 1:T], in0=half(bank, b)[:, 0:T - 1],
                                                              scalar=dcol(f"cw{f}", j, off + nblk),
                                                              in1=acc[:, b, 1:T], op0=ALU.mult, op1=ALU.add)
                    return last

                def product(q, par):
                    dve.wait_ge(gate_on, q + (base + 1))
                    if both:
                        dve.wait_ge(up_conv, q + (base + 1))
                        up = up_acc[par][:]
                    else:
                        up = ps[:, 2 * par, :].rearrange("p (b t) -> p b t", b=2)
                        if not isinstance(q, int) or q >= 2:
                            dve.wait_ge(hid_lo, q + (base - 1))
                    nc.vector.tensor_tensor(up_acc[par][:], up, gate_acc[par][:], ALU.mult).then_inc(prod_made, 1)

                def rest_hid(q, par):
                    dve.wait_ge(hid_hi, q + (base + 1))
                    nc.vector.tensor_tensor(rows(hid, q * 2, 2, 1), up_acc[par][:], rows(hid, q * 2, 2, 0).bitcast(F32),
                                            ALU.subtract).then_inc(hid_lo, 1)

                def pair(q, par, cu, cg, first=False):
                    split_lo(cu.ahead())
                    if both:
                        dve.wait_ge(up_lin, q + (base + 1))
                        convolve(up_acc[par], 2 * par, q, 0, 0).then_inc(up_conv, 1)
                    if not first:
                        product(q - 1, 1 - par)
                    split_lo(cg.ahead())
                    dve.wait_ge(gate_lin, q + (base + 1))
                    convolve(gate_acc[par], 2 * par + 1, q, goff, taps - 2).then_inc(gate_conv, 1)
                    if not first:
                        rest_hid(q - 1, 1 - par)

                pair(0, 0, Chunk(c0), Chunk(c0 + 1), first=True)
                pair(1, 1, Chunk(c0 + 2), Chunk(c0 + 3))
                pair(2, 0, Chunk(c0 + 4), Chunk(c0 + 5))
                with dve.Fori(0, (PAIRS - 3) // 2) as it:
                    for j in range(2):
                        pair(it * 2 + (3 + j), (3 + j) % 2, Chunk(c0 + 6 + 2 * j, it), Chunk(c0 + 7 + 2 * j, it))
                product(PAIRS - 1, (PAIRS - 1) % 2)
                rest_hid(PAIRS - 1, (PAIRS - 1) % 2)
                d0 = C0[f"dn{f}"]
                with dve.Fori(0, 2) as it:
                    for s in range(RING):
                        split_lo(Chunk(d0 + s, it).ahead())
                if f >= 2:
                    dve.wait_ge(p_hi, f - 1)
                    nc.vector.tensor_tensor(pl_x[:, :, 1, :], pl_in[:], pl_x[:, :, 0, :].bitcast(F32),
                                            ALU.subtract).then_inc(p_lo, 1)
                for s in range(8, PAIRS):
                    split_lo(Chunk(d0 + s).ahead())
                for b in range(4):
                    if b < 3:
                        dve.wait_ge(down_bank, 3 * f + b + 1)
                    else:
                        dve.wait_ge(chunk_used, d0 + PAIRS)
                    add_quarter(b, 4 + b)

            def attention(a, pr, st, bias):
                h0, m0 = HEADS * a, KD * a

                def biased_max(h):
                    dve.wait_ge(scored, h0 + h + 1)
                    if h >= 3:
                        dve.wait_ge(prob_turned, h0 + h - 2)
                    for t, (lo, hi) in enumerate(((0, P), (P, 384))):
                        last = nc.vector.tensor_tensor_reduce(
                            pr[h % 3][:, lo:hi], ps[:, h % 2, lo:hi], bias(h, t), 1.0, 3e38, ALU.add, ALU.min,
                            st[:, 0, 2 * h + t:2 * h + t + 1])
                    last.then_inc(max_made, 1)

                def normalise(h):
                    dve.wait_ge(exp_made, h0 + h + 1)
                    link(nc.vector.reciprocal(st[:, 2, 2 * h:2 * h + 2], st[:, 1, 2 * h:2 * h + 2]))
                    for t, (lo, hi) in enumerate(((0, P), (P, 384))):
                        last = nc.vector.tensor_scalar(pr[h % 3][:, lo:hi], pr[h % 3][:, lo:hi],
                                                       st[:, 2, 2 * h + t:2 * h + t + 1], None, ALU.mult)
                    last.then_inc(prob_made, 1)

                def rest_o(m):
                    dve.wait_ge(o_hi, m0 + m + 1)
                    nc.vector.tensor_tensor(xB[:, m, 1, :], half(4 + m % 4, 0), xB[:, m, 0, :].bitcast(F32),
                                            ALU.subtract).then_inc(o_lo, 1)

                for i in range(HEADS + 5):
                    if i < HEADS:
                        biased_max(i)
                    if 1 <= i <= HEADS:
                        normalise(i - 1)
                    if i >= 6 and i % 2 == 0:
                        rest_o((i - 6) // 2)

            split_lo(Chunk(0))
            dve.wait_ge(vec_landed, 16)
            root(N_GM)
            scale_x(OUT_GM, xA, "a_norm", ahead=range(1, AHEAD))
            for g in range(8):
                split_lo(Chunk(g).ahead())
                if g < 4:
                    dve.wait_ge(gm_evac, g + 1)
                    for t in range(2):
                        own.mark(nc.vector.tensor_tensor_reduce(
                            gm_junk[:], vnat[:, t, T * g:T * g + T], vnat[:, t, T * g:T * g + T], 1.0, 0.0, ALU.mult,
                            ALU.add, gm_sum[:, 4 * t + g:4 * t + g + 1]))
                        own.wait()
                if g == 3:
                    nc.vector.tensor_reduce(gm_rs[:, 2:4], gm_sum[:].rearrange("p (t g) -> p t g", t=2), AX_X,
                                            ALU.add).then_inc(gm_sums, 1)
            dve.wait_ge(gm_std, 1)
            for t in range(2):
                nc.vector.tensor_scalar(vnat[:, t, :], vnat[:, t, :], gm_rs[:, t:t + 1], None,
                                        ALU.mult).then_inc(gm_scaled, 1)
            dve.wait_ge(gm_evac, 8)
            for k in range(KD):
                dve.wait_ge(gm_mixed, k // 2 + 1)
                if k == 0:
                    dve.wait_ge(gm_landed, 32)
                xk = xt[:, k, :].rearrange("p (n i) -> p n i", n=2)
                link(nc.vector.scalar_tensor_tensor(
                    out=xk, in0=half(4 + k // 2, k % 2).rearrange("p (n i) -> p n i", n=2), scalar=col("a_vnorm", k),
                    in1=bsb[:, k:k + 1, :].broadcast_to([P, 2, P]), op0=ALU.mult, op1=ALU.add))
                nc.vector.tensor_tensor(xt[:, k, :], xt[:, k, :], uT[:, k, :], ALU.mult).then_inc(xt_made, 1)
                if k in rest_after:
                    rest_x(OUT_GATED, xB, rest_after[k])
            rest_x(OUT_GATED, xB, 4)
            add_projection("gm_o")
            root(N_FF0)
            scale_x(OUT_FF0, xA, "f_norm0")
            ffn(0)
            root(N_AT)
            refine(rs[:], half(4, 0), D, at_pr[0][:, 0:T])
            scale_x(OUT_KV, xB, "kv_norm")
            dve.wait_ge(x_lo_made, 5 * OUT_Q)
            scale_x(OUT_Q, xA, "b_norm")
            for g in range(12):
                split_lo(Chunk(C0["at_k"] + g).ahead())
            dve.wait_ge(bias_ready, 1)
            attention(0, at_pr, at_st, lambda h, t: at_bias[:, h, P:T] if t == 0 else at_bias[:, h, :])
            add_projection("at_o")
            root(N_FF1)
            scale_x(OUT_FF1, xA, "f_norm1")
            ffn(1)
            root(N_FIN1)
            for k in range(KD):
                ins = nc.vector.scalar_tensor_tensor(out=hT[:, k, :], in0=hT[:, k, :], scalar=col("fin1", k), in1=rs[:],
                                                     op0=ALU.mult, op1=ALU.mult)
                if k % 2:
                    ins.then_inc(h_updated, 1)
            nc.vector.tensor_scalar(om_mu[:], col("rw_mu", 0, 15), -1.0, 1.0, ALU.mult, ALU.add).then_inc(mu_ready, 1)
            root(N_HY)
            dve.wait_ge(h_updated, 20)
            scale_x(OUT_HY, xA, "at_norm0")
            c0 = C0["hy"]

            def diagonal(tile):
                return tile[:].rearrange("p h (b q) -> p h b q", b=3)[:, :, 0:3:2, :]

            tri = h_tri.unsqueeze(1).unsqueeze(1).broadcast_to([P, 2, 2, P])

            def logs(u):
                dve.wait_ge(stick_made, u + 1)
                z = ps[:, 4 + 2 * (u % 2):6 + 2 * (u % 2), 0:384]
                if u >= 2:
                    dve.wait_ge(sb_mixed, u - 1)
                link(nc.vector.scalar_tensor_tensor(out=sb_ls[u % 2][:], in0=z, scalar=0.0, in1=sb_l[u % 2][:],
                                                    op0=ALU.min, op1=ALU.subtract))
                link(nc.vector.tensor_tensor(sb_l[u % 2][:], sb_ls[u % 2][:], z, ALU.subtract))
                nc.vector.tensor_tensor(diagonal(sb_l[u % 2]), diagonal(sb_l[u % 2]), tri, ALU.mult).then_inc(log_made, 1)

            def arguments(u):
                dve.wait_ge(after_made, u + 1)
                nc.vector.tensor_tensor(sb_ls[u % 2][:], sb_ls[u % 2][:],
                                        ps[:, 4 + 2 * (u % 2):6 + 2 * (u % 2), 0:384], ALU.add).then_inc(arg_made, 1)
                dve.wait_ge(w_made, u + 1)
                nc.vector.tensor_tensor(diagonal(sb_ls[u % 2]), diagonal(sb_ls[u % 2]), tri, ALU.mult).then_inc(w_masked, 1)

            def rest_sb(u):
                dve.wait_ge(sb_hi, u + 1)
                nc.vector.tensor_tensor(xB[:, u, 1, :], half(3, u % 2), xB[:, u, 0, :].bitcast(F32),
                                        ALU.subtract).then_inc(sb_lo, 1)

            dve.wait_ge(hy_landed, 32)
            for g in range(14):
                split_lo(Chunk(c0 + g).ahead())
                if g == 4:
                    dve.wait_ge(hy_mixed, 4)
                    for b in range(RBLK):
                        last = nc.vector.tensor_scalar(slot[8][:, b, :], slot[1][:, b, :], col("rw_kk", b), None, ALU.mult)
                    last.then_inc(kk_made, 1)
                elif g == 5:
                    for t in range(2):
                        dve.wait_ge(w_proj, t + 1)
                        nc.vector.tensor_tensor(flat(3)[:, 512 * t:512 * t + 512], ps[:, 2 + t, :], w0b[:],
                                                ALU.add).then_inc(w_arg, 1)
                    for b in range(2):
                        dve.wait_ge(kk_ss, b + 1)
                        nc.vector.tensor_scalar(slot[9][:, 2 * b:2 * b + 2, :],
                                                ps[:, 6 + b, :].rearrange("p (b t) -> p b t", b=2), 1e-24, None,
                                                ALU.max).then_inc(kk_max, 1)
                elif g == 7:
                    dve.wait_ge(kk_rn, 1)
                    link(nc.vector.tensor_tensor(slot[8][:], slot[8][:], slot[9][:], ALU.mult))
                    dve.wait_ge(a_sig, 1)
                    for b in range(RBLK):
                        own.mark(nc.vector.tensor_scalar(slot[9][:, b, :], slot[4][:, b, :], -1.0, col("rw_ka", b),
                                                         ALU.add, ALU.mult))
                    own.wait()
                    link(nc.vector.scalar_tensor_tensor(out=slot[1][:], in0=slot[9][:], scalar=1.0, in1=slot[1][:],
                                                        op0=ALU.add, op1=ALU.mult))
                    for b in range(RBLK):
                        last = nc.vector.scalar_tensor_tensor(out=slot[9][:, b, :], in0=slot[0][:, b, :],
                                                              scalar=col("rw_rk", b), in1=slot[1][:, b, :], op0=ALU.mult,
                                                              op1=ALU.mult)
                        if b % 2:
                            last.then_inc(rk_made, 1)
                elif g == 8:
                    link(nc.vector.tensor_tensor(slot[4][:], slot[4][:], slot[8][:], ALU.mult))
                    dve.wait_ge(decay_made, 2)
                    for dst, by in ((8, 5), (4, 6), (1, 6)):
                        nc.vector.tensor_tensor(slot[dst][:], slot[dst][:], slot[by][:], ALU.mult).then_inc(factors, 1)
                elif g == 10:
                    dve.wait_ge(decay_made, 3)
                    nc.vector.tensor_tensor(slot[0][:], slot[0][:], slot[5][:], ALU.mult).then_inc(factors, 1)
                    nc.vector.tensor_copy(pend[:], slot[5][:].rearrange("p b (c t) -> p b c t", c=NRCH)[:, :, :, RCH - 1]).then_inc(factors, 1)
                    for b in range(2):
                        dve.wait_ge(rk_sum, b + 1)
                        nc.vector.tensor_tensor(slot[9][:, 2 * b:2 * b + 2, :],
                                                ps[:, 6 + b, :].rearrange("p (b t) -> p b t", b=2),
                                                slot[2][:, 2 * b:2 * b + 2, :], ALU.mult).then_inc(bonus_made, 1)
                if g < 8:
                    dve.wait_ge(hy_lin, g + 1)
                    for b in range(2 if g < 7 else 1):
                        dst = mixed_block(2 * g + b)
                        last = nc.vector.scalar_tensor_tensor(out=dst[:, 1:T], in0=half(g % 2, b)[:, 0:T - 1],
                                                              scalar=col("rw_mu", 2 * g + b), in1=dst[:, 1:T],
                                                              op0=ALU.mult, op1=ALU.add)
                    last.then_inc(hy_mixed, 1)
            logs(0)
            logs(1)
            arguments(0)
            arguments(1)
            logs(2)
            rest_sb(0)
            logs(3)
            rest_sb(1)
            arguments(2)
            arguments(3)
            rest_sb(2)
            rest_sb(3)
            split_lo(Chunk(C0["hy_o"]).ahead())

            def halves(i, b):
                return ps[:, 2 * (i % 4) + b, :].rearrange("p (m s) -> p m s", s=64)

            def part(d, b):
                return slot[d][:, 2 * b:2 * b + 2, :].rearrange("p b (c s) -> p (b c) s", s=64)

            def wide(mask):
                return mask.unsqueeze(1).broadcast_to([P, 8, 64])

            eye64 = hcon[:, HCON - 64:HCON]

            def masked(i, dsts):
                for b in range(2):
                    dve.wait_ge(mat_done, 2 * i + b + 1)
                    for dst, mask in dsts:
                        nc.vector.tensor_tensor(part(dst, b), halves(i, b), wide(mask), ALU.mult).then_inc(mat[i], 1)

            def with_eye(i, dsts):
                for b in range(2):
                    dve.wait_ge(mat_done, 2 * i + b + 1)
                    for dst, how in dsts:
                        if how == 0:
                            ins = nc.vector.tensor_copy(part(dst, b), halves(i, b))
                        else:
                            ins = nc.vector.scalar_tensor_tensor(out=part(dst, b), in0=halves(i, b), scalar=float(how),
                                                                 in1=wide(eye64), op0=ALU.mult, op1=ALU.add)
                        ins.then_inc(mat[i], 1)

            masked(3, ((7, m_d),))
            masked(4, ((10, m_dt), (11, m_ot)))
            masked(5, ((12, m_strict),))
            masked(6, ((13, m_incl),))
            masked(7, ((14, m_incl),))
            dve.wait_ge(mat[4], 4)
            for b in range(2):
                nc.vector.scalar_tensor_tensor(out=part(15, b), in0=part(10, b), scalar=-1.0, in1=wide(eye64),
                                               op0=ALU.mult, op1=ALU.add).then_inc(imdt_made, 1)
            with_eye(8, ((1, 0), (2, 1)))
            with_eye(10, ((7, 1),))
            with_eye(14, ((4, 0), (7, -1)))
            with_eye(16, ((11, 0), (15, 1)))
            with_eye(18, ((4, 1),))
            states = [flat(10)[:, 256 * i:256 * i + 256].rearrange("p (b i) -> p b i", b=RBLK) for i in range(3)]
            small = lambda bank: ps[:, bank, 0:256].rearrange("p (b i) -> p b i", b=RBLK)
            uall = slot[11][:].rearrange("p c (b i) -> p c b i", b=RBLK)
            for c in range(NRCH):
                dve.wait_ge(ch_x, c + 1)
                if c == 0:
                    dve.wait_ge(mat[20], 2)
                nc.vector.tensor_copy(states[2], small(0)).then_inc(ch_xs, 1)
                dve.wait_ge(ch_u, c + 1)
                nc.vector.tensor_scalar(uall[:, c], small(1), -1.0, None, ALU.mult).then_inc(ch_us, 1)
                if c == NRCH - 1:
                    break
                dve.wait_ge(ch_s, c + 1)
                fade = pend[:, :, c:c + 1].broadcast_to([P, RBLK, 64])
                if c == 0:
                    nc.vector.tensor_tensor(states[0], small(2), fade, ALU.mult).then_inc(ch_st, 1)
                else:
                    link(nc.vector.tensor_tensor(states[c % 2], states[(c - 1) % 2], small(2), ALU.add))
                    nc.vector.tensor_tensor(states[c % 2], states[c % 2], fade, ALU.mult).then_inc(ch_st, 1)
            for b in range(2):
                dve.wait_ge(y_mean, b + 1)
                y = slot[12][:, 2 * b:2 * b + 2, :]
                nc.vector.tensor_tensor(y, y, ps[:, b, :].rearrange("p (b t) -> p b t", b=2), ALU.subtract).then_inc(yc_made, 1)
            for b in range(2):
                dve.wait_ge(y_rstd, b + 1)
                for k in (2 * b, 2 * b + 1):
                    own.mark(nc.vector.scalar_tensor_tensor(out=slot[15][:, k, :], in0=slot[12][:, k, :],
                                                            scalar=col("rw_lnw", k), in1=slot[14][:, k, :], op0=ALU.mult,
                                                            op1=ALU.mult))
                own.wait()
                for k in (2 * b, 2 * b + 1):
                    own.mark(nc.vector.scalar_tensor_tensor(out=slot[15][:, k, :], in0=slot[15][:, k, :],
                                                            scalar=col("rw_lnb", k), in1=slot[9][:, k, :], op0=ALU.add,
                                                            op1=ALU.add))
                own.wait()
                dve.wait_ge(g_proj, b + 1)
                nc.vector.tensor_tensor(slot[15][:, 2 * b:2 * b + 2, :], slot[15][:, 2 * b:2 * b + 2, :],
                                        ps[:, 2 + b, :].rearrange("p (b t) -> p b t", b=2), ALU.mult).then_inc(ro_made, 1)
            for b in range(2):
                dve.wait_ge(ro_hi, b + 1)
                nc.vector.tensor_tensor(xB[:, 4 + 2 * b:6 + 2 * b, 1, :], slot[15][:, 2 * b:2 * b + 2, :],
                                        xB[:, 4 + 2 * b:6 + 2 * b, 0, :].bitcast(F32), ALU.subtract).then_inc(ro_lo, 1)
            add_projection("hy_o", 1)
            root(N_FF2)
            scale_x(OUT_FF2, xA, "ff_norm0")
            ffn(2)

            def ple(i):
                n, o = (N_PL0, OUT_PL0) if i == 0 else (N_PL1, OUT_PL1)
                c0 = C0[f"pl_p{i}"]
                root(n)
                scale_x(o, xA, f"pl_gnorm{i}")
                split_lo(Chunk(c0).ahead())
                dve.wait_ge(e_rs, i + 1)
                for k in range(KD):
                    own.mark(nc.vector.scalar_tensor_tensor(out=pl_e[:, k, :], in0=half(k // 2, k % 2),
                                                            scalar=col(f"pl_norm{i}", k), in1=pl_rb[:], op0=ALU.mult,
                                                            op1=ALU.mult))
                own.wait()
                for g in range(4):
                    c = Chunk(c0 + 1 + g)
                    split_lo(c.ahead())
                    dve.wait_ge(g_on, 4 * i + g + 1)
                    link(nc.vector.tensor_tensor(pl_sg[g % 2][:], pl_sg[g % 2][:], pl_e[:, 2 * g:2 * g + 2, :], ALU.mult))
                    nc.vector.tensor_tensor(hT[:, 2 * g:2 * g + 2, :], hT[:, 2 * g:2 * g + 2, :], pl_sg[g % 2][:],
                                            ALU.add).then_inc(h_updated, 1)

            ple(0)
            root(N_ML)
            scale_x(OUT_ML, xA, "at_norm1")
            dve.wait_ge(ml_landed, 32)
            two_pi = 2 * np.pi
            c1 = 6.28125
            c2 = float(np.float32(np.round((two_pi - c1) * 2 ** 20) / 2 ** 20))
            c3 = float(np.float32(two_pi - c1 - c2))
            magic = 1.5 * 2.0 ** 23
            link(nc.vector.tensor_copy(ml_ang, ml_pos[:]))
            link(nc.vector.tensor_scalar(ml_ang, ml_ang, col("freq"), None, ALU.mult))
            link(nc.vector.tensor_scalar(ml_n, ml_ang, 1.0 / two_pi, col("turn"), ALU.mult, ALU.add))
            link(nc.vector.tensor_scalar(ml_n, ml_n, magic, None, ALU.add))
            link(nc.vector.tensor_scalar(ml_n, ml_n, magic, None, ALU.subtract))
            for c in (c1, c2, c3):
                link(nc.vector.scalar_tensor_tensor(out=ml_ang, in0=ml_n, scalar=-c, in1=ml_ang, op0=ALU.mult, op1=ALU.add))
            link(nc.vector.tensor_scalar(ml_ang, ml_ang, col("phase"), None, ALU.add))
            lim = 3.1415925
            nc.vector.tensor_scalar(ml_ang, ml_ang, lim, -lim, ALU.min, ALU.max).then_inc(cs_arg, 1)
            for g in range(3):
                split_lo(Chunk(C0["ml_d"] + g).ahead())
            dve.wait_ge(c_evac, 3)
            dve.wait_ge(cs_made, 1)
            nc.vector.tensor_tensor(ml_kr[64:128, :], half(2, 1)[64:128], ml_cs[64:128, :], ALU.mult).then_inc(kr_made, 1)
            for j in range(2):
                dve.wait_ge(c_rs, j + 1)
                refine(ml_rs[j], half(4 + j, 0), (384, 256)[j], ml_pr[2][:, 0:T])
                for k in ((0, 1, 2), (3, 4))[j]:
                    gain = col("q_norm", k) if j == 0 else col("c_norm", k - 3)
                    nc.vector.scalar_tensor_tensor(out=xt[:, k, :], in0=ml_c[:, k, :], scalar=gain, in1=ml_rs[j],
                                                   op0=ALU.mult, op1=ALU.mult).then_inc(c_made, 1)
                for k in ((0, 1, 2), (3, 4))[j]:
                    dve.wait_ge(c_hi, k + 1)
                    nc.vector.tensor_tensor(xB[:, k, 1, :], xt[:, k, :], xB[:, k, 0, :].bitcast(F32),
                                            ALU.subtract).then_inc(c_lo, 1)
            dve.wait_ge(fold_done, 2)
            src = ps[64:128, 7, 0:T].unsqueeze(1).broadcast_to([64, HEADS // 2, T])
            nc.vector.tensor_copy(ml_k[64:128, HEADS // 2:HEADS, :], src).then_inc(kr_spread, 1)
            for g in range(20):
                if g in (0, 2, 5, 8, 12, 16):
                    split_lo(Chunk(C0["ml_q"] + (0, 2, 5, 8, 12, 16).index(g)).ahead())
                if g < 8:
                    wait_up(dve, g)
                    nc.vector.scalar_tensor_tensor(
                        out=ml_q[64:128, 2 * g:2 * g + 2, :], in0=ps[64:128, g % 4, :].rearrange("p (b t) -> p b t", b=2),
                        scalar=-MLA_SCALE, in1=ml_cs[64:128, :].unsqueeze(1).broadcast_to([64, 2, T]), op0=ALU.mult,
                        op1=ALU.mult).then_inc(ml_rope, 1)
            attention(1, ml_pr, ml_st, lambda h, t: ml_bias[:, P:T] if t == 0 else ml_bias[:, 0:T])
            add_projection("ml_o")
            root(N_FF3)
            scale_x(OUT_FF3, xA, "ff_norm1")
            ffn(3)
            ple(1)
            root(N_FIN2)
            for k in range(KD):
                nc.vector.scalar_tensor_tensor(out=xt[:, k, :], in0=hT[:, k, :], scalar=col("fin2", k), in1=rs[:],
                                               op0=ALU.mult, op1=ALU.mult).then_inc(xt_made, 1)

        @block.tensor
        def _(pe):
            def three(out, wh, wl, xh, xl, start, stop):
                nc.tensor.matmul(out, wh, xh, start=start, stop=False, skip_group_check=True)
                nc.tensor.matmul(out, wh, xl, start=False, stop=False, skip_group_check=True)
                return nc.tensor.matmul(out, wl, xh, start=False, stop=stop, skip_group_check=True)

            def three_natural(out, xh, xl, wh, wl, start, stop):
                nc.tensor.matmul(out, xh, wh, start=start, stop=False, skip_group_check=True)
                nc.tensor.matmul(out, xh, wl, start=False, stop=False, skip_group_check=True)
                return nc.tensor.matmul(out, xl, wh, start=False, stop=stop, skip_group_check=True)

            def plain(out, lhsT, rhs, start=True, stop=True):
                return nc.tensor.matmul(out, lhsT, rhs, start=start, stop=stop, skip_group_check=True)

            def weight(c, i, n=1):
                return w_hi[c.slot][:, P * i:P * (i + n)], w_lo[c.slot][:, P * i:P * (i + n)]

            def keep_clock(n):
                for _ in range(n):
                    plain(ps[:, 6, 0:P], ones, ones)

            def sum_quarters(n, quarters, idle=True):
                for b in quarters:
                    if b == 1:
                        continue
                    if b == 0:
                        pe.wait_ge(sq_added, n + 1)
                    else:
                        if b == 3 and idle:
                            keep_clock(FILL[0])
                        pe.wait_ge(sq_made, 4 * n + b + 1)
                    for k in (2 * b, 2 * b + 1):
                        last = plain(half(4, 0), ones, xt[:, k, :], k == 0, k == KD - 1)
                if b == 3:
                    last.then_inc(ss_summed, 1)
                    if idle:
                        keep_clock(FILL[1])

            def wide_chunk(c, bank, x, ready=None, between={}, blocks=2):
                pe.wait_ge(lo_made, c.count(1))
                for k in range(KD):
                    if k in between:
                        between[k]()
                    if ready is not None:
                        ready(k, x_hi_made)
                        for part in range(2):
                            for b in range(blocks):
                                plain(half(bank, b), weight(c, 2 * k + b)[part], x[:, k, 0, :],
                                      k == 0 and b == 0 and part == 0, False)
                        ready(k, x_lo_made)
                        for b in range(blocks):
                            last = plain(half(bank, b), weight(c, 2 * k + b)[0], x[:, k, 1, :], False, k == KD - 1)
                        continue
                    for b in range(blocks):
                        last = three(half(bank, b), *weight(c, 2 * k + b), x[:, k, 0, :], x[:, k, 1, :],
                                     k == 0 and b == 0, k == KD - 1)
                last.then_inc(chunk_used, 1)

            def natural_chunk(c, bank, x, ready=None):
                pe.wait_ge(lo_made, c.count(1))
                for k in range(KD):
                    if ready is not None:
                        ready(k, x_lo_made)
                    for t in range(2):
                        last = three_natural(half(bank, t), x[:, k, 0, P * t:P * t + P], x[:, k, 1, P * t:P * t + P],
                                             *weight(c, 2 * k, 2), k == 0 and t == 0, k == KD - 1)
                last.then_inc(chunk_used, 1)

            def x_ready(o):
                def ready(k, made):
                    for u, (lo, _) in enumerate(UNITS):
                        if lo == k:
                            pe.wait_ge(made, 5 * o + u + 1)
                return ready

            def ffn(f, n, o):
                c0, base, both = C0[f"up{f}"], PAIRS * f, f < 2
                up_used = up_conv if both else prod_made

                def pair(q, par, cu, cg, ready=None, first=False):
                    if not first:
                        pe.wait_ge(up_used, q + (base - 1))
                    wide_chunk(cu, 2 * par, xA, ready)
                    if not first:
                        pe.wait_ge(gate_conv, q + (base - 1))
                    wide_chunk(cg, 2 * par + 1, xA)

                def down(d, c, start=False, stop=False):
                    pe.wait_ge(lo_made, c.count(1))
                    pe.wait_ge(hid_lo, d + (base + 1))
                    for b in range(KD):
                        for k in range(2):
                            if isinstance(d, int):
                                xh, xl = hid[:, 2 * d + k, 0, :], hid[:, 2 * d + k, 1, :]
                            else:
                                xh, xl = [rows(hid, d * 2 + k, 1, i).rearrange("p a t -> p (a t)") for i in range(2)]
                            last = three(half(4 + b // 2, b % 2), *weight(c, KD * k + b), xh, xl,
                                         start and k == 0 and b % 2 == 0, stop and k == 1)
                        if stop and b % 2 and b < KD - 1:
                            last.then_inc(down_bank, 1)
                    last.then_inc(chunk_used, 1)

                sum_quarters(n, (3,))
                pair(0, 0, Chunk(c0), Chunk(c0 + 1), x_ready(o), True)
                pair(1, 1, Chunk(c0 + 2), Chunk(c0 + 3), None, True)
                pair(2, 0, Chunk(c0 + 4), Chunk(c0 + 5))
                with pe.Fori(0, (PAIRS - 3) // 2) as it:
                    for j in range(2):
                        pair(it * 2 + (3 + j), (3 + j) % 2, Chunk(c0 + 6 + 2 * j, it), Chunk(c0 + 7 + 2 * j, it))
                d0 = C0[f"dn{f}"]
                down(0, Chunk(d0), start=True)
                with pe.Fori(0, 2) as it:
                    for s in range(RING):
                        down(it * RING + (1 + s), Chunk(d0 + 1 + s, it))
                down(9, Chunk(d0 + 9))
                down(10, Chunk(d0 + 10), stop=True)

            def attention(a, q, k, v, pr, pt):
                h0, m0 = HEADS * a, KD * a

                def scores(h):
                    if h >= 2:
                        pe.wait_ge(max_made, h0 + h - 1)
                    plain(ps[:, h % 2, 0:P], q(h)[:, 0:P], k(h)[:, 0:P])
                    plain(ps[:, h % 2, P:384], q(h)[:, P:T], k(h)).then_inc(scored, 1)

                def turn(h):
                    pe.wait_ge(prob_made, h0 + h + 1)
                    if h >= 2:
                        pe.wait_ge(turned_copied, h0 + h - 1)
                    for i in range(3):
                        last = nc.tensor.transpose(ps[:, 2 + h % 2, P * i:P * i + P], pr[h % 3][:, P * i:P * i + P], eye)
                    last.then_inc(prob_turned, 1)

                def mix(h):
                    pe.wait_ge(turned_copied, h0 + h + 1)
                    m, r = h // 2, 64 * (h % 2)
                    if m >= 4 and h % 2 == 0:
                        pe.wait_ge(o_lo, m0 + m - 3)
                    out = half(4 + m % 4, 0)[r:r + 64]
                    plain(out, v[:, 0, 64 * h:64 * h + 64], pt[h % 2][:, 0:T], stop=False)
                    plain(out[:, P:T], v[:, 1, 64 * h:64 * h + 64], pt[h % 2][:, T:384], start=False).then_inc(mixed, 1)

                for i in range(HEADS + 3):
                    if i < HEADS:
                        scores(i)
                    if 2 <= i <= HEADS + 1:
                        turn(i - 2)
                    if i >= 3:
                        mix(i - 3)

            def project(name, x, ready, n):
                for g in range(4):
                    early = {7: lambda: sum_quarters(n, (0, 1, 2))} if g == 3 else {}
                    wide_chunk(Chunk(C0[name] + g), 4 + g, x, ready if g == 0 else None, early)

            pe.wait_ge(eye_landed, 16)
            keep_clock(16)
            sum_quarters(N_GM, range(4))
            for g in range(4):
                natural_chunk(Chunk(g), g, xA, x_ready(OUT_GM) if g == 0 else None)
            for g in range(4, 8):
                pe.wait_ge(gm_evac, g - 3)
                wide_chunk(Chunk(g), g % 4, xA)
            pe.wait_ge(gm_masked, 1)
            pe.wait_ge(gm_scaled, 2)
            for k in range(KD):
                for t in range(2):
                    last = plain(half(4 + k // 2, k % 2)[:, P * t:P * t + P], vnat[:, t, P * k:P * k + P], wsT[:, k, :])
                if k % 2:
                    last.then_inc(gm_mixed, 1)
            pe.wait_ge(xt_made, 8 * OUT_GATED + 2)
            project("gm_o", xB, x_ready(OUT_GATED), N_FF0)
            ffn(0, N_FF0, OUT_FF0)
            sum_quarters(N_AT, range(4))
            for g in range(12):
                if g >= 4:
                    pe.wait_ge(qkv_evac, g - 3)
                x, o = (xB, OUT_KV) if g < 8 else (xA, OUT_Q)
                (natural_chunk if 4 <= g < 8 else wide_chunk)(Chunk(C0["at_k"] + g), g % 4, x,
                                                              x_ready(o) if g in (0, 8) else None)
            pe.wait_ge(qkv_evac, 12)
            attention(0, lambda h: at_qT[64 * (h % 2):64 * (h % 2) + 64, h // 2, :],
                      lambda h: at_k[64 * (h % 2):64 * (h % 2) + 64, h // 2, :], at_v, at_pr, at_pt)
            pe.wait_ge(o_lo, 8)
            project("at_o", xB, None, N_FF1)
            ffn(1, N_FF1, OUT_FF1)
            sum_quarters(N_FIN1, range(4))
            sum_quarters(N_HY, range(4))

            def stick_scores(u):
                if u >= 2:
                    pe.wait_ge(arg_made, u - 1)
                for i in range(2):
                    bank = 4 + 2 * (u % 2) + i
                    r = slice(64 * i, 64 * i + 64)
                    plain(ps[:, bank, 0:T], sb_k[r, u, 0:P], sb_q[r, u, :])
                    last = plain(ps[:, bank, T:384], sb_k[r, u, P:T], sb_q[r, u, P:T])
                last.then_inc(z_made, 1)

            def stick_after(u):
                pe.wait_ge(log_made, u + 1)
                for i in range(2):
                    bank = 4 + 2 * (u % 2) + i
                    plain(ps[:, bank, 0:384], h_after, sb_l[u % 2][:, i, :], stop=False)
                    last = plain(ps[:, bank, P:T], ones, sb_l[u % 2][:, i, T:384], start=False)
                last.then_inc(after_made, 1)

            def stick_mix(u):
                pe.wait_ge(w_masked, u + 1)
                if u >= 1:
                    pe.wait_ge(sb_lo, u)
                for i in range(2):
                    h, out = 2 * u + i, half(3, u % 2)[64 * i:64 * i + 64]
                    plain(out, sb_v[:, 0, 64 * h:64 * h + 64], sb_ls[u % 2][:, i, 0:T], stop=False)
                    last = plain(out[:, P:T], sb_v[:, 1, 64 * h:64 * h + 64], sb_ls[u % 2][:, i, T:384], start=False)
                last.then_inc(sb_mixed, 1)

            c0 = C0["hy"]
            def head_sums(bank, src, mat_, signal, ready):
                for b in range(RBLK):
                    ready(b)
                    last = plain(half(bank + b // 2, b % 2), mat_, slot[src][:, b, :])
                    if b % 2:
                        last.then_inc(signal, 1)

            for g in range(14):
                if 2 <= g < 10:
                    pe.wait_ge(hy_mixed, g - 1)
                elif g >= 10:
                    pe.wait_ge(hy_evac, g - 9)
                if g >= 12:
                    natural_chunk(Chunk(c0 + g), g % 2, xA)
                else:
                    wide_chunk(Chunk(c0 + g), g % 2, xA, x_ready(OUT_HY) if g == 0 else None, blocks=1 if g == 7 else 2)
                if g == 4:
                    pe.wait_ge(lora_landed, 16)
                    pe.wait_ge(lora_in, 1)
                    for t in range(2):
                        plain(ps[:, 2 + t, :], wlal[:, P * t:P * t + P], lora_w[:, 0, :]).then_inc(w_proj, 1)
                    for b in range(RBLK):
                        last = plain(half(4 + b // 2, b % 2), lora_w[:, 1, P * b:P * b + P], wlal[:])
                        if b % 2:
                            last.then_inc(a_proj, 1)
                    pe.wait_ge(kk_sq, 1)
                    pe.wait_ge(hy_landed, 32)
                    head_sums(6, 9, h_sum, kk_ss, lambda b: None)
                elif g == 5:
                    pe.wait_ge(w_sig, 2)
                    pe.wait_ge(a_sig, 1)
                    for t in range(2):
                        for b in range(RBLK):
                            last = plain(half(2 + b, t), flat(3)[:, 512 * t + P * b:512 * t + P * b + P], h_cum)
                    last.then_inc(cum_made, 1)
                elif g == 8:
                    pe.wait_ge(kk_max, 2)
                    head_sums(6, 9, h_sum, rk_sum, lambda b: pe.wait_ge(rk_made, b // 2 + 1) if b % 2 == 0 else None)

            def tile(d, hf, p, c):
                return slot[d][64 * hf:64 * hf + 64, p, RCH * c:RCH * c + RCH]

            def product(i, lhs, rhs, needs, used=None):
                for b in range(2):
                    for j, n in needs:
                        pe.wait_ge(mat[j], n * (b + 1))
                    if i >= 7:
                        pe.wait_ge(mat[i - 4], EVACS.get(i - 4, 1) * (b + 1))
                    elif i < 3 and 2 * i + b >= 3:
                        j, h = divmod(2 * i + b - 3, 2)
                        pe.wait_ge(mat[j], h + 1)
                    for p in (2 * b, 2 * b + 1):
                        for c in range(NRCH):
                            at = ((p % 2) * NRCH + c) * RCH
                            for hf in range(2):
                                out = ps[64 * hf:64 * hf + 64, product_bank(i, b), at:at + RCH]
                                right = eye[64 * hf:64 * hf + 64, 64 * hf:64 * hf + 64] if rhs is None else tile(rhs, hf, p, c)
                                last = plain(out, tile(lhs, hf, p, c), right)
                    last.then_inc(mat_done, 1)

            pe.wait_ge(decay_made, 3)
            pe.wait_ge(bonus_made, 2)
            stick_scores(0)
            stick_scores(1)
            pe.wait_ge(factors, 5)
            pe.wait_ge(hy_evac, 6)
            product(0, 4, None, ())
            stick_after(0)
            product(1, 1, None, ())
            stick_after(1)
            stick_scores(2)
            stick_mix(0)
            product(2, 2, None, ())
            stick_scores(3)
            stick_mix(1)
            stick_after(2)
            stick_after(3)
            stick_mix(2)
            stick_mix(3)
            pe.wait_ge(sb_lo, 4)
            pe.wait_ge(mat[1], 2)
            pe.wait_ge(mat[2], 2)
            product(3, 8, 4, ())
            product(4, 4, 8, ())
            product(5, 1, 8, ())
            product(6, 4, 0, ())
            product(7, 1, 0, ())
            product(8, 10, 7, ((3, 1), (4, 2)))
            product(9, 7, 10, ((3, 1), (4, 2)))
            product(10, 4, 1, ((8, 2), (9, 1)))
            pe.wait_ge(imdt_made, 2)
            product(11, 2, 15, ((8, 2),))
            product(12, 7, 10, ((10, 1), (11, 1)))
            product(13, 1, None, ((12, 1),))
            product(14, 11, 2, ((13, 1),))
            product(15, 2, 11, ((13, 1),))
            product(16, 10, 4, ((14, 2), (15, 1)))
            product(17, 4, 10, ((14, 2), (15, 1)))
            product(18, 2, 11, ((16, 2), (17, 1)))
            product(19, 7, 1, ((14, 2), (12, 1)))
            product(20, 15, 10, ((16, 2), (19, 1)))
            product(21, 4, 7, ((18, 1), (20, 1)))
            for i in range(18, 22):
                pe.wait_ge(mat[i], 2)
            pe.wait_ge(mat[2], 2)

            def each():
                for p in range(RBLK):
                    for hf in range(2):
                        yield p, slice(64 * hf, 64 * hf + 64), hf

            def state(i, p, s):
                return flat(10)[s, 256 * i + 64 * p:256 * i + 64 * p + 64]

            co = [Chunk(C0["hy_o"] + g) for g in range(4)]

            def out_rows(g, k):
                for b in range(2):
                    last = three(half(4 + g, b), *weight(co[g], 2 * k + b), xB[:, k, 0, :], xB[:, k, 1, :],
                                 k == 0 and b == 0, k == KD - 1)
                return last

            pe.wait_ge(lo_made, co[3].count(1))
            fill = [(g, k) for g in (2, 3) for k in range(4)]
            for c in range(NRCH):
                if c:
                    pe.wait_ge(ch_st, c)
                for p, s, hf in each():
                    last = plain(ps[s, 0, 64 * p:64 * p + 64], tile(12, hf, p, c), tile(6, hf, p, c), stop=c == 0)
                    if c:
                        last = plain(ps[s, 0, 64 * p:64 * p + 64], tile(8, hf, p, c), state((c - 1) % 2, p, s), start=False)
                last.then_inc(ch_x, 1)
                out_rows(*fill[2 * c])
                pe.wait_ge(ch_xs, c + 1)
                for p, s, hf in each():
                    last = plain(ps[s, 1, 64 * p:64 * p + 64], tile(1, hf, p, c), state(2, p, s))
                last.then_inc(ch_u, 1)
                out_rows(*fill[2 * c + 1])
                pe.wait_ge(ch_us, c + 1)

                def u(p, s):
                    return slot[11][s, c, 64 * p:64 * p + 64]

                if c < NRCH - 1:
                    for p, s, hf in each():
                        plain(ps[s, 2, 64 * p:64 * p + 64], tile(3, hf, p, c), u(p, s), stop=False)
                        last = plain(ps[s, 2, 64 * p:64 * p + 64], tile(5, hf, p, c), tile(6, hf, p, c), start=False)
                    last.then_inc(ch_s, 1)
                for p, s, hf in each():
                    out = ps[s, 4 + p // 2, T * (p % 2) + RCH * c:T * (p % 2) + RCH * c + RCH]
                    if c:
                        plain(out, state((c - 1) % 2, p, s), tile(0, hf, p, c), stop=False)
                    plain(out, u(p, s), tile(13, hf, p, c), start=c == 0, stop=False)
                    last = plain(out, tile(6, hf, p, c), tile(14, hf, p, c), start=False)
            last.then_inc(ch_y, 1)
            for b in range(RBLK):
                for k in range(2):
                    last = plain(half(2 + b // 2, b % 2), lora_w[:, 2 + k, P * b:P * b + P], gl[:, k, :], k == 0, k == 1)
                if b % 2:
                    last.then_inc(g_proj, 1)
            head_sums(0, 12, h_mean, y_mean, lambda b: pe.wait_ge(y_made, b // 2 + 1) if b % 2 == 0 else None)
            for k in range(4):
                out_rows(0, k)
            head_sums(0, 13, h_mean, y_var, lambda b: pe.wait_ge(y_sq, b // 2 + 1) if b % 2 == 0 else None)
            for k in range(4):
                out_rows(1, k)
            for g in range(4):
                for k in range(4, KD):
                    if g == 0 and k % 2 == 0:
                        pe.wait_ge(ro_lo, k // 2 - 1)
                    if g == 3 and k == 7:
                        sum_quarters(N_FF2, (0, 1, 2))
                    last = out_rows(g, k)
                last.then_inc(chunk_used, 1)
            ffn(2, N_FF2, OUT_FF2)

            def ple(i):
                n, o = (N_PL0, OUT_PL0) if i == 0 else (N_PL1, OUT_PL1)
                c = Chunk(C0[f"pl_p{i}"])
                pe.wait_ge(p_lo, i + 1)
                pe.wait_ge(lo_made, c.count(1))
                for b in range(KD):
                    if b == 5:
                        sum_quarters(n, range(4), idle=False)
                    for k in range(2):
                        last = three(half(b // 2, b % 2), *weight(c, KD * k + b), pl_x[:, k, 0, :], pl_x[:, k, 1, :],
                                     k == 0, k == 1)
                    if b % 2 and b < KD - 1:
                        last.then_inc(e_done, 1)
                last.then_inc(chunk_used, 1)
                for g in range(4):
                    if g == 3:
                        pe.wait_ge(e_rs, i + 1)
                    early = {}
                    if g == 3:
                        early = {7: lambda: sum_quarters(n + 1, (0, 1, 2))}
                    wide_chunk(Chunk(C0[f"pl_g{i}"] + g), GATE_BANK[g], xA, x_ready(o) if g == 0 else None, early)
                    if g == 0:
                        pe.wait_ge(e_evac, 4 * i + 4)
                        for k in range(KD):
                            last = plain(half(5, 1), ones, pl_sq[:, k, :], k == 0, k == KD - 1)
                        last.then_inc(e_ss, 1)

            ple(0)
            sum_quarters(N_ML, (3,))
            for g in range(3):
                wide_chunk(Chunk(C0["ml_d"] + g), g, xA, x_ready(OUT_ML) if g == 0 else None)
            for j, ks in enumerate(((0, 1, 2), (3, 4))):
                for k in ks:
                    pe.wait_ge(c_evac, k // 2 + 1)
                    last = plain(half(4 + j, 0), ones, xt[:, k, :], k == ks[0], k == ks[-1])
                last.then_inc(c_ss, 1)
            pe.wait_ge(kr_made, 1)
            for bank in (6, 7):
                plain(ps[:, bank, 0:T], ml_fold[64:128, :], ml_kr[64:128, :]).then_inc(fold_done, 1)
            group = 0
            pe.wait_ge(c_evac, 3)
            for kn, name, k0 in ((3, "ml_q", 0), (2, "ml_k", 3)):
                for i in range(HEADS * kn):
                    h, k = divmod(i, kn)
                    c = Chunk(C0[name] + i // 16)
                    if i % 16 == 0:
                        pe.wait_ge(lo_made, c.count(1))
                    if h % 2 == 0 and k == 0:
                        g = h // 2 + (8 if kn == 2 else 0)
                        if g >= 4:
                            pe.wait_ge(ml_evac, g - 3)
                            if g < 12:
                                pe.wait_ge(ml_rope, g - 3)
                    if i < kn:
                        pe.wait_ge(c_lo, k0 + k + 1)
                    last = three(half(g % 4, h % 2), *weight(c, i % 16), xB[:, k0 + k, 0, :], xB[:, k0 + k, 1, :],
                                 k == 0, k == kn - 1)
                    if i % 16 == 15:
                        last.then_inc(chunk_used, 1)
                    elif h % 2 and k == kn - 1:
                        last.then_inc(up_done, 1)
            c = Chunk(C0["ml_v"])
            pe.wait_ge(lo_made, c.count(1))
            for i in range(4):
                t, n = divmod(i, 2)
                pe.wait_ge(ml_evac, 16 + i - 3)
                for k in range(2):
                    last = three_natural(ps[:, (16 + i) % 4, :], xB[:, 3 + k, 0, P * t:P * t + P], xB[:, 3 + k, 1, P * t:P * t + P],
                                         *weight(c, KD * k + 4 * n, 4), k == 0, k == 1)
                last.then_inc(chunk_used if i == 3 else up_done, 1)
            pe.wait_ge(ml_evac, 20)
            pe.wait_ge(ml_rope, 8)
            pe.wait_ge(kr_spread, 2)
            attention(1, lambda h: ml_q[:, h, :], lambda h: ml_k[:, h, :], ml_v, ml_pr, ml_pt)
            pe.wait_ge(o_lo, 16)
            project("ml_o", xB, None, N_FF3)
            ffn(3, N_FF3, OUT_FF3)
            ple(1)
            sum_quarters(N_FIN2, (3,))


def _cols(v):
    v = np.asarray(v).reshape(-1)
    return v.reshape(-1, P).T


def _chunks(blocks):
    return blocks.transpose(0, 2, 1, 3).reshape(-1, P, CHUNK)


def _by_columns(w):
    n = w.shape[1] // 256
    return w.reshape(KD, P, n, 256).transpose(2, 1, 0, 3).reshape(n, P, CHUNK)


def _by_rows(w):
    n = w.shape[0] // 256
    return w.reshape(n, 2, P, D).transpose(0, 2, 1, 3).reshape(n, P, CHUNK)


def _paired(w):
    up, gate = _by_columns(w[:, :FF]), _by_columns(w[:, FF:])
    return np.stack([up, gate], 1).reshape(-1, P, CHUNK)


def _by_heads(w):
    k, h = w.shape[0] // P, w.shape[1] // P
    return _chunks(w.reshape(k, P, h, P).transpose(2, 0, 1, 3).reshape(-1, 16, P, P))


def _constants():
    i = np.arange(P)
    s = np.arange(64)
    eye, ones = np.eye(P), np.ones((P, P))
    after = (i[:, None] > i[None, :])
    tri = (i[:, None] < i[None, :])
    head = (i[:, None] // 64 == i[None, :] // 64)
    cum = head * (i[:, None] <= i[None, :]) * DECAY
    cum_x = head * (i[:, None] < i[None, :]) * DECAY
    d = (s[:, None] > s[None, :]) & (s[:, None] // 8 == s[None, :] // 8)
    dt = d.T
    ot = (s[:, None] < s[None, :]) & ~dt
    strict, incl = s[:, None] < s[None, :], s[:, None] <= s[None, :]
    small = [np.concatenate([m, m], 0) for m in (d, dt, ot, strict, incl, np.eye(64))]
    hyc = np.concatenate([eye, ones, after, tri, head, head / 64.0, cum, cum_x] + small, 1)
    causal = np.where(i[None, :] <= i[:, None], 0.0, -NEG)
    fold = (i[:, None] >= 64) & (i[:, None] % 32 == i[None, :] % 32)
    mlc = np.concatenate([np.zeros((P, P)), causal, fold], 1)
    return np.ascontiguousarray(hyc, np.float32), np.ascontiguousarray(mlc, np.float32)


def kernel(**inputs):
    import concourse.bacc as bacc
    from concourse.bass_utils import run_bass_kernel_spmd

    a = {k: np.asarray(v) for k, v in inputs.items()}
    f32 = np.float32

    def zeros(*shape):
        return np.zeros(shape, f32)

    hyb = a["hyb_w_in_2"][0]
    rw = hyb[:, 1536:]
    hyb = np.concatenate([rw[:, 1536:], zeros(D, 96), rw[:, 512:1024], rw[:, :512], rw[:, 1024:1536], zeros(D, P),
                          hyb[:, :1536]], 1)
    down = a["mla_w_down_2"][0]
    kr = down[:, 640:672]
    kr_swap = np.concatenate([kr[:, 16:], kr[:, :16]], 1)
    down = np.concatenate([down[:, :640], zeros(D, 64), kr, kr_swap], 1)
    uq = a["mla_w_uq_2"][0].reshape(384, HEADS, 96)
    uq = np.concatenate([uq, uq[:, :, 80:96], uq[:, :, 64:80]], 2).reshape(384, HEADS * P)
    ukv = a["mla_w_ukv_2"][0].reshape(256, HEADS, P)
    uk = np.concatenate([ukv[:, :, :64], zeros(256, HEADS, 64)], 2).reshape(256, HEADS * P)
    uv = np.ascontiguousarray(ukv[:, :, 64:]).reshape(256, HEADS * 64)
    a_in, kv = a["a_w_in"][0], a["w_kv"]
    parts = [_by_columns(a_in[:, D:]), _by_columns(a_in[:, :D]), _by_columns(a["a_w_out"][0]),
             _paired(a["f_w_in"][0]), _by_rows(a["f_w_down"][0]),
             _by_columns(kv[:, :D]), _by_columns(kv[:, D:]), _by_columns(a["b_w_q"][0]), _by_columns(a["b_w_o"][0]),
             _paired(a["f_w_in"][1]), _by_rows(a["f_w_down"][1]),
             _by_columns(hyb), _by_columns(a["hyb_w_out_2"][0]),
             _paired(a["ffn_w_in_2"][0]), _by_rows(a["ffn_w_out_2"][0]),
             _by_rows(a["ple_w_proj_2"][0]), _by_columns(a["ple_w_gate_2"][0]),
             _by_columns(down), _by_heads(uq), _by_heads(uk), _by_rows(uv), _by_columns(a["mla_w_o_2"][0]),
             _paired(a["ffn_w_in_2"][1]), _by_rows(a["ffn_w_out_2"][1]),
             _by_rows(a["ple_w_proj_2"][1]), _by_columns(a["ple_w_gate_2"][1])]
    stream = np.concatenate(parts, 0)

    half_freq = (f32(10000.0) ** (-np.arange(16, dtype=f32) / f32(16))).astype(f32)
    freq, phase = zeros(P), zeros(P)
    freq[64:128] = np.tile(half_freq, 4)
    phase[64:96], phase[96:112] = np.pi / 2, np.pi
    mu = a["rw_mu_2"][0]
    vecs = {
        "a_norm": a["a_norm_g"][0], "a_vnorm": a["a_v_norm_g"][0], "kv_norm": a["kv_norm_g"], "b_norm": a["b_norm_g"][0],
        "f_norm0": a["f_norm_g"][0], "f_norm1": a["f_norm_g"][1], "cw0": a["f_conv_w"][0], "cw1": a["f_conv_w"][1],
        "cb0": a["f_conv_b"][0], "cb1": a["f_conv_b"][1], "fin1": a["final_norm_g"],
        "at_norm0": a["attn_norm_2"][0], "at_norm1": a["attn_norm_2"][1], "ff_norm0": a["ffn_norm_2"][0],
        "ff_norm1": a["ffn_norm_2"][1], "cw2": a["ffn_conv_w_2"][0], "cw3": a["ffn_conv_w_2"][1],
        "cb2": a["ffn_conv_b_2"][0], "cb3": a["ffn_conv_b_2"][1], "pl_norm0": a["ple_norm_2"][0],
        "pl_norm1": a["ple_norm_2"][1], "pl_gnorm0": a["ple_gate_norm_2"][0], "pl_gnorm1": a["ple_gate_norm_2"][1],
        "rw_mu": np.concatenate([mu[1536:], zeros(96), mu[512:1024], mu[:512], mu[1024:1536]]), "rw_a0": a["rw_a0_2"][0], "rw_kk": a["rw_k_k_2"][0],
        "rw_ka": a["rw_k_a_2"][0], "rw_rk": a["rw_r_k_2"][0], "rw_lnw": a["rw_ln_w_2"][0], "rw_lnb": a["rw_ln_b_2"][0],
        "q_norm": a["mla_q_norm_2"][0], "c_norm": a["mla_kv_norm_2"][0], "fin2": a["final_norm_2"],
        "eps": zeros(P) + f32(EPS), "gn_eps": zeros(P) + f32(GN_EPS), "freq": freq, "turn": phase / f32(2 * np.pi),
        "phase": phase, "ln256": zeros(P) + f32(8 * np.log(2.0)),
    }
    packed = np.concatenate([_cols(vecs[name]) for name, _ in _VECS], 1).astype(f32)
    hyc, mlc = _constants()
    rel = a["b_rel_bias"][0][:, ::-1]
    ext = np.concatenate([np.repeat(rel[:, :1], P, 1), rel[:, :256]], 1)
    rel = np.lib.stride_tricks.sliding_window_view(ext, T, 1)[:, P:0:-1].transpose(1, 0, 2)
    lora = np.concatenate([a["rw_w2_2"][0], zeros(64, 512), zeros(64, 512), a["rw_a2_2"][0], a["rw_g2_2"][0],
                           zeros(96, 512)], 0).reshape(4, P, 512).transpose(1, 0, 2)
    arrays = {
        "stream": stream,
        "x_t": a["x"][0].T.reshape(KD, P, T).transpose(1, 0, 2),
        "vecs": packed,
        "wst": a["a_w_s"][0].transpose(2, 0, 1),
        "bsp": a["a_b_s"][0],
        "rel": rel, "hyc": hyc, "w0": a["rw_w0_2"], "lora": lora, "mlc": mlc, "pos": a["positions_2"],
        "p_t": a["p_2"][:, 0].transpose(0, 2, 1).reshape(2, 2, P, T).transpose(0, 2, 1, 3),
    }
    nc = bacc.Bacc("TRN2", target_bir_lowering=False, num_devices=1)
    args = []
    for name in arrays:
        arrays[name] = np.ascontiguousarray(arrays[name])
        args.append(nc.dram_tensor(name, arrays[name].shape, mybir.dt.from_np(arrays[name].dtype),
                                   kind="ExternalInput").ap())
    args.append(nc.dram_tensor("out_t", (P, KD, T), F32, kind="ExternalOutput").ap())
    build(nc, *args)
    r = run_bass_kernel_spmd(nc, [arrays], core_ids=[0])
    got = r.results[0]["out_t"]
    return np.ascontiguousarray(got.transpose(2, 1, 0).reshape(1, T, D))
```

```python
from contextlib import ExitStack

import numpy as np

import concourse.bass as bass
from concourse import mybir

F32 = mybir.dt.float32
F32R = mybir.dt.float32r
I32 = mybir.dt.int32
ALU = mybir.AluOpType
ACT = mybir.ActivationFunctionType
AX_X = mybir.AxisListType.X

P = 128
T = 256
D = 1024
KD = D // P
FF = 2816
KF = FF // P
PAIRS = KF // 2
CHUNK = 16 * P
RING = 4
AHEAD = 3
EPS = 1e-6
GN_EPS = 64e-5
NEG = -1e30
HCON = 6 * 128 + 6 * 64
HEADS = 16
RBLK = 4
RCH = 64
NRCH = T // RCH
MLA_SCALE = 96 ** -0.5
DECAY = -float(np.exp(np.float64(-0.5)))

_PLAN = [("gm_v", 4), ("gm_u", 4), ("gm_o", 4), ("up0", 22), ("dn0", 11),
         ("at_k", 4), ("at_v", 4), ("at_q", 4), ("at_o", 4), ("up1", 22), ("dn1", 11),
         ("hy", 14), ("hy_o", 4), ("up2", 22), ("dn2", 11), ("pl_p0", 1), ("pl_g0", 4),
         ("ml_d", 3), ("ml_q", 3), ("ml_k", 2), ("ml_v", 1), ("ml_o", 4),
         ("up3", 22), ("dn3", 11), ("pl_p1", 1), ("pl_g1", 4)]
C0, NCH = {}, 0
for _name, _n in _PLAN:
    C0[_name] = NCH
    NCH += _n

_VECS = [("a_norm", 8), ("a_vnorm", 8), ("kv_norm", 8), ("b_norm", 8), ("f_norm0", 8), ("f_norm1", 8),
         ("cw0", 132), ("cw1", 132), ("cb0", 44), ("cb1", 44), ("fin1", 8),
         ("at_norm0", 8), ("at_norm1", 8), ("ff_norm0", 8), ("ff_norm1", 8),
         ("cw2", 66), ("cw3", 66), ("cb2", 22), ("cb3", 22),
         ("pl_norm0", 8), ("pl_norm1", 8), ("pl_gnorm0", 8), ("pl_gnorm1", 8),
         ("rw_mu", 15), ("rw_a0", 4), ("rw_kk", 4), ("rw_ka", 4), ("rw_rk", 4), ("rw_lnw", 4), ("rw_lnb", 4),
         ("q_norm", 3), ("c_norm", 2), ("fin2", 8),
         ("eps", 1), ("gn_eps", 1), ("freq", 1), ("turn", 1), ("phase", 1), ("ln256", 1)]
VC, NV = {}, 0
for _name, _n in _VECS:
    VC[_name] = NV
    NV += _n

OUT_GM, OUT_GATED, OUT_FF0, OUT_KV, OUT_Q, OUT_FF1, OUT_HY, OUT_FF2, OUT_PL0, OUT_FF3, OUT_PL1 = range(11)
N_GM, N_FF0, N_AT, N_FF1, N_FIN1, N_HY, N_FF2, N_PL0, N_ML, N_FF3, N_PL1, N_FIN2 = range(12)

EARLY = {N_FF0: ("f_norm0", 2), N_AT: ("kv_norm", 3), N_FF1: ("f_norm1", 2), N_HY: ("at_norm0", 3),
         N_FF2: ("ff_norm0", 2), N_ML: ("at_norm1", 3), N_FF3: ("ff_norm1", 2)}
EARLY_AT = {n: i for i, n in enumerate(EARLY)}
SCALED_AT = {n: sum(c for m, (_, c) in EARLY.items() if m < n) for n in EARLY}
FINAL_XT = 8 * 11
FILL = (3, 9)
GATE_BANK = (4, 6, 7, 5)
UNITS = ((0, 1), (1, 2), (2, 4), (4, 6), (6, 8))
ML_SPLITS = (0, 2, 4, 6, 9, 12, 16)
BESIDE = 5
EVACS = {4: 2, 8: 2, 14: 2, 16: 2}


def build(nc, stream, x_t, vecs, wst, bsp, rel, hyc, w0, lora, mlc, pos, p_t, out):
    with ExitStack() as ctx:
        def sem(name):
            return ctx.enter_context(nc.semaphore(name))

        def sb(name, shape, dt=F32, where=ctx):
            return where.enter_context(nc.sbuf_tensor(name, shape, dt))

        raw = [sb(f"raw{i}", [P, CHUNK]) for i in range(RING)]
        w_hi = [sb(f"w_hi{i}", [P, CHUNK], F32R) for i in range(RING)]
        w_lo = [sb(f"w_lo{i}", [P, CHUNK], F32R) for i in range(RING)]
        hT = sb("hT", [P, KD, T])
        vec = sb("vec", [P, NV])
        eye_ones = sb("eye_ones", [P, 2 * P])
        rs = sb("rs", [P, T])
        xB = sb("xB", [P, KD, 2, T], F32R)
        with ExitStack() as ph:
            xt = sb("xt", [P, KD, T], where=ph)
            xA = sb("xA", [P, KD, 2, T], F32R, ph)
            with ExitStack() as f:
                hid = sb("hid", [P, KF, 2, T], F32R, f)
                up_acc = [sb(f"up_acc{i}", [P, 2, T], where=f) for i in range(2)]
                gate_acc = [sb(f"gate_acc{i}", [P, 2, T], where=f) for i in range(2)]
                pl_in = sb("pl_in", [P, 2, T], where=f)
                pl_x = sb("pl_x", [P, 2, 2, T], F32R, f)
            with ExitStack() as f:
                uT = sb("uT", [P, KD, T], where=f)
                vnat = sb("vnat", [P, 2, D], where=f)
                wsT = sb("wsT", [P, KD, P], where=f)
                bsb = sb("bsb", [P, KD, P], where=f)
                gm_junk = sb("gm_junk", [P, T], where=f)
                gm_sum = sb("gm_sum", [P, 8], where=f)
                gm_rs = sb("gm_rs", [P, 4], where=f)
            with ExitStack() as f:
                at_qT = sb("at_qT", [P, KD, T], where=f)
                at_k = sb("at_k", [P, KD, T], where=f)
                at_v = sb("at_v", [P, 2, D], where=f)
                at_bias = sb("at_bias", [P, HEADS, T], where=f)
                at_pr = [sb(f"at_pr{i}", [P, 384], where=f) for i in range(3)]
                at_pt = [sb(f"at_pt{i}", [P, 384], where=f) for i in range(2)]
                at_st = sb("at_st", [P, 3, 2 * HEADS], where=f)
            with ExitStack() as f:
                ml_q = sb("ml_q", [P, HEADS, T], where=f)
                ml_k = sb("ml_k", [P, HEADS, T], where=f)
                ml_v = sb("ml_v", [P, 2, D], where=f)
                ml_c = sb("ml_c", [P, 5, T], where=f)
                ml_pr = [sb(f"ml_pr{i}", [P, 384], where=f) for i in range(3)]
                ml_pt = [sb(f"ml_pt{i}", [P, 384], where=f) for i in range(2)]
                ml_st = sb("ml_st", [P, 3, 2 * HEADS], where=f)
                ml_con = sb("ml_con", [P, 384], where=f)
                ml_cs = sb("ml_cs", [P, T], where=f)
                ml_pos = sb("ml_pos", [P, T], I32, f)
                ml_kr = sb("ml_kr", [P, T], where=f)
            ml_bias, ml_fold = ml_con[:, 0:256], ml_con[:, 256:384]
            ml_rs = [t[:, 0:T] for t in ml_pt]
            ml_ang, ml_n = ml_pr[0][:, 0:T], ml_pr[1][:, 0:T]
            with ExitStack() as f:
                pl_e = sb("pl_e", [P, KD, T], where=f)
                pl_sq = sb("pl_sq", [P, KD, T], where=f)
                pl_rb = sb("pl_rb", [P, T], where=f)
                pl_sg = [sb(f"pl_sg{i}", [P, 2, T], where=f) for i in range(2)]
            with ExitStack() as f:
                hcon = sb("hcon", [P, HCON], where=f)
                w0b = sb("w0b", [P, 512], where=f)
                wlal = sb("wlal", [P, T], where=f)
                gl = sb("gl", [P, 2, T], where=f)
                pend = sb("pend", [P, RBLK, NRCH], where=f)
                om_mu = sb("om_mu", [P, 15], where=f)
                slot = [sb(f"slot{i}", [P, RBLK, T], where=f) for i in range(12)]
        with ExitStack() as f:
            lora_w = sb("lora_w", [P, 4, 512], where=f)
            with ExitStack() as g:
                sb_l = [sb(f"sb_l{i}", [P, 2, 384], where=g) for i in range(2)]
                sb_ls = [sb(f"sb_ls{i}", [P, 2, 384], where=g) for i in range(2)]
            slot += [sb(f"slot{i}", [P, RBLK, T], where=f) for i in range(12, 16)]
        sb_q, sb_k, sb_v = slot[7], slot[10], slot[11][:].rearrange("p b t -> p (b t)").rearrange("p (a n) -> p a n", a=2)
        h_after, h_tri, h_sum, h_mean = [hcon[:, P * i:P * i + P] for i in range(4)]
        h_cum = hcon[:, 4 * P:6 * P]
        m_d, m_dt, m_ot, m_strict, m_incl = [hcon[:, 6 * P + 64 * i:6 * P + 64 * i + 64] for i in range(5)]
        ps = ctx.enter_context(nc.psum_tensor("ps", [P, 8, 512], F32))

        eye, ones = eye_ones[:, 0:P], eye_ones[:, P:2 * P]

        def half(bank, h):
            return ps[:, bank, T * h:T * h + T]

        def col(name, j=0, n=1):
            return vec[:, VC[name] + j:VC[name] + j + n]

        def dcol(name, j, off):
            if isinstance(j, int):
                return col(name, off + j)
            return vec[:, bass.ds(j + (VC[name] + off), 1)]

        def rows(tile, k, n, part):
            if isinstance(k, int):
                return tile[:, k:k + n, part, :]
            return tile[:, bass.ds(k, n), part, :]

        raw_landed = [sem(f"raw_landed{i}") for i in range(RING)]
        hi_made = sem("hi_made")
        lo_made = sem("lo_made")
        chunk_used = sem("chunk_used")
        x_landed = [sem(f"x_landed{b}") for b in range(4)]
        vec_landed, eye_landed = sem("vec_landed"), sem("eye_landed")
        gm_landed = sem("gm_landed")
        h_updated = sem("h_updated")
        sq_made = sem("sq_made")
        ss_summed = sem("ss_summed")
        sq_added = sem("sq_added")
        rs_made = sem("rs_made")
        xt_made = sem("xt_made")
        x_hi_made = sem("x_hi_made")
        x_lo_made = sem("x_lo_made")
        raw_hi = sem("raw_hi")
        raw_lo = sem("raw_lo")
        raw_scaled = sem("raw_scaled")
        dve_own = sem("dve_own")
        act_own = sem("act_own")
        up_lin, gate_lin = sem("up_lin"), sem("gate_lin")
        tap_done = sem("tap_done")
        up_conv, gate_conv = sem("up_conv"), sem("gate_conv")
        gate_on = sem("gate_on")
        prod_made = sem("prod_made")
        hid_hi, hid_lo = sem("hid_hi"), sem("hid_lo")
        down_bank = sem("down_bank")
        gm_evac, gm_sums, gm_std, gm_scaled, gm_mixed, gm_masked = [
            sem(n) for n in ("gm_evac", "gm_sums", "gm_std", "gm_scaled", "gm_mixed", "gm_masked")]
        qkv_evac, bias_ready = sem("qkv_evac"), sem("bias_ready")
        bias_landed, bias_negated = sem("bias_landed"), sem("bias_negated")
        scored, max_made, exp_made, prob_made, prob_turned, turned_copied, mixed = [
            sem(n) for n in ("scored", "max_made", "exp_made", "prob_made", "prob_turned", "turned_copied", "mixed")]
        o_hi, o_lo = sem("o_hi"), sem("o_lo")
        hy_landed, lora_landed = sem("hy_landed"), sem("lora_landed")
        hy_evac, hy_lin, hy_mixed = sem("hy_evac"), sem("hy_lin"), sem("hy_mixed")
        z_made, log_made, stick_made, after_made, arg_made, w_made, w_masked, sb_mixed, sb_hi, sb_lo = [
            sem(n) for n in ("z_made", "log_made", "stick_made", "after_made", "arg_made", "w_made", "w_masked",
                             "sb_mixed", "sb_hi", "sb_lo")]
        (mu_ready, lora_in, w_proj, a_proj, w_arg, w_sig, a_sig, cum_made, decay_made, kk_made, kk_sq, kk_ss, kk_max,
         kk_rn, rk_made, rk_sum, factors, imdt_made, bonus_made) = [sem(n) for n in (
             "mu_ready", "lora_in", "w_proj", "a_proj", "w_arg", "w_sig", "a_sig", "cum_made", "decay_made", "kk_made",
             "kk_sq", "kk_ss", "kk_max", "kk_rn", "rk_made", "rk_sum", "factors", "imdt_made", "bonus_made")]
        mat_done = sem("mat_done")
        mat = [sem(f"mat{i}") for i in range(22)]
        ch_x, ch_xs, ch_u, ch_us, ch_s, ch_st, ch_y = [
            sem(n) for n in ("ch_x", "ch_xs", "ch_u", "ch_us", "ch_s", "ch_st", "ch_y")]
        y_made, y_mean, yc_made, y_sq, y_var, y_rstd, g_proj, ro_made, ro_hi, ro_lo = [
            sem(n) for n in ("y_made", "y_mean", "yc_made", "y_sq", "y_var", "y_rstd", "g_proj", "ro_made", "ro_hi",
                             "ro_lo")]
        p_landed, p_hi, p_lo, e_done, e_evac, e_ss, e_rs, g_on = [
            sem(n) for n in ("p_landed", "p_hi", "p_lo", "e_done", "e_evac", "e_ss", "e_rs", "g_on")]
        ml_landed, cs_arg, cs_made, c_evac, kr_made, c_ss, c_rs, c_made, c_hi, c_lo = [
            sem(n) for n in ("ml_landed", "cs_arg", "cs_made", "c_evac", "kr_made", "c_ss", "c_rs", "c_made", "c_hi",
                             "c_lo")]
        up_done, ml_evac, ml_rope, fold_done, kr_spread = [
            sem(n) for n in ("up_done", "ml_evac", "ml_rope", "fold_done", "kr_spread")]
        stored = sem("stored")

        block = ctx.enter_context(nc.Block())

        def at_least(eng, s, value):
            if not isinstance(value, int) or value > 0:
                eng.wait_ge(s, value)

        def mixed_block(j):
            if j < 3:
                return gl[:, j - 1, :] if j else wlal[:]
            i, b = divmod(j - 3, 4)
            return slot[(1, 0, 2)[i]][:, b, :]

        def hy_bank(g):
            return g if g < 4 else g % 2

        def product_bank(i, b):
            return (2 * i + b) % 3 if i < BESIDE else 2 * (i % 4) + b

        def early_tile(n):
            return xB if n in (N_HY, N_ML) else xA

        def flat(i):
            return slot[i][:].rearrange("p b t -> p (b t)")

        class Own:

            def __init__(self, eng, s):
                self.eng, self.s, self.n = eng, s, 0

            def mark(self, ins):
                ins.then_inc(self.s, 1)
                self.n += 1
                return self.n

            def wait(self, n=None):
                self.eng.wait_ge(self.s, self.n if n is None else n)

        class Chunk:

            def __init__(self, first, it=None):
                self.first, self.it, self.slot = first, it, first % RING

            def count(self, more):
                return self.first + more if self.it is None else self.it * RING + (self.first + more)

            def landed(self):
                n = 16 * (self.first // RING + 1)
                return n if self.it is None else self.it * 16 + n

            def ahead(self):
                if self.it is None and self.first + AHEAD >= NCH:
                    return None
                return Chunk(self.first + AHEAD, self.it)

        ends_chunk = {7: C0["ml_q"] + 2, 11: C0["ml_k"], 15: C0["ml_k"] + 1, 19: C0["ml_v"]}

        def wait_up(eng, g):
            if g in ends_chunk:
                eng.wait_ge(chunk_used, ends_chunk[g] + 1)
            else:
                eng.wait_ge(up_done, g + 1 - sum(e < g for e in ends_chunk))

        @block.sync
        def _(sp):
            sp.dma_start(raw[0][:], stream[0]).then_inc(raw_landed[0], 16)
            sp.dma_start(eye_ones[:], hyc[:, 0:2 * P]).then_inc(eye_landed, 16)
            for b in range(4):
                sp.dma_start(hT[:, 2 * b:2 * b + 2], x_t[:, 2 * b:2 * b + 2]).then_inc(x_landed[b], 16)
            sp.dma_start(vec[:], vecs).then_inc(vec_landed, 16)
            for c in range(1, RING):
                sp.dma_start(raw[c][:], stream[c]).then_inc(raw_landed[c], 16)
            with sp.Fori(1, NCH // RING) as it:
                for s in range(RING):
                    sp.wait_ge(lo_made, it * RING + (s + 1 - RING))
                    src = stream[bass.ds(it * RING + s, 1)].rearrange("a p n -> p (a n)")
                    sp.dma_start(raw[s][:], src).then_inc(raw_landed[s], 16)
            for c in range(NCH // RING * RING, NCH):
                sp.wait_ge(lo_made, c + 1 - RING)
                sp.dma_start(raw[c % RING][:], stream[c]).then_inc(raw_landed[c % RING], 16)
            for b in range(4):
                sp.wait_ge(xt_made, FINAL_XT + 2 * b + 2)
                sp.dma_start(out[:, 2 * b:2 * b + 2], xt[:, 2 * b:2 * b + 2]).then_inc(stored, 16)
            sp.wait_ge(stored, 64)

        @block.gpsimd
        def _(pool):
            def add_squares(n):
                pool.wait_ge(sq_made, 4 * n + 2)
                nc.gpsimd.tensor_tensor(xt[:, 0:2, :], xt[:, 0:2, :], xt[:, 2:4, :], ALU.add).then_inc(sq_added, 1)

            add_squares(N_GM)
            pool.wait_ge(sq_added, N_GM + 1)
            pool.wait_ge(gm_landed, 32)
            nc.gpsimd.memset(wsT[64:128, :, 0:64], 0.0).then_inc(gm_masked, 1)
            add_squares(N_FF0)
            add_squares(N_AT)
            pool.wait_ge(h_updated, 8)
            pool.dma_start(at_bias[:], rel).then_inc(bias_landed, 16)
            pool.wait_ge(sq_added, N_AT + 1)
            pool.wait_ge(bias_landed, 16)
            nc.gpsimd.tensor_scalar(at_bias[:], at_bias[:], -1.0, None, ALU.mult).then_inc(bias_negated, 1)
            pool.wait_ge(bias_negated, 1)
            nc.gpsimd.memset(at_bias[0:64, :, 192:256], -NEG).then_inc(bias_ready, 1)
            add_squares(N_FF1)
            add_squares(N_FIN1)
            pool.wait_ge(h_updated, 16)
            pool.dma_start(hcon[:], hyc[:, 2 * P:]).then_inc(hy_landed, 16)
            pool.dma_start(w0b[:], bass.AP(w0.tensor, 0, [[0, P], [1, 512]])).then_inc(hy_landed, 16)
            add_squares(N_HY)
            pool.wait_ge(x_lo_made, 5 * (OUT_HY + 1))
            pool.dma_start(lora_w[:], lora).then_inc(lora_landed, 16)
            add_squares(N_FF2)
            pool.wait_ge(h_updated, 24)
            pool.dma_start(pl_in[:], p_t[0]).then_inc(p_landed, 16)
            add_squares(N_PL0)
            add_squares(N_ML)
            pool.wait_ge(h_updated, 32)
            pool.dma_start(ml_con[:], mlc).then_inc(ml_landed, 16)
            pool.dma_start(ml_pos[:], bass.AP(pos.tensor, 0, [[0, P], [1, T]])).then_inc(ml_landed, 16)
            add_squares(N_FF3)
            pool.wait_ge(h_updated, 36)
            pool.dma_start(pl_in[:], p_t[1]).then_inc(p_landed, 16)
            add_squares(N_PL1)
            add_squares(N_FIN2)

        @block.scalar
        def _(act):
            own = Own(act, act_own)

            def split_hi(c):
                if c is None:
                    return
                act.wait_ge(raw_landed[c.slot], c.landed())
                at_least(act, chunk_used, c.count(1 - RING))
                nc.scalar.activation(w_hi[c.slot][:], raw[c.slot][:], ACT.Copy).then_inc(hi_made, 1)

            def inverse_root(dst, sums, width, made):
                own.mark(nc.scalar.activation(dst, sums, ACT.Ln, bias=col("eps"), scale=1.0 / width))
                own.wait()
                nc.scalar.activation(dst, dst, ACT.Exp, scale=-0.5).then_inc(made, 1)

            def square(n, b, preload=True):
                if n == 0:
                    act.wait_ge(x_landed[b], 16)
                else:
                    act.wait_ge(h_updated, 4 * (n - 1) + b + 1)
                if b == 2 and preload:
                    nc.scalar.preload_act_table_set("natural_log_exp_and_others")
                if n in EARLY:
                    for k in (2 * b, 2 * b + 1):
                        last = nc.scalar.activation(early_tile(n)[:, k, 0, :], hT[:, k, :], ACT.Copy,
                                                    scale=col(EARLY[n][0], k))
                    last.then_inc(raw_hi, 1)
                nc.scalar.activation(xt[:, 2 * b:2 * b + 2, :], hT[:, 2 * b:2 * b + 2, :],
                                     ACT.Square).then_inc(sq_made, 1)

            def square_norm(n):
                for b in range(4):
                    square(n, b)
                root_norm(n)

            def root_norm(n):
                act.wait_ge(ss_summed, n + 1)
                inverse_root(rs[:], half(4, 0), D, rs_made)

            def round_x(o, dst, ahead=()):
                for u, (lo, hi) in enumerate(UNITS):
                    act.wait_ge(xt_made, 8 * o + hi)
                    nc.scalar.activation(dst[:, lo:hi, 0, :], xt[:, lo:hi, :], ACT.Copy).then_inc(x_hi_made, 1)
                    if u == 2:
                        for c in ahead:
                            split_hi(Chunk(c))

            def split_and_square(name, n):
                for g in range(4):
                    split_hi(Chunk(C0[name] + g).ahead())
                    if g:
                        square(n, g - 1)
                square(n, 3)
                root_norm(n)

            def ffn(f, n):
                c0, base, both = C0[f"up{f}"], PAIRS * f, f < 2
                goff = KF if both else 0

                def linear(acc, bank, q, off):
                    for b in range(2):
                        j = 2 * q + b if isinstance(q, int) else q * 2 + b
                        last = nc.scalar.activation(acc[:, b, :], half(bank, b), ACT.Identity,
                                                    bias=dcol(f"cb{f}", j, off),
                                                    scale=dcol(f"cw{f}", j, off + 2 * (goff + KF)))
                    return last

                def gate(q, par):
                    act.wait_ge(gate_conv, q + (base + 1))
                    nc.scalar.activation(gate_acc[par][:], gate_acc[par][:],
                                         ACT.Silu if both else ACT.Gelu).then_inc(gate_on, 1)

                def round_hid(q, par):
                    act.wait_ge(prod_made, q + (base + 1))
                    nc.scalar.activation(rows(hid, q * 2, 2, 0), up_acc[par][:], ACT.Copy).then_inc(hid_hi, 1)

                def pair(q, par, cu, cg, first=False, second=False):
                    split_hi(cu.ahead())
                    if not first:
                        gate(q - 1, 1 - par)
                    if both:
                        act.wait_ge(chunk_used, cu.count(1))
                        if first:
                            act.wait_ge(raw_scaled, SCALED_AT[n] + 1)
                        if not (first or second):
                            act.wait_ge(hid_lo, q + (base - 1))
                        linear(up_acc[par], 2 * par, q, 0).then_inc(up_lin, 1)
                    split_hi(cg.ahead())
                    if not first:
                        round_hid(q - 1, 1 - par)
                    act.wait_ge(chunk_used, cg.count(1))
                    if first:
                        act.wait_ge(raw_scaled, SCALED_AT[n] + 2)
                    if not (first or second):
                        act.wait_ge(prod_made, q + (base - 1))
                    linear(gate_acc[par], 2 * par + 1, q, goff).then_inc(gate_lin, 1)

                pair(0, 0, Chunk(c0), Chunk(c0 + 1), first=True)
                pair(1, 1, Chunk(c0 + 2), Chunk(c0 + 3), second=True)
                pair(2, 0, Chunk(c0 + 4), Chunk(c0 + 5))
                with act.Fori(0, (PAIRS - 3) // 2) as it:
                    for j in range(2):
                        pair(it * 2 + (3 + j), (3 + j) % 2, Chunk(c0 + 6 + 2 * j, it), Chunk(c0 + 7 + 2 * j, it))
                gate(PAIRS - 1, (PAIRS - 1) % 2)
                round_hid(PAIRS - 1, (PAIRS - 1) % 2)
                d0 = C0[f"dn{f}"]
                with act.Fori(0, 2) as it:
                    for s in range(RING):
                        split_hi(Chunk(d0 + s, it).ahead())
                if f >= 2:
                    act.wait_ge(p_landed, 16 * (f - 1))
                    nc.scalar.activation(pl_x[:, :, 0, :], pl_in[:], ACT.Copy).then_inc(p_hi, 1)
                for s in range(8, PAIRS):
                    split_hi(Chunk(d0 + s).ahead())

            def attention(a, pr, pt, st):
                h0, m0 = HEADS * a, KD * a

                def exponent(h):
                    act.wait_ge(max_made, h0 + h + 1)
                    for t, (lo, hi) in enumerate(((0, P), (P, 384))):
                        last = nc.scalar.activation(pr[h % 3][:, lo:hi], pr[h % 3][:, lo:hi], ACT.Exp, scale=-1.0,
                                                    bias=st[:, 0, 2 * h + t:2 * h + t + 1],
                                                    accum_out=st[:, 1, 2 * h + t:2 * h + t + 1])
                    last.then_inc(exp_made, 1)

                def copy_turned(h):
                    act.wait_ge(prob_turned, h0 + h + 1)
                    if h >= 2:
                        act.wait_ge(mixed, h0 + h - 1)
                    nc.scalar.activation(pt[h % 2][:], ps[:, 2 + h % 2, 0:384], ACT.Copy).then_inc(turned_copied, 1)

                def round_o(m):
                    act.wait_ge(mixed, h0 + 2 * m + 2)
                    nc.scalar.activation(xB[:, m, 0, :], half(4 + m % 4, 0), ACT.Copy).then_inc(o_hi, 1)

                for i in range(HEADS + 4):
                    if i < HEADS:
                        exponent(i)
                    if 2 <= i <= HEADS + 1:
                        copy_turned(i - 2)
                    if i >= 5 and i % 2:
                        round_o((i - 5) // 2)

            split_hi(Chunk(0))
            for b in range(4):
                square(N_GM, b)
            act.wait_ge(vec_landed, 16)
            root_norm(N_GM)
            act.dma_start(wsT[:], wst).then_inc(gm_landed, 16)
            act.dma_start(bsb[:], bass.AP(bsp.tensor, 0, [[0, P], [P, KD], [1, P]])).then_inc(gm_landed, 16)
            round_x(OUT_GM, xA, ahead=range(1, AHEAD))
            for g in range(8):
                split_hi(Chunk(g).ahead())
                act.wait_ge(chunk_used, g + 1)
                if g < 4:
                    dst = vnat[:, :, T * g:T * g + T]
                else:
                    dst = uT[:, 2 * (g - 4):2 * (g - 4) + 2, :]
                nc.scalar.activation(dst, ps[:, g % 4, :].rearrange("p (b t) -> p b t", b=2),
                                     ACT.Gelu_apprx_tanh).then_inc(gm_evac, 1)
                if g == 4:
                    act.wait_ge(gm_sums, 1)
                    inverse_root(gm_rs[:, 0:2], gm_rs[:, 2:4], D, gm_std)
            round_x(OUT_GATED, xB)
            split_and_square("gm_o", N_FF0)
            round_x(OUT_FF0, xB)
            ffn(0, N_FF0)
            square_norm(N_AT)
            round_x(OUT_KV, xB)
            early = EARLY[N_AT][1]
            for g in range(early):
                split_hi(Chunk(C0["at_k"] + g).ahead())
            for g in range(12):
                if g >= early:
                    split_hi(Chunk(C0["at_k"] + g).ahead())
                else:
                    act.wait_ge(raw_scaled, SCALED_AT[N_AT] + g + 1)
                act.wait_ge(chunk_used, C0["at_k"] + g + 1)
                two = ps[:, g % 4, :].rearrange("p (b t) -> p b t", b=2)
                if g < 4:
                    ins = nc.scalar.activation(at_k[:, 2 * g:2 * g + 2, :], two, ACT.Copy)
                elif g < 8:
                    ins = nc.scalar.activation(at_v[:, :, T * (g - 4):T * (g - 3)], two, ACT.Copy)
                else:
                    ins = nc.scalar.activation(at_qT[:, 2 * (g - 8):2 * (g - 8) + 2, :], two, ACT.Copy, scale=-0.125)
                ins.then_inc(qkv_evac, 1)
                if g == early:
                    round_x(OUT_Q, xA)
            attention(0, at_pr, at_pt, at_st)
            split_and_square("at_o", N_FF1)
            round_x(OUT_FF1, xB)
            ffn(1, N_FF1)
            square_norm(N_FIN1)
            square_norm(N_HY)
            round_x(OUT_HY, xA)
            c0 = C0["hy"]

            def log_parts(u):
                act.wait_ge(z_made, u + 1)
                if u >= 2:
                    act.wait_ge(after_made, u - 1)
                buf, z = sb_l[u % 2][:], ps[:, 4 + 2 * (u % 2):6 + 2 * (u % 2), 0:384]
                own.mark(nc.scalar.activation(buf, z, ACT.Abs))
                own.wait()
                own.mark(nc.scalar.activation(buf, buf, ACT.Exp, scale=-1.0))
                own.wait()
                nc.scalar.activation(buf, buf, ACT.Ln, bias=1.0).then_inc(stick_made, 1)

            def weights(u):
                act.wait_ge(arg_made, u + 1)
                nc.scalar.activation(sb_ls[u % 2][:], sb_ls[u % 2][:], ACT.Exp).then_inc(w_made, 1)

            def round_sb(u):
                act.wait_ge(sb_mixed, u + 1)
                nc.scalar.activation(xB[:, u, 0, :], half(3, u % 2), ACT.Copy).then_inc(sb_hi, 1)

            def decay(dst, i, sign):
                cums = ps[:, 2:6, :].rearrange("p b (t i n) -> p b t i n", t=2, i=2)
                nc.scalar.activation(slot[dst][:].rearrange("p b (t n) -> p b t n", t=2), cums[:, :, :, i, :], ACT.Exp,
                                     scale=sign).then_inc(decay_made, 1)

            act.wait_ge(mu_ready, 1)
            for g in range(14):
                if g == 6:
                    for t in range(2):
                        act.wait_ge(w_arg, t + 1)
                        nc.scalar.activation(flat(3)[:, 512 * t:512 * t + 512], flat(3)[:, 512 * t:512 * t + 512],
                                             ACT.Sigmoid).then_inc(w_sig, 1)
                    act.wait_ge(a_proj, 2)
                    for b in range(RBLK):
                        last = nc.scalar.activation(slot[4][:, b, :], half(4 + b // 2, b % 2), ACT.Sigmoid,
                                                    bias=col("rw_a0", b))
                    last.then_inc(a_sig, 1)
                split_hi(Chunk(c0 + g).ahead())
                if g == 2:
                    act.wait_ge(hy_mixed, 1)
                    nc.scalar.activation(wlal[0:64, :], wlal[0:64, :], ACT.Tanh).then_inc(lora_in, 1)
                elif g == 3:
                    act.wait_ge(hy_mixed, 2)
                    nc.scalar.activation(gl[:], gl[:], ACT.Sigmoid).then_inc(lora_in, 1)
                elif g == 4:
                    act.wait_ge(kk_made, 1)
                    nc.scalar.activation(slot[9][:], slot[8][:], ACT.Square).then_inc(kk_sq, 1)
                elif g == 6:
                    nc.scalar.preload_act_table_set("natural_log_exp_and_others")
                    act.wait_ge(kk_max, 2)
                    own.mark(nc.scalar.activation(slot[9][:], slot[9][:], ACT.Ln, scale=65536.0))
                    own.wait()
                    nc.scalar.activation(slot[9][:], slot[9][:], ACT.Exp, scale=-0.5, bias=col("ln256")).then_inc(kk_rn, 1)
                elif g == 7:
                    act.wait_ge(cum_made, 1)
                    decay(5, 1, 1.0)
                    decay(6, 0, -1.0)
                elif g == 9:
                    act.wait_ge(factors, 1)
                    decay(5, 0, 1.0)
                act.wait_ge(chunk_used, c0 + g + 1)
                if g < EARLY[N_HY][1]:
                    act.wait_ge(raw_scaled, SCALED_AT[N_HY] + g + 1)
                two = ps[:, hy_bank(g), :].rearrange("p (b t) -> p b t", b=2)
                if g < 8:
                    for b in range(2 if g < 7 else 1):
                        last = nc.scalar.activation(mixed_block(2 * g + b), half(hy_bank(g), b), ACT.Copy,
                                                    scale=om_mu[:, 2 * g + b:2 * g + b + 1])
                    last.then_inc(hy_lin, 1)
                elif g < 10:
                    nc.scalar.activation(sb_q[:, 2 * g - 16:2 * g - 14, :], two, ACT.Copy, scale=0.125).then_inc(hy_evac, 1)
                elif g < 12:
                    nc.scalar.activation(sb_k[:, 2 * g - 20:2 * g - 18, :], two, ACT.Copy).then_inc(hy_evac, 1)
                else:
                    nc.scalar.activation(sb_v[:, :, T * (g - 12):T * (g - 11)], two, ACT.Copy).then_inc(hy_evac, 1)

            def copy_product(i, dst):
                for b in range(2):
                    act.wait_ge(mat_done, 2 * i + b + 1)
                    nc.scalar.activation(slot[dst][:, 2 * b:2 * b + 2, :],
                                         ps[:, product_bank(i, b), :].rearrange("p (b t) -> p b t", b=2),
                                         ACT.Copy).then_inc(mat[i], 1)

            log_parts(0)
            log_parts(1)
            act.wait_ge(factors, 5)
            copy_product(0, 3)
            weights(0)
            copy_product(1, 5)
            weights(1)
            log_parts(2)
            round_sb(0)
            copy_product(2, 6)
            log_parts(3)
            round_sb(1)
            weights(2)
            weights(3)
            round_sb(2)
            round_sb(3)
            split_hi(Chunk(C0["hy_o"]).ahead())
            for i, dst in ((9, 4), (11, 10), (12, 1), (13, 2), (15, 10), (17, 2), (19, 10), (20, 7), (21, 1)):
                copy_product(i, dst)
            act.wait_ge(ch_y, 1)
            for b in range(2):
                nc.scalar.activation(slot[12][:, 2 * b:2 * b + 2, :],
                                     ps[:, 4 + b, :].rearrange("p (b t) -> p b t", b=2), ACT.Copy).then_inc(y_made, 1)
            for b in range(2):
                act.wait_ge(yc_made, b + 1)
                nc.scalar.activation(slot[13][:, 2 * b:2 * b + 2, :], slot[12][:, 2 * b:2 * b + 2, :],
                                     ACT.Square).then_inc(y_sq, 1)
            for b in range(2):
                act.wait_ge(y_var, b + 1)
                own.mark(nc.scalar.activation(slot[14][:, 2 * b:2 * b + 2, :],
                                              ps[:, b, :].rearrange("p (b t) -> p b t", b=2), ACT.Ln,
                                              bias=col("gn_eps")))
                own.wait()
                nc.scalar.activation(slot[14][:, 2 * b:2 * b + 2, :], slot[14][:, 2 * b:2 * b + 2, :], ACT.Exp,
                                     scale=-0.5).then_inc(y_rstd, 1)
            for b in range(2):
                act.wait_ge(ro_made, b + 1)
                nc.scalar.activation(xB[:, 4 + 2 * b:6 + 2 * b, 0, :], slot[15][:, 2 * b:2 * b + 2, :],
                                     ACT.Copy).then_inc(ro_hi, 1)
            co = C0["hy_o"]
            split_hi(Chunk(co + 1).ahead())
            square(N_FF2, 0)
            split_hi(Chunk(co + 2).ahead())
            for b in range(1, 4):
                square(N_FF2, b)
            split_hi(Chunk(co + 3).ahead())
            root_norm(N_FF2)
            round_x(OUT_FF2, xB)
            ffn(2, N_FF2)
            def ple(i):
                n, o = (N_PL0, OUT_PL0) if i == 0 else (N_PL1, OUT_PL1)
                c0 = C0[f"pl_p{i}"]
                square_norm(n)
                round_x(o, xA)
                split_hi(Chunk(c0).ahead())
                for b in range(4):
                    if b < 3:
                        act.wait_ge(e_done, 3 * i + b + 1)
                    else:
                        act.wait_ge(chunk_used, c0 + 1)
                    nc.scalar.activation(pl_sq[:, 2 * b:2 * b + 2, :], ps[:, b, :].rearrange("p (b t) -> p b t", b=2),
                                         ACT.Square).then_inc(e_evac, 1)
                act.wait_ge(e_ss, i + 1)
                inverse_root(pl_rb[:], half(5, 1), D, e_rs)
                for g in range(4):
                    c = Chunk(c0 + 1 + g)
                    if g < 3:
                        split_hi(c.ahead())
                    act.wait_ge(chunk_used, c.count(1))
                    if g >= 2:
                        act.wait_ge(h_updated, 4 * (n if i == 0 else n) + g - 1)
                    nc.scalar.activation(pl_sg[g % 2][:], ps[:, GATE_BANK[g], :].rearrange("p (b t) -> p b t", b=2),
                                         ACT.Sigmoid).then_inc(g_on, 1)
                    if g == 3:
                        nc.scalar.preload_act_table_set("natural_log_exp_and_others")
                    for b in ((), (0,), (1,), (2, 3))[g]:
                        square(n + 1, b, preload=False)
                split_hi(c.ahead())
                root_norm(n + 1)

            ple(0)
            c0 = C0["ml_d"]

            def latent(g):
                act.wait_ge(raw_scaled, SCALED_AT[N_ML] + g + 1)
                n = 2 if g < 2 else 1
                two = ps[:, g, 0:n * T].rearrange("p (b t) -> p b t", b=n)
                nc.scalar.activation(ml_c[:, 2 * g:2 * g + n, :], two, ACT.Copy)
                nc.scalar.activation(xt[:, 2 * g:2 * g + n, :], two, ACT.Square).then_inc(c_evac, 1)

            def latent_norm(j):
                act.wait_ge(c_ss, j + 1)
                inverse_root(ml_rs[j], half(4 + j, 0), (384, 256)[j], c_rs)
                for k in ((0, 1, 2), (3, 4))[j]:
                    act.wait_ge(c_made, k + 1)
                    nc.scalar.activation(xA[:, k, 0, :], xt[:, k, :], ACT.Copy).then_inc(c_hi, 1)

            split_hi(Chunk(c0).ahead())
            act.wait_ge(cs_arg, 1)
            nc.scalar.activation(ml_cs[:], ml_ang, ACT.Sin).then_inc(cs_made, 1)
            nc.scalar.preload_act_table_set("natural_log_exp_and_others")
            latent(0)
            latent(1)
            latent_norm(0)
            split_hi(Chunk(c0 + 1).ahead())
            latent(2)
            latent_norm(1)
            for g in range(20):
                if g == 14:
                    act.wait_ge(fold_done, 1)
                    src = ps[64:128, 6, 0:T].unsqueeze(1).broadcast_to([64, HEADS // 2, T])
                    nc.scalar.activation(ml_k[64:128, 0:HEADS // 2, :], src, ACT.Copy).then_inc(kr_spread, 1)
                wait_up(act, g)
                two = ps[:, g % 4, :].rearrange("p (b t) -> p b t", b=2)
                if g < 8:
                    ins = nc.scalar.activation(ml_q[0:64, 2 * g:2 * g + 2, :], two[0:64], ACT.Copy, scale=-MLA_SCALE)
                elif g < 16:
                    ins = nc.scalar.activation(ml_k[0:64, 2 * (g - 8):2 * (g - 8) + 2, :], two[0:64], ACT.Copy)
                else:
                    t, n = divmod(g - 16, 2)
                    ins = nc.scalar.activation(ml_v[:, t, 512 * n:512 * n + 512], ps[:, g % 4, :], ACT.Copy)
                ins.then_inc(ml_evac, 1)
                if g in ML_SPLITS:
                    split_hi(Chunk(C0["ml_q"] - 1 + ML_SPLITS.index(g)).ahead())
            attention(1, ml_pr, ml_pt, ml_st)
            split_and_square("ml_o", N_FF3)
            round_x(OUT_FF3, xB)
            ffn(3, N_FF3)
            ple(1)

        @block.vector
        def _(dve):
            own = Own(dve, dve_own)

            def link(ins):
                own.mark(ins)
                own.wait()

            def split_lo(c):
                if c is None:
                    return
                dve.wait_ge(hi_made, c.count(1))
                nc.vector.tensor_tensor(w_lo[c.slot][:], raw[c.slot][:], w_hi[c.slot][:].bitcast(F32),
                                        ALU.subtract).then_inc(lo_made, 1)

            def root(n):
                dve.wait_ge(rs_made, n + 1)

            def refine(y, sums, width, tmp):
                link(nc.vector.tensor_tensor(tmp, y, y, ALU.mult))
                link(nc.vector.scalar_tensor_tensor(out=tmp, in0=sums, scalar=EPS * width, in1=tmp, op0=ALU.add, op1=ALU.mult))
                link(nc.vector.tensor_scalar(tmp, tmp, -0.5 / width, 1.5, ALU.mult, ALU.add))
                link(nc.vector.tensor_tensor(y, y, tmp, ALU.mult))

            def rest_x(o, dst, u):
                lo, hi = UNITS[u]
                dve.wait_ge(x_hi_made, 5 * o + u + 1)
                nc.vector.tensor_tensor(dst[:, lo:hi, 1, :], xt[:, lo:hi, :], dst[:, lo:hi, 0, :].bitcast(F32),
                                        ALU.subtract).then_inc(x_lo_made, 1)

            rest_after = {2: 0, 3: 1, 5: 2, 7: 3}

            def scale_x(o, dst, gain, ahead=()):
                for k in range(KD):
                    nc.vector.scalar_tensor_tensor(out=xt[:, k, :], in0=hT[:, k, :], scalar=col(gain, k), in1=rs[:],
                                                   op0=ALU.mult, op1=ALU.mult).then_inc(xt_made, 1)
                    if k in rest_after:
                        rest_x(o, dst, rest_after[k])
                rest_x(o, dst, 4)
                for c in ahead:
                    split_lo(Chunk(c))

            def rest_early(n, b):
                dve.wait_ge(raw_hi, 4 * EARLY_AT[n] + b + 1)
                for k in (2 * b, 2 * b + 1):
                    last = nc.vector.scalar_tensor_tensor(out=early_tile(n)[:, k, 1, :], in0=hT[:, k, :],
                                                          scalar=col(EARLY[n][0], k),
                                                          in1=early_tile(n)[:, k, 0, :].bitcast(F32), op0=ALU.mult,
                                                          op1=ALU.subtract)
                last.then_inc(raw_lo, 1)

            def scale_early(n, i, c, bank):
                dve.wait_ge(chunk_used, c + 1)
                two = ps[:, bank, :].rearrange("p (b t) -> p b t", b=2)
                nc.vector.tensor_tensor(two, two, rs[:].unsqueeze(1).broadcast_to([P, 2, T]),
                                        ALU.mult).then_inc(raw_scaled, 1)

            def add_quarter(b, bank):
                nc.vector.tensor_tensor(hT[:, 2 * b:2 * b + 2, :], hT[:, 2 * b:2 * b + 2, :],
                                        ps[:, bank, :].rearrange("p (b t) -> p b t", b=2),
                                        ALU.add).then_inc(h_updated, 1)

            def add_projection(name, n, splits=True):
                for g in range(4):
                    if splits or g == 1:
                        split_lo(Chunk(C0[name] + g).ahead())
                    dve.wait_ge(chunk_used, C0[name] + g + 1)
                    add_quarter(g, 4 + g)
                    if g:
                        rest_early(n, g - 1)
                rest_early(n, 3)

            def ffn(f, n):
                c0, base, both = C0[f"up{f}"], PAIRS * f, f < 2
                goff = KF if both else 0
                nblk = 2 * KF if both else KF
                taps = 4 if both else 2
                tap0 = 4 * PAIRS * min(f, 2) + 2 * PAIRS * max(f - 2, 0)

                def convolve(acc, bank, q, off, nth):
                    for b in range(2):
                        j = q * 2 + b
                        nc.vector.scalar_tensor_tensor(out=acc[:, b, 2:T], in0=half(bank, b)[:, 0:T - 2],
                                                       scalar=dcol(f"cw{f}", j, off), in1=acc[:, b, 2:T],
                                                       op0=ALU.mult, op1=ALU.add).then_inc(tap_done, 1)
                    for b in range(2):
                        j = q * 2 + b
                        dve.wait_ge(tap_done, q * taps + (tap0 + nth + b + 1))
                        last = nc.vector.scalar_tensor_tensor(out=acc[:, b, 1:T], in0=half(bank, b)[:, 0:T - 1],
                                                              scalar=dcol(f"cw{f}", j, off + nblk),
                                                              in1=acc[:, b, 1:T], op0=ALU.mult, op1=ALU.add)
                    return last

                def product(q, par):
                    dve.wait_ge(gate_on, q + (base + 1))
                    if both:
                        dve.wait_ge(up_conv, q + (base + 1))
                        up = up_acc[par][:]
                    else:
                        up = ps[:, 2 * par, :].rearrange("p (b t) -> p b t", b=2)
                        if isinstance(q, int) and q == 0:
                            dve.wait_ge(raw_scaled, SCALED_AT[n] + 1)
                        if not isinstance(q, int) or q >= 2:
                            dve.wait_ge(hid_lo, q + (base - 1))
                    nc.vector.tensor_tensor(up_acc[par][:], up, gate_acc[par][:], ALU.mult).then_inc(prod_made, 1)

                def rest_hid(q, par):
                    dve.wait_ge(hid_hi, q + (base + 1))
                    nc.vector.tensor_tensor(rows(hid, q * 2, 2, 1), up_acc[par][:], rows(hid, q * 2, 2, 0).bitcast(F32),
                                            ALU.subtract).then_inc(hid_lo, 1)

                def pair(q, par, cu, cg, first=False):
                    split_lo(cu.ahead())
                    if first:
                        for i in range(2):
                            scale_early(n, i, c0 + i, i)
                    if both:
                        dve.wait_ge(up_lin, q + (base + 1))
                        convolve(up_acc[par], 2 * par, q, 0, 0).then_inc(up_conv, 1)
                    if not first:
                        product(q - 1, 1 - par)
                    split_lo(cg.ahead())
                    dve.wait_ge(gate_lin, q + (base + 1))
                    convolve(gate_acc[par], 2 * par + 1, q, goff, taps - 2).then_inc(gate_conv, 1)
                    if not first:
                        rest_hid(q - 1, 1 - par)

                pair(0, 0, Chunk(c0), Chunk(c0 + 1), first=True)
                pair(1, 1, Chunk(c0 + 2), Chunk(c0 + 3))
                pair(2, 0, Chunk(c0 + 4), Chunk(c0 + 5))
                with dve.Fori(0, (PAIRS - 3) // 2) as it:
                    for j in range(2):
                        pair(it * 2 + (3 + j), (3 + j) % 2, Chunk(c0 + 6 + 2 * j, it), Chunk(c0 + 7 + 2 * j, it))
                product(PAIRS - 1, (PAIRS - 1) % 2)
                rest_hid(PAIRS - 1, (PAIRS - 1) % 2)
                d0 = C0[f"dn{f}"]
                with dve.Fori(0, 2) as it:
                    for s in range(RING):
                        split_lo(Chunk(d0 + s, it).ahead())
                if f >= 2:
                    dve.wait_ge(p_hi, f - 1)
                    nc.vector.tensor_tensor(pl_x[:, :, 1, :], pl_in[:], pl_x[:, :, 0, :].bitcast(F32),
                                            ALU.subtract).then_inc(p_lo, 1)
                for s in range(8, PAIRS):
                    split_lo(Chunk(d0 + s).ahead())
                for b in range(4):
                    if b < 3:
                        dve.wait_ge(down_bank, 3 * f + b + 1)
                    else:
                        dve.wait_ge(chunk_used, d0 + PAIRS)
                    add_quarter(b, 4 + b)
                    if n + 1 in EARLY and b:
                        rest_early(n + 1, b - 1)
                if n + 1 in EARLY:
                    rest_early(n + 1, 3)

            def attention(a, pr, st, bias):
                h0, m0 = HEADS * a, KD * a

                def biased_max(h):
                    dve.wait_ge(scored, h0 + h + 1)
                    if h >= 3:
                        dve.wait_ge(prob_turned, h0 + h - 2)
                    for t, (lo, hi) in enumerate(((0, P), (P, 384))):
                        last = nc.vector.tensor_tensor_reduce(
                            pr[h % 3][:, lo:hi], ps[:, h % 2, lo:hi], bias(h, t), 1.0, 3e38, ALU.add, ALU.min,
                            st[:, 0, 2 * h + t:2 * h + t + 1])
                    last.then_inc(max_made, 1)

                def normalise(h):
                    dve.wait_ge(exp_made, h0 + h + 1)
                    link(nc.vector.reciprocal(st[:, 2, 2 * h:2 * h + 2], st[:, 1, 2 * h:2 * h + 2]))
                    for t, (lo, hi) in enumerate(((0, P), (P, 384))):
                        last = nc.vector.tensor_scalar(pr[h % 3][:, lo:hi], pr[h % 3][:, lo:hi],
                                                       st[:, 2, 2 * h + t:2 * h + t + 1], None, ALU.mult)
                    last.then_inc(prob_made, 1)

                def rest_o(m):
                    dve.wait_ge(o_hi, m0 + m + 1)
                    nc.vector.tensor_tensor(xB[:, m, 1, :], half(4 + m % 4, 0), xB[:, m, 0, :].bitcast(F32),
                                            ALU.subtract).then_inc(o_lo, 1)

                for i in range(HEADS + 5):
                    if i < HEADS:
                        biased_max(i)
                    if 1 <= i <= HEADS:
                        normalise(i - 1)
                    if i >= 6 and i % 2 == 0:
                        rest_o((i - 6) // 2)

            split_lo(Chunk(0))
            dve.wait_ge(vec_landed, 16)
            root(N_GM)
            scale_x(OUT_GM, xA, "a_norm", ahead=range(1, AHEAD))
            for g in range(8):
                split_lo(Chunk(g).ahead())
                if g < 4:
                    dve.wait_ge(gm_evac, g + 1)
                    for t in range(2):
                        own.mark(nc.vector.tensor_tensor_reduce(
                            gm_junk[:], vnat[:, t, T * g:T * g + T], vnat[:, t, T * g:T * g + T], 1.0, 0.0, ALU.mult,
                            ALU.add, gm_sum[:, 4 * t + g:4 * t + g + 1]))
                        own.wait()
                if g == 3:
                    nc.vector.tensor_reduce(gm_rs[:, 2:4], gm_sum[:].rearrange("p (t g) -> p t g", t=2), AX_X,
                                            ALU.add).then_inc(gm_sums, 1)
            dve.wait_ge(gm_std, 1)
            for t in range(2):
                nc.vector.tensor_scalar(vnat[:, t, :], vnat[:, t, :], gm_rs[:, t:t + 1], None,
                                        ALU.mult).then_inc(gm_scaled, 1)
            dve.wait_ge(gm_evac, 8)
            for k in range(KD):
                dve.wait_ge(gm_mixed, k // 2 + 1)
                if k == 0:
                    dve.wait_ge(gm_landed, 32)
                xk = xt[:, k, :].rearrange("p (n i) -> p n i", n=2)
                link(nc.vector.scalar_tensor_tensor(
                    out=xk, in0=half(4 + k // 2, k % 2).rearrange("p (n i) -> p n i", n=2), scalar=col("a_vnorm", k),
                    in1=bsb[:, k:k + 1, :].broadcast_to([P, 2, P]), op0=ALU.mult, op1=ALU.add))
                nc.vector.tensor_tensor(xt[:, k, :], xt[:, k, :], uT[:, k, :], ALU.mult).then_inc(xt_made, 1)
                if k in rest_after:
                    rest_x(OUT_GATED, xB, rest_after[k])
            rest_x(OUT_GATED, xB, 4)
            add_projection("gm_o", N_FF0)
            root(N_FF0)
            scale_x(OUT_FF0, xB, "f_norm0")
            ffn(0, N_FF0)
            root(N_AT)
            refine(rs[:], half(4, 0), D, at_pr[0][:, 0:T])
            scale_x(OUT_KV, xB, "kv_norm")
            early = EARLY[N_AT][1]
            for g in range(12):
                split_lo(Chunk(C0["at_k"] + g).ahead())
                if g < early:
                    scale_early(N_AT, g, C0["at_k"] + g, g)
                if g == early:
                    dve.wait_ge(x_lo_made, 5 * OUT_Q)
                    scale_x(OUT_Q, xA, "b_norm")
            dve.wait_ge(bias_ready, 1)
            attention(0, at_pr, at_st, lambda h, t: at_bias[:, h, P:T] if t == 0 else at_bias[:, h, :])
            add_projection("at_o", N_FF1)
            root(N_FF1)
            scale_x(OUT_FF1, xB, "f_norm1")
            ffn(1, N_FF1)
            root(N_FIN1)
            for k in range(KD):
                ins = nc.vector.scalar_tensor_tensor(out=hT[:, k, :], in0=hT[:, k, :], scalar=col("fin1", k), in1=rs[:],
                                                     op0=ALU.mult, op1=ALU.mult)
                if k % 2:
                    ins.then_inc(h_updated, 1)
            nc.vector.tensor_scalar(om_mu[:], col("rw_mu", 0, 15), -1.0, 1.0, ALU.mult, ALU.add).then_inc(mu_ready, 1)
            dve.wait_ge(h_updated, 20)
            for b in range(4):
                rest_early(N_HY, b)
            root(N_HY)
            scale_x(OUT_HY, xA, "at_norm0")
            c0 = C0["hy"]

            def diagonal(tile):
                return tile[:].rearrange("p h (b q) -> p h b q", b=3)[:, :, 0:3:2, :]

            tri = h_tri.unsqueeze(1).unsqueeze(1).broadcast_to([P, 2, 2, P])

            def logs(u):
                dve.wait_ge(stick_made, u + 1)
                z = ps[:, 4 + 2 * (u % 2):6 + 2 * (u % 2), 0:384]
                if u >= 2:
                    dve.wait_ge(sb_mixed, u - 1)
                link(nc.vector.scalar_tensor_tensor(out=sb_ls[u % 2][:], in0=z, scalar=0.0, in1=sb_l[u % 2][:],
                                                    op0=ALU.min, op1=ALU.subtract))
                link(nc.vector.tensor_tensor(sb_l[u % 2][:], sb_ls[u % 2][:], z, ALU.subtract))
                nc.vector.tensor_tensor(diagonal(sb_l[u % 2]), diagonal(sb_l[u % 2]), tri, ALU.mult).then_inc(log_made, 1)

            def arguments(u):
                dve.wait_ge(after_made, u + 1)
                nc.vector.tensor_tensor(sb_ls[u % 2][:], sb_ls[u % 2][:],
                                        ps[:, 4 + 2 * (u % 2):6 + 2 * (u % 2), 0:384], ALU.add).then_inc(arg_made, 1)
                dve.wait_ge(w_made, u + 1)
                nc.vector.tensor_tensor(diagonal(sb_ls[u % 2]), diagonal(sb_ls[u % 2]), tri, ALU.mult).then_inc(w_masked, 1)

            def rest_sb(u):
                dve.wait_ge(sb_hi, u + 1)
                nc.vector.tensor_tensor(xB[:, u, 1, :], half(3, u % 2), xB[:, u, 0, :].bitcast(F32),
                                        ALU.subtract).then_inc(sb_lo, 1)

            dve.wait_ge(hy_landed, 32)
            for g in range(14):
                if g == 5:
                    for t in range(2):
                        dve.wait_ge(w_proj, t + 1)
                        nc.vector.tensor_tensor(flat(3)[:, 512 * t:512 * t + 512], ps[:, 2 + t, :], w0b[:],
                                                ALU.add).then_inc(w_arg, 1)
                elif g == 6:
                    for b in range(2):
                        dve.wait_ge(kk_ss, b + 1)
                        nc.vector.tensor_scalar(slot[9][:, 2 * b:2 * b + 2, :],
                                                ps[:, 6 + b, :].rearrange("p (b t) -> p b t", b=2), 1e-24, None,
                                                ALU.max).then_inc(kk_max, 1)
                split_lo(Chunk(c0 + g).ahead())
                if g == 4:
                    dve.wait_ge(hy_mixed, 4)
                    for b in range(RBLK):
                        last = nc.vector.tensor_scalar(slot[8][:, b, :], slot[1][:, b, :], col("rw_kk", b), None, ALU.mult)
                    last.then_inc(kk_made, 1)
                elif g == 8:
                    link(nc.vector.tensor_tensor(slot[4][:], slot[4][:], slot[8][:], ALU.mult))
                    dve.wait_ge(decay_made, 2)
                    for dst, by in ((8, 5), (4, 6), (1, 6)):
                        nc.vector.tensor_tensor(slot[dst][:], slot[dst][:], slot[by][:], ALU.mult).then_inc(factors, 1)
                elif g == 10:
                    dve.wait_ge(decay_made, 3)
                    nc.vector.tensor_tensor(slot[0][:], slot[0][:], slot[5][:], ALU.mult).then_inc(factors, 1)
                    nc.vector.tensor_copy(pend[:], slot[5][:].rearrange("p b (c t) -> p b c t", c=NRCH)[:, :, :, RCH - 1]).then_inc(factors, 1)
                elif g == 12:
                    for b in range(2):
                        dve.wait_ge(rk_sum, b + 1)
                        nc.vector.tensor_tensor(slot[9][:, 2 * b:2 * b + 2, :],
                                                ps[:, 6 + b, :].rearrange("p (b t) -> p b t", b=2),
                                                slot[2][:, 2 * b:2 * b + 2, :], ALU.mult).then_inc(bonus_made, 1)
                if g < EARLY[N_HY][1]:
                    scale_early(N_HY, g, c0 + g, hy_bank(g))
                if g < 8:
                    dve.wait_ge(hy_lin, g + 1)
                    for b in range(2 if g < 7 else 1):
                        dst = mixed_block(2 * g + b)
                        last = nc.vector.scalar_tensor_tensor(out=dst[:, 1:T], in0=half(hy_bank(g), b)[:, 0:T - 1],
                                                              scalar=col("rw_mu", 2 * g + b), in1=dst[:, 1:T],
                                                              op0=ALU.mult, op1=ALU.add)
                    last.then_inc(hy_mixed, 1)
                if g == 7:
                    dve.wait_ge(kk_rn, 1)
                    link(nc.vector.tensor_tensor(slot[8][:], slot[8][:], slot[9][:], ALU.mult))
                    dve.wait_ge(a_sig, 1)
                    for b in range(RBLK):
                        own.mark(nc.vector.tensor_scalar(slot[9][:, b, :], slot[4][:, b, :], -1.0, col("rw_ka", b),
                                                         ALU.add, ALU.mult))
                    own.wait()
                    link(nc.vector.scalar_tensor_tensor(out=slot[1][:], in0=slot[9][:], scalar=1.0, in1=slot[1][:],
                                                        op0=ALU.add, op1=ALU.mult))
                    for b in range(RBLK):
                        last = nc.vector.scalar_tensor_tensor(out=slot[9][:, b, :], in0=slot[0][:, b, :],
                                                              scalar=col("rw_rk", b), in1=slot[1][:, b, :], op0=ALU.mult,
                                                              op1=ALU.mult)
                        if b % 2:
                            last.then_inc(rk_made, 1)
            logs(0)
            logs(1)
            arguments(0)
            arguments(1)
            logs(2)
            rest_sb(0)
            logs(3)
            rest_sb(1)

            def halves(i, b):
                return ps[:, product_bank(i, b), :].rearrange("p (m s) -> p m s", s=64)

            def part(d, b):
                return slot[d][:, 2 * b:2 * b + 2, :].rearrange("p b (c s) -> p (b c) s", s=64)

            def wide(mask):
                return mask.unsqueeze(1).broadcast_to([P, 8, 64])

            eye64 = hcon[:, HCON - 64:HCON]

            def masked(i, dsts):
                for b in range(2):
                    dve.wait_ge(mat_done, 2 * i + b + 1)
                    for dst, mask in dsts:
                        nc.vector.tensor_tensor(part(dst, b), halves(i, b), wide(mask), ALU.mult).then_inc(mat[i], 1)

            def with_eye(i, dsts):
                for b in range(2):
                    dve.wait_ge(mat_done, 2 * i + b + 1)
                    for dst, how in dsts:
                        if how == 0:
                            ins = nc.vector.tensor_copy(part(dst, b), halves(i, b))
                        else:
                            ins = nc.vector.scalar_tensor_tensor(out=part(dst, b), in0=halves(i, b), scalar=float(how),
                                                                 in1=wide(eye64), op0=ALU.mult, op1=ALU.add)
                        ins.then_inc(mat[i], 1)

            arguments(2)
            masked(3, ((7, m_d),))
            arguments(3)
            rest_sb(2)
            masked(4, ((10, m_dt), (15, m_ot)))
            rest_sb(3)
            split_lo(Chunk(C0["hy_o"]).ahead())
            masked(5, ((12, m_strict),))
            masked(6, ((13, m_incl),))
            masked(7, ((14, m_incl),))
            dve.wait_ge(mat[4], 4)
            for b in range(2):
                nc.vector.scalar_tensor_tensor(out=part(11, b), in0=part(10, b), scalar=-1.0, in1=wide(eye64),
                                               op0=ALU.mult, op1=ALU.add).then_inc(imdt_made, 1)
            with_eye(8, ((1, 0), (2, 1)))
            with_eye(10, ((7, 1),))
            with_eye(14, ((4, 0), (7, -1)))
            with_eye(16, ((11, 0), (15, 1)))
            with_eye(18, ((4, 1),))
            states = [flat(10)[:, 256 * i:256 * i + 256].rearrange("p (b i) -> p b i", b=RBLK) for i in range(3)]
            small = lambda bank: ps[:, bank, 0:256].rearrange("p (b i) -> p b i", b=RBLK)
            uall = slot[11][:].rearrange("p c (b i) -> p c b i", b=RBLK)
            for c in range(NRCH):
                dve.wait_ge(ch_x, c + 1)
                if c == 0:
                    dve.wait_ge(mat[20], 2)
                nc.vector.tensor_copy(states[2], small(0)).then_inc(ch_xs, 1)
                dve.wait_ge(ch_u, c + 1)
                nc.vector.tensor_scalar(uall[:, c], small(1), -1.0, None, ALU.mult).then_inc(ch_us, 1)
                if c == NRCH - 1:
                    break
                dve.wait_ge(ch_s, c + 1)
                fade = pend[:, :, c:c + 1].broadcast_to([P, RBLK, 64])
                if c == 0:
                    nc.vector.tensor_tensor(states[0], small(2), fade, ALU.mult).then_inc(ch_st, 1)
                else:
                    link(nc.vector.tensor_tensor(states[c % 2], states[(c - 1) % 2], small(2), ALU.add))
                    nc.vector.tensor_tensor(states[c % 2], states[c % 2], fade, ALU.mult).then_inc(ch_st, 1)
            for b in range(2):
                dve.wait_ge(y_mean, b + 1)
                y = slot[12][:, 2 * b:2 * b + 2, :]
                nc.vector.tensor_tensor(y, y, ps[:, b, :].rearrange("p (b t) -> p b t", b=2), ALU.subtract).then_inc(yc_made, 1)
            for b in range(2):
                dve.wait_ge(y_rstd, b + 1)
                for k in (2 * b, 2 * b + 1):
                    own.mark(nc.vector.scalar_tensor_tensor(out=slot[15][:, k, :], in0=slot[12][:, k, :],
                                                            scalar=col("rw_lnw", k), in1=slot[14][:, k, :], op0=ALU.mult,
                                                            op1=ALU.mult))
                own.wait()
                for k in (2 * b, 2 * b + 1):
                    own.mark(nc.vector.scalar_tensor_tensor(out=slot[15][:, k, :], in0=slot[15][:, k, :],
                                                            scalar=col("rw_lnb", k), in1=slot[9][:, k, :], op0=ALU.add,
                                                            op1=ALU.add))
                own.wait()
                dve.wait_ge(g_proj, b + 1)
                nc.vector.tensor_tensor(slot[15][:, 2 * b:2 * b + 2, :], slot[15][:, 2 * b:2 * b + 2, :],
                                        ps[:, 2 + b, :].rearrange("p (b t) -> p b t", b=2), ALU.mult).then_inc(ro_made, 1)
            for b in range(2):
                dve.wait_ge(ro_hi, b + 1)
                nc.vector.tensor_tensor(xB[:, 4 + 2 * b:6 + 2 * b, 1, :], slot[15][:, 2 * b:2 * b + 2, :],
                                        xB[:, 4 + 2 * b:6 + 2 * b, 0, :].bitcast(F32), ALU.subtract).then_inc(ro_lo, 1)
            add_projection("hy_o", N_FF2, splits=False)
            for g in (2, 3):
                split_lo(Chunk(C0["hy_o"] + g).ahead())
            root(N_FF2)
            scale_x(OUT_FF2, xB, "ff_norm0")
            ffn(2, N_FF2)

            def ple(i):
                n, o = (N_PL0, OUT_PL0) if i == 0 else (N_PL1, OUT_PL1)
                c0 = C0[f"pl_p{i}"]
                root(n)
                scale_x(o, xA, f"pl_gnorm{i}")
                split_lo(Chunk(c0).ahead())
                dve.wait_ge(e_rs, i + 1)
                for k in range(KD):
                    own.mark(nc.vector.scalar_tensor_tensor(out=pl_e[:, k, :], in0=half(k // 2, k % 2),
                                                            scalar=col(f"pl_norm{i}", k), in1=pl_rb[:], op0=ALU.mult,
                                                            op1=ALU.mult))
                own.wait()
                for g in range(4):
                    c = Chunk(c0 + 1 + g)
                    if g < 2:
                        split_lo(c.ahead())
                    dve.wait_ge(g_on, 4 * i + g + 1)
                    link(nc.vector.tensor_tensor(pl_sg[g % 2][:], pl_sg[g % 2][:], pl_e[:, 2 * g:2 * g + 2, :], ALU.mult))
                    nc.vector.tensor_tensor(hT[:, 2 * g:2 * g + 2, :], hT[:, 2 * g:2 * g + 2, :], pl_sg[g % 2][:],
                                            ALU.add).then_inc(h_updated, 1)
                    if n + 1 in EARLY and g:
                        rest_early(n + 1, g - 1)
                    if g == 2:
                        split_lo(c.ahead())
                if n + 1 in EARLY:
                    rest_early(n + 1, 3)
                split_lo(c.ahead())

            ple(0)
            dve.wait_ge(ml_landed, 32)
            two_pi = 2 * np.pi
            c1 = 6.28125
            c2 = float(np.float32(np.round((two_pi - c1) * 2 ** 20) / 2 ** 20))
            c3 = float(np.float32(two_pi - c1 - c2))
            magic = 1.5 * 2.0 ** 23
            link(nc.vector.tensor_copy(ml_ang, ml_pos[:]))
            link(nc.vector.tensor_scalar(ml_ang, ml_ang, col("freq"), None, ALU.mult))
            link(nc.vector.tensor_scalar(ml_n, ml_ang, 1.0 / two_pi, col("turn"), ALU.mult, ALU.add))
            link(nc.vector.tensor_scalar(ml_n, ml_n, magic, None, ALU.add))
            link(nc.vector.tensor_scalar(ml_n, ml_n, magic, None, ALU.subtract))
            for c in (c1, c2, c3):
                link(nc.vector.scalar_tensor_tensor(out=ml_ang, in0=ml_n, scalar=-c, in1=ml_ang, op0=ALU.mult, op1=ALU.add))
            link(nc.vector.tensor_scalar(ml_ang, ml_ang, col("phase"), None, ALU.add))
            lim = 3.1415925
            nc.vector.tensor_scalar(ml_ang, ml_ang, lim, -lim, ALU.min, ALU.max).then_inc(cs_arg, 1)
            root(N_ML)
            c0 = C0["ml_d"]

            def scale_latent(j):
                dve.wait_ge(c_rs, j + 1)
                refine(ml_rs[j], half(4 + j, 0), (384, 256)[j], ml_pr[2][:, 0:T])
                for k in ((0, 1, 2), (3, 4))[j]:
                    gain = col("q_norm", k) if j == 0 else col("c_norm", k - 3)
                    nc.vector.scalar_tensor_tensor(out=xt[:, k, :], in0=ml_c[:, k, :], scalar=gain, in1=ml_rs[j],
                                                   op0=ALU.mult, op1=ALU.mult).then_inc(c_made, 1)

            def rest_latent(j):
                for k in ((0, 1, 2), (3, 4))[j]:
                    dve.wait_ge(c_hi, k + 1)
                    nc.vector.tensor_tensor(xA[:, k, 1, :], xt[:, k, :], xA[:, k, 0, :].bitcast(F32),
                                            ALU.subtract).then_inc(c_lo, 1)

            scale_early(N_ML, 0, c0, 0)
            scale_early(N_ML, 1, c0 + 1, 1)
            split_lo(Chunk(c0).ahead())
            scale_latent(0)
            rest_latent(0)
            scale_early(N_ML, 2, c0 + 2, 2)
            split_lo(Chunk(c0 + 1).ahead())
            dve.wait_ge(cs_made, 1)
            dve.wait_ge(c_evac, 3)
            nc.vector.tensor_tensor(ml_kr[64:128, :], half(2, 1)[64:128], ml_cs[64:128, :], ALU.mult).then_inc(kr_made, 1)
            scale_latent(1)
            rest_latent(1)
            for g in range(20):
                if g == 14:
                    dve.wait_ge(fold_done, 2)
                    src = ps[64:128, 7, 0:T].unsqueeze(1).broadcast_to([64, HEADS // 2, T])
                    nc.vector.tensor_copy(ml_k[64:128, HEADS // 2:HEADS, :], src).then_inc(kr_spread, 1)
                if g < 8:
                    wait_up(dve, g)
                    nc.vector.scalar_tensor_tensor(
                        out=ml_q[64:128, 2 * g:2 * g + 2, :], in0=ps[64:128, g % 4, :].rearrange("p (b t) -> p b t", b=2),
                        scalar=-MLA_SCALE, in1=ml_cs[64:128, :].unsqueeze(1).broadcast_to([64, 2, T]), op0=ALU.mult,
                        op1=ALU.mult).then_inc(ml_rope, 1)
                if g in ML_SPLITS:
                    split_lo(Chunk(C0["ml_q"] - 1 + ML_SPLITS.index(g)).ahead())
            attention(1, ml_pr, ml_st, lambda h, t: ml_bias[:, P:T] if t == 0 else ml_bias[:, 0:T])
            add_projection("ml_o", N_FF3)
            root(N_FF3)
            scale_x(OUT_FF3, xB, "ff_norm1")
            ffn(3, N_FF3)
            ple(1)
            root(N_FIN2)
            for k in range(KD):
                nc.vector.scalar_tensor_tensor(out=xt[:, k, :], in0=hT[:, k, :], scalar=col("fin2", k), in1=rs[:],
                                               op0=ALU.mult, op1=ALU.mult).then_inc(xt_made, 1)

        @block.tensor
        def _(pe):
            def three(out, wh, wl, xh, xl, start, stop):
                nc.tensor.matmul(out, wh, xh, start=start, stop=False, skip_group_check=True)
                nc.tensor.matmul(out, wh, xl, start=False, stop=False, skip_group_check=True)
                return nc.tensor.matmul(out, wl, xh, start=False, stop=stop, skip_group_check=True)

            def three_natural(out, xh, xl, wh, wl, start, stop):
                nc.tensor.matmul(out, xh, wh, start=start, stop=False, skip_group_check=True)
                nc.tensor.matmul(out, xh, wl, start=False, stop=False, skip_group_check=True)
                return nc.tensor.matmul(out, xl, wh, start=False, stop=stop, skip_group_check=True)

            def plain(out, lhsT, rhs, start=True, stop=True):
                return nc.tensor.matmul(out, lhsT, rhs, start=start, stop=stop, skip_group_check=True)

            def weight(c, i, n=1):
                return w_hi[c.slot][:, P * i:P * (i + n)], w_lo[c.slot][:, P * i:P * (i + n)]

            def keep_clock(n, bank=6):
                for _ in range(n):
                    plain(ps[:, bank, 0:P], ones, ones)

            def sum_quarters(n, quarters, idle=True):
                for b in quarters:
                    if b == 1:
                        continue
                    if b == 0:
                        pe.wait_ge(sq_added, n + 1)
                    else:
                        if b == 3 and idle:
                            keep_clock(FILL[0])
                        pe.wait_ge(sq_made, 4 * n + b + 1)
                    for k in (2 * b, 2 * b + 1):
                        last = plain(half(4, 0), ones, xt[:, k, :], k == 0, k == KD - 1)
                if b == 3:
                    last.then_inc(ss_summed, 1)
                    if idle:
                        keep_clock(FILL[1])

            def wide_chunk(c, bank, x, ready=None, between={}, blocks=2):
                pe.wait_ge(lo_made, c.count(1))
                for k in range(KD):
                    if k in between:
                        between[k]()
                    if ready is not None:
                        ready(k, x_hi_made)
                        for part in range(2):
                            for b in range(blocks):
                                plain(half(bank, b), weight(c, 2 * k + b)[part], x[:, k, 0, :],
                                      k == 0 and b == 0 and part == 0, False)
                        ready(k, x_lo_made)
                        for b in range(blocks):
                            last = plain(half(bank, b), weight(c, 2 * k + b)[0], x[:, k, 1, :], False, k == KD - 1)
                        continue
                    for b in range(blocks):
                        last = three(half(bank, b), *weight(c, 2 * k + b), x[:, k, 0, :], x[:, k, 1, :],
                                     k == 0 and b == 0, k == KD - 1)
                last.then_inc(chunk_used, 1)

            def natural_chunk(c, bank, x, ready=None):
                pe.wait_ge(lo_made, c.count(1))
                for k in range(KD):
                    if ready is not None:
                        ready(k, x_lo_made)
                    for t in range(2):
                        last = three_natural(half(bank, t), x[:, k, 0, P * t:P * t + P], x[:, k, 1, P * t:P * t + P],
                                             *weight(c, 2 * k, 2), k == 0 and t == 0, k == KD - 1)
                last.then_inc(chunk_used, 1)

            def x_ready(o):
                def ready(k, made):
                    for u, (lo, _) in enumerate(UNITS):
                        if lo == k:
                            pe.wait_ge(made, 5 * o + u + 1)
                return ready

            def early_ready(n):
                def ready(k, made):
                    if k % 2 == 0:
                        pe.wait_ge(raw_hi if made is x_hi_made else raw_lo, 4 * EARLY_AT[n] + k // 2 + 1)
                return ready

            def early_chunk(n, c, bank):
                wide_chunk(c, bank, early_tile(n), early_ready(n), {5: lambda: sum_quarters(n, range(4), idle=False)})

            def ffn(f, n, o):
                c0, base, both = C0[f"up{f}"], PAIRS * f, f < 2
                up_used = up_conv if both else prod_made

                def pair(q, par, cu, cg, ready=None):
                    if ready is None:
                        pe.wait_ge(up_used, q + (base - 1))
                    wide_chunk(cu, 2 * par, xB, ready)
                    if ready is None:
                        pe.wait_ge(gate_conv, q + (base - 1))
                    wide_chunk(cg, 2 * par + 1, xB)

                def down(d, c, start=False, stop=False):
                    pe.wait_ge(lo_made, c.count(1))
                    pe.wait_ge(hid_lo, d + (base + 1))
                    for b in range(KD):
                        for k in range(2):
                            if isinstance(d, int):
                                xh, xl = hid[:, 2 * d + k, 0, :], hid[:, 2 * d + k, 1, :]
                            else:
                                xh, xl = [rows(hid, d * 2 + k, 1, i).rearrange("p a t -> p (a t)") for i in range(2)]
                            last = three(half(4 + b // 2, b % 2), *weight(c, KD * k + b), xh, xl,
                                         start and k == 0 and b % 2 == 0, stop and k == 1)
                        if stop and b % 2 and b < KD - 1:
                            last.then_inc(down_bank, 1)
                    last.then_inc(chunk_used, 1)

                early_chunk(n, Chunk(c0), 0)
                wide_chunk(Chunk(c0 + 1), 1, early_tile(n))
                pair(1, 1, Chunk(c0 + 2), Chunk(c0 + 3), x_ready(o))
                pair(2, 0, Chunk(c0 + 4), Chunk(c0 + 5))
                with pe.Fori(0, (PAIRS - 3) // 2) as it:
                    for j in range(2):
                        pair(it * 2 + (3 + j), (3 + j) % 2, Chunk(c0 + 6 + 2 * j, it), Chunk(c0 + 7 + 2 * j, it))
                d0 = C0[f"dn{f}"]
                down(0, Chunk(d0), start=True)
                with pe.Fori(0, 2) as it:
                    for s in range(RING):
                        down(it * RING + (1 + s), Chunk(d0 + 1 + s, it))
                down(9, Chunk(d0 + 9))
                down(10, Chunk(d0 + 10), stop=True)

            def attention(a, q, k, v, pr, pt):
                h0, m0 = HEADS * a, KD * a

                def scores(h):
                    if h >= 2:
                        pe.wait_ge(max_made, h0 + h - 1)
                    plain(ps[:, h % 2, 0:P], q(h)[:, 0:P], k(h)[:, 0:P])
                    plain(ps[:, h % 2, P:384], q(h)[:, P:T], k(h)).then_inc(scored, 1)

                def turn(h):
                    pe.wait_ge(prob_made, h0 + h + 1)
                    if h >= 2:
                        pe.wait_ge(turned_copied, h0 + h - 1)
                    for i in range(3):
                        last = nc.tensor.transpose(ps[:, 2 + h % 2, P * i:P * i + P], pr[h % 3][:, P * i:P * i + P], eye)
                    last.then_inc(prob_turned, 1)

                def mix(h):
                    pe.wait_ge(turned_copied, h0 + h + 1)
                    m, r = h // 2, 64 * (h % 2)
                    if m >= 4 and h % 2 == 0:
                        pe.wait_ge(o_lo, m0 + m - 3)
                    out = half(4 + m % 4, 0)[r:r + 64]
                    plain(out, v[:, 0, 64 * h:64 * h + 64], pt[h % 2][:, 0:T], stop=False)
                    plain(out[:, P:T], v[:, 1, 64 * h:64 * h + 64], pt[h % 2][:, T:384], start=False).then_inc(mixed, 1)

                for i in range(HEADS + 3):
                    if i == 2:
                        keep_clock(2)
                    if i < HEADS:
                        scores(i)
                    if i == 2:
                        keep_clock(4)
                    if 2 <= i <= HEADS + 1:
                        turn(i - 2)
                    if i >= 3:
                        mix(i - 3)

            def project(name, x, ready):
                for g in range(4):
                    wide_chunk(Chunk(C0[name] + g), 4 + g, x, ready if g == 0 else None)

            pe.wait_ge(eye_landed, 16)
            keep_clock(8)
            sum_quarters(N_GM, range(4))
            for g in range(4):
                natural_chunk(Chunk(g), g, xA, x_ready(OUT_GM) if g == 0 else None)
            for g in range(4, 8):
                pe.wait_ge(gm_evac, g - 3)
                wide_chunk(Chunk(g), g % 4, xA)
            pe.wait_ge(gm_masked, 1)
            pe.wait_ge(gm_scaled, 2)
            for k in range(KD):
                for t in range(2):
                    last = plain(half(4 + k // 2, k % 2)[:, P * t:P * t + P], vnat[:, t, P * k:P * k + P], wsT[:, k, :])
                if k % 2:
                    last.then_inc(gm_mixed, 1)
            pe.wait_ge(xt_made, 8 * OUT_GATED + 2)
            project("gm_o", xB, x_ready(OUT_GATED))
            ffn(0, N_FF0, OUT_FF0)
            for g in range(12):
                if g >= 4:
                    pe.wait_ge(qkv_evac, g - 3)
                c = Chunk(C0["at_k"] + g)
                if g == 0:
                    early_chunk(N_AT, c, 0)
                elif g < EARLY[N_AT][1]:
                    wide_chunk(c, g, early_tile(N_AT))
                elif 4 <= g < 8:
                    natural_chunk(c, g % 4, xB)
                elif g < 4:
                    wide_chunk(c, g, xB, x_ready(OUT_KV) if g == EARLY[N_AT][1] else None)
                else:
                    wide_chunk(c, g % 4, xA, x_ready(OUT_Q) if g == 8 else None)
            keep_clock(4)
            pe.wait_ge(qkv_evac, 12)
            attention(0, lambda h: at_qT[64 * (h % 2):64 * (h % 2) + 64, h // 2, :],
                      lambda h: at_k[64 * (h % 2):64 * (h % 2) + 64, h // 2, :], at_v, at_pr, at_pt)
            pe.wait_ge(o_lo, 8)
            project("at_o", xB, None)
            ffn(1, N_FF1, OUT_FF1)
            keep_clock(10, 3)
            sum_quarters(N_FIN1, range(4))

            def stick_scores(u):
                if u >= 2:
                    pe.wait_ge(arg_made, u - 1)
                for i in range(2):
                    bank = 4 + 2 * (u % 2) + i
                    r = slice(64 * i, 64 * i + 64)
                    plain(ps[:, bank, 0:T], sb_k[r, u, 0:P], sb_q[r, u, :])
                    last = plain(ps[:, bank, T:384], sb_k[r, u, P:T], sb_q[r, u, P:T])
                last.then_inc(z_made, 1)

            def stick_after(u):
                pe.wait_ge(log_made, u + 1)
                for i in range(2):
                    bank = 4 + 2 * (u % 2) + i
                    plain(ps[:, bank, 0:384], h_after, sb_l[u % 2][:, i, :], stop=False)
                    last = plain(ps[:, bank, P:T], ones, sb_l[u % 2][:, i, T:384], start=False)
                last.then_inc(after_made, 1)

            def stick_mix(u):
                pe.wait_ge(w_masked, u + 1)
                if u >= 1:
                    pe.wait_ge(sb_lo, u)
                for i in range(2):
                    h, out = 2 * u + i, half(3, u % 2)[64 * i:64 * i + 64]
                    plain(out, sb_v[:, 0, 64 * h:64 * h + 64], sb_ls[u % 2][:, i, 0:T], stop=False)
                    last = plain(out[:, P:T], sb_v[:, 1, 64 * h:64 * h + 64], sb_ls[u % 2][:, i, T:384], start=False)
                last.then_inc(sb_mixed, 1)

            c0 = C0["hy"]
            def head_sums(bank, src, mat_, signal, ready):
                for b in range(RBLK):
                    ready(b)
                    last = plain(half(bank + b // 2, b % 2), mat_, slot[src][:, b, :])
                    if b % 2:
                        last.then_inc(signal, 1)

            for g in range(14):
                if 4 <= g < 6:
                    pe.wait_ge(hy_mixed, g - 3)
                elif 6 <= g < 10:
                    pe.wait_ge(hy_mixed, g - 1)
                elif g >= 10:
                    pe.wait_ge(hy_evac, g - 9)
                if g == 0:
                    early_chunk(N_HY, Chunk(c0), 0)
                elif g < EARLY[N_HY][1]:
                    wide_chunk(Chunk(c0 + g), hy_bank(g), early_tile(N_HY))
                elif g >= 12:
                    natural_chunk(Chunk(c0 + g), hy_bank(g), xA)
                else:
                    wide_chunk(Chunk(c0 + g), hy_bank(g), xA, x_ready(OUT_HY) if g == EARLY[N_HY][1] else None,
                               blocks=1 if g == 7 else 2)
                if g == 5:
                    pe.wait_ge(lora_landed, 16)
                    pe.wait_ge(lora_in, 1)
                    pe.wait_ge(hy_mixed, 4)
                    for t in range(2):
                        plain(ps[:, 2 + t, :], wlal[:, P * t:P * t + P], lora_w[:, 0, :]).then_inc(w_proj, 1)
                    for b in range(RBLK):
                        last = plain(half(4 + b // 2, b % 2), lora_w[:, 1, P * b:P * b + P], wlal[:])
                        if b % 2:
                            last.then_inc(a_proj, 1)
                elif g == 6:
                    pe.wait_ge(kk_sq, 1)
                    pe.wait_ge(hy_landed, 32)
                    head_sums(6, 9, h_sum, kk_ss, lambda b: None)
                    pe.wait_ge(w_sig, 2)
                    pe.wait_ge(a_sig, 1)
                    for t in range(2):
                        for b in range(RBLK):
                            last = plain(half(2 + b, t), flat(3)[:, 512 * t + P * b:512 * t + P * b + P], h_cum)
                    last.then_inc(cum_made, 1)
                elif g == 10:
                    pe.wait_ge(kk_max, 2)
                    head_sums(6, 9, h_sum, rk_sum, lambda b: pe.wait_ge(rk_made, b // 2 + 1) if b % 2 == 0 else None)

            def tile(d, hf, p, c):
                return slot[d][64 * hf:64 * hf + 64, p, RCH * c:RCH * c + RCH]

            def product(i, lhs, rhs, needs, used=None):
                for b in range(2):
                    for j, n in needs:
                        pe.wait_ge(mat[j], n * (b + 1))
                    if i >= 7:
                        pe.wait_ge(mat[i - 4], EVACS.get(i - 4, 1) * (b + 1))
                    elif i < BESIDE and 2 * i + b >= 3:
                        j, h = divmod(2 * i + b - 3, 2)
                        pe.wait_ge(mat[j], h + 1)
                    for p in (2 * b, 2 * b + 1):
                        for c in range(NRCH):
                            at = ((p % 2) * NRCH + c) * RCH
                            for hf in range(2):
                                out = ps[64 * hf:64 * hf + 64, product_bank(i, b), at:at + RCH]
                                right = eye[64 * hf:64 * hf + 64, 64 * hf:64 * hf + 64] if rhs is None else tile(rhs, hf, p, c)
                                last = plain(out, tile(lhs, hf, p, c), right)
                    last.then_inc(mat_done, 1)

            pe.wait_ge(decay_made, 3)
            pe.wait_ge(bonus_made, 2)
            stick_scores(0)
            stick_scores(1)
            pe.wait_ge(factors, 5)
            pe.wait_ge(hy_evac, 6)
            product(0, 4, None, ())
            keep_clock(8, 3)
            stick_after(0)
            product(1, 1, None, ())
            stick_after(1)
            stick_scores(2)
            stick_scores(3)
            stick_mix(0)
            product(2, 2, None, ())
            stick_mix(1)
            stick_after(2)
            product(3, 8, 4, ())
            stick_after(3)
            product(4, 4, 8, ())
            pe.wait_ge(arg_made, 3)
            keep_clock(5, 4)
            stick_mix(2)
            keep_clock(8, 4)
            stick_mix(3)
            keep_clock(8, 4)
            pe.wait_ge(sb_lo, 4)
            pe.wait_ge(mat[1], 2)
            pe.wait_ge(mat[2], 2)
            pe.wait_ge(mat[4], 2)
            product(5, 1, 8, ())
            product(6, 4, 0, ())
            product(7, 1, 0, ())
            pe.wait_ge(mat[4], 4)
            product(8, 10, 7, ((3, 1), (4, 2)))
            product(9, 7, 10, ((3, 1), (4, 2)))
            product(10, 4, 1, ((8, 2), (9, 1)))
            pe.wait_ge(imdt_made, 2)
            product(11, 2, 11, ((8, 2),))
            product(12, 7, 10, ((10, 1), (11, 1)))
            product(13, 1, None, ((12, 1),))
            product(14, 15, 2, ((13, 1),))
            product(15, 2, 15, ((13, 1),))
            product(16, 10, 4, ((14, 2), (15, 1)))
            product(17, 4, 10, ((14, 2), (15, 1)))
            product(18, 2, 11, ((16, 2), (17, 1)))
            product(19, 7, 1, ((14, 2), (12, 1)))
            product(20, 15, 10, ((16, 2), (19, 1)))
            product(21, 4, 7, ((18, 1), (20, 1)))
            for i in range(18, 22):
                pe.wait_ge(mat[i], 2)
            pe.wait_ge(mat[2], 2)

            def each():
                for p in range(RBLK):
                    for hf in range(2):
                        yield p, slice(64 * hf, 64 * hf + 64), hf

            def state(i, p, s):
                return flat(10)[s, 256 * i + 64 * p:256 * i + 64 * p + 64]

            co = [Chunk(C0["hy_o"] + g) for g in range(4)]

            def out_rows(g, k):
                for b in range(2):
                    last = three(half(4 + g, b), *weight(co[g], 2 * k + b), xB[:, k, 0, :], xB[:, k, 1, :],
                                 k == 0 and b == 0, k == KD - 1)
                return last

            pe.wait_ge(lo_made, co[3].count(1))
            fill = [(g, k) for g in (2, 3) for k in range(4)]
            for c in range(NRCH):
                if c:
                    pe.wait_ge(ch_st, c)
                for p, s, hf in each():
                    last = plain(ps[s, 0, 64 * p:64 * p + 64], tile(12, hf, p, c), tile(6, hf, p, c), stop=c == 0)
                    if c:
                        last = plain(ps[s, 0, 64 * p:64 * p + 64], tile(8, hf, p, c), state((c - 1) % 2, p, s), start=False)
                last.then_inc(ch_x, 1)
                out_rows(*fill[2 * c])
                pe.wait_ge(ch_xs, c + 1)
                for p, s, hf in each():
                    last = plain(ps[s, 1, 64 * p:64 * p + 64], tile(1, hf, p, c), state(2, p, s))
                last.then_inc(ch_u, 1)
                out_rows(*fill[2 * c + 1])
                pe.wait_ge(ch_us, c + 1)

                def u(p, s):
                    return slot[11][s, c, 64 * p:64 * p + 64]

                if c < NRCH - 1:
                    for p, s, hf in each():
                        plain(ps[s, 2, 64 * p:64 * p + 64], tile(3, hf, p, c), u(p, s), stop=False)
                        last = plain(ps[s, 2, 64 * p:64 * p + 64], tile(5, hf, p, c), tile(6, hf, p, c), start=False)
                    last.then_inc(ch_s, 1)
                for p, s, hf in each():
                    out = ps[s, 4 + p // 2, T * (p % 2) + RCH * c:T * (p % 2) + RCH * c + RCH]
                    if c:
                        plain(out, state((c - 1) % 2, p, s), tile(0, hf, p, c), stop=False)
                    plain(out, u(p, s), tile(13, hf, p, c), start=c == 0, stop=False)
                    last = plain(out, tile(6, hf, p, c), tile(14, hf, p, c), start=False)
            last.then_inc(ch_y, 1)
            for b in range(RBLK):
                for k in range(2):
                    last = plain(half(2 + b // 2, b % 2), lora_w[:, 2 + k, P * b:P * b + P], gl[:, k, :], k == 0, k == 1)
                if b % 2:
                    last.then_inc(g_proj, 1)
            head_sums(0, 12, h_mean, y_mean, lambda b: pe.wait_ge(y_made, b // 2 + 1) if b % 2 == 0 else None)
            for k in range(4):
                out_rows(0, k)
            head_sums(0, 13, h_mean, y_var, lambda b: pe.wait_ge(y_sq, b // 2 + 1) if b % 2 == 0 else None)
            for k in range(4):
                out_rows(1, k)
            for g in range(4):
                for k in range(4, KD):
                    if g == 0 and k % 2 == 0:
                        pe.wait_ge(ro_lo, k // 2 - 1)
                    last = out_rows(g, k)
                last.then_inc(chunk_used, 1)
            ffn(2, N_FF2, OUT_FF2)

            def ple(i):
                n, o = (N_PL0, OUT_PL0) if i == 0 else (N_PL1, OUT_PL1)
                c = Chunk(C0[f"pl_p{i}"])
                pe.wait_ge(p_lo, i + 1)
                pe.wait_ge(lo_made, c.count(1))
                for b in range(KD):
                    if b == 5:
                        sum_quarters(n, range(4), idle=False)
                    for k in range(2):
                        last = three(half(b // 2, b % 2), *weight(c, KD * k + b), pl_x[:, k, 0, :], pl_x[:, k, 1, :],
                                     k == 0, k == 1)
                    if b % 2 and b < KD - 1:
                        last.then_inc(e_done, 1)
                last.then_inc(chunk_used, 1)
                for g in range(4):
                    if g == 3:
                        pe.wait_ge(e_rs, i + 1)
                    early = {}
                    if g == 3 and n + 1 not in EARLY:
                        early = {7: lambda: sum_quarters(n + 1, (0, 1))}
                    wide_chunk(Chunk(C0[f"pl_g{i}"] + g), GATE_BANK[g], xA, x_ready(o) if g == 0 else None, early)
                    if g == 0:
                        pe.wait_ge(e_evac, 4 * i + 4)
                        for k in range(KD):
                            last = plain(half(5, 1), ones, pl_sq[:, k, :], k == 0, k == KD - 1)
                        last.then_inc(e_ss, 1)

            ple(0)
            def latent_sums(j):
                ks = ((0, 1, 2), (3, 4))[j]
                for k in ks:
                    pe.wait_ge(c_evac, k // 2 + 1)
                    last = plain(half(4 + j, 0), ones, xt[:, k, :], k == ks[0], k == ks[-1])
                last.then_inc(c_ss, 1)

            for g in range(3):
                c = Chunk(C0["ml_d"] + g)
                if g == 0:
                    early_chunk(N_ML, c, 0)
                else:
                    wide_chunk(c, g, early_tile(N_ML), None, {3: lambda: latent_sums(0)} if g == 2 else {})
            for kn, name, k0 in ((3, "ml_q", 0), (2, "ml_k", 3)):
                for i in range(HEADS * kn):
                    h, k = divmod(i, kn)
                    if kn == 3 and i == 6:
                        latent_sums(1)
                    c = Chunk(C0[name] + i // 16)
                    if i % 16 == 0:
                        pe.wait_ge(lo_made, c.count(1))
                    if h % 2 == 0 and k == 0:
                        g = h // 2 + (8 if kn == 2 else 0)
                        if g == 2:
                            pe.wait_ge(kr_made, 1)
                        elif g == 4:
                            for bank in (6, 7):
                                plain(ps[:, bank, 0:T], ml_fold[64:128, :], ml_kr[64:128, :]).then_inc(fold_done, 1)
                        if g >= 4:
                            pe.wait_ge(ml_evac, g - 3)
                            if g < 12:
                                pe.wait_ge(ml_rope, g - 3)
                    if i < kn:
                        pe.wait_ge(c_lo, k0 + k + 1)
                    last = three(half(g % 4, h % 2), *weight(c, i % 16), xA[:, k0 + k, 0, :], xA[:, k0 + k, 1, :],
                                 k == 0, k == kn - 1)
                    if i % 16 == 15:
                        last.then_inc(chunk_used, 1)
                    elif h % 2 and k == kn - 1:
                        last.then_inc(up_done, 1)
            c = Chunk(C0["ml_v"])
            pe.wait_ge(lo_made, c.count(1))
            for i in range(4):
                t, n = divmod(i, 2)
                pe.wait_ge(ml_evac, 16 + i - 3)
                for k in range(2):
                    last = three_natural(ps[:, (16 + i) % 4, :], xA[:, 3 + k, 0, P * t:P * t + P], xA[:, 3 + k, 1, P * t:P * t + P],
                                         *weight(c, KD * k + 4 * n, 4), k == 0, k == 1)
                last.then_inc(chunk_used if i == 3 else up_done, 1)
            keep_clock(4)
            pe.wait_ge(ml_evac, 20)
            pe.wait_ge(ml_rope, 8)
            pe.wait_ge(kr_spread, 2)
            attention(1, lambda h: ml_q[:, h, :], lambda h: ml_k[:, h, :], ml_v, ml_pr, ml_pt)
            pe.wait_ge(o_lo, 16)
            project("ml_o", xB, None)
            ffn(3, N_FF3, OUT_FF3)
            ple(1)
            keep_clock(12)
            sum_quarters(N_FIN2, (2, 3), idle=False)


def _cols(v):
    v = np.asarray(v).reshape(-1)
    return v.reshape(-1, P).T


def _chunks(blocks):
    return blocks.transpose(0, 2, 1, 3).reshape(-1, P, CHUNK)


def _by_columns(w):
    n = w.shape[1] // 256
    return w.reshape(KD, P, n, 256).transpose(2, 1, 0, 3).reshape(n, P, CHUNK)


def _by_rows(w):
    n = w.shape[0] // 256
    return w.reshape(n, 2, P, D).transpose(0, 2, 1, 3).reshape(n, P, CHUNK)


def _paired(w):
    up, gate = _by_columns(w[:, :FF]), _by_columns(w[:, FF:])
    return np.stack([up, gate], 1).reshape(-1, P, CHUNK)


def _by_heads(w):
    k, h = w.shape[0] // P, w.shape[1] // P
    return _chunks(w.reshape(k, P, h, P).transpose(2, 0, 1, 3).reshape(-1, 16, P, P))


def _constants():
    i = np.arange(P)
    s = np.arange(64)
    eye, ones = np.eye(P), np.ones((P, P))
    after = (i[:, None] > i[None, :])
    tri = (i[:, None] < i[None, :])
    head = (i[:, None] // 64 == i[None, :] // 64)
    cum = head * (i[:, None] <= i[None, :]) * DECAY
    cum_x = head * (i[:, None] < i[None, :]) * DECAY
    d = (s[:, None] > s[None, :]) & (s[:, None] // 8 == s[None, :] // 8)
    dt = d.T
    ot = (s[:, None] < s[None, :]) & ~dt
    strict, incl = s[:, None] < s[None, :], s[:, None] <= s[None, :]
    small = [np.concatenate([m, m], 0) for m in (d, dt, ot, strict, incl, np.eye(64))]
    hyc = np.concatenate([eye, ones, after, tri, head, head / 64.0, cum, cum_x] + small, 1)
    causal = np.where(i[None, :] <= i[:, None], 0.0, -NEG)
    fold = (i[:, None] >= 64) & (i[:, None] % 32 == i[None, :] % 32)
    mlc = np.concatenate([np.zeros((P, P)), causal, fold], 1)
    return np.ascontiguousarray(hyc, np.float32), np.ascontiguousarray(mlc, np.float32)


def kernel(**inputs):
    import concourse.bacc as bacc
    from concourse.bass_utils import run_bass_kernel_spmd

    a = {k: np.asarray(v) for k, v in inputs.items()}
    f32 = np.float32

    def zeros(*shape):
        return np.zeros(shape, f32)

    hyb = a["hyb_w_in_2"][0]
    rw = hyb[:, 1536:]
    hyb = np.concatenate([rw[:, 1536:], zeros(D, 96), rw[:, 512:1024], rw[:, :512], rw[:, 1024:1536], zeros(D, P),
                          hyb[:, :1536]], 1)
    down = a["mla_w_down_2"][0]
    kr = down[:, 640:672]
    kr_swap = np.concatenate([kr[:, 16:], kr[:, :16]], 1)
    down = np.concatenate([down[:, :640], zeros(D, 64), kr, kr_swap], 1)
    uq = a["mla_w_uq_2"][0].reshape(384, HEADS, 96)
    uq = np.concatenate([uq, uq[:, :, 80:96], uq[:, :, 64:80]], 2).reshape(384, HEADS * P)
    ukv = a["mla_w_ukv_2"][0].reshape(256, HEADS, P)
    uk = np.concatenate([ukv[:, :, :64], zeros(256, HEADS, 64)], 2).reshape(256, HEADS * P)
    uv = np.ascontiguousarray(ukv[:, :, 64:]).reshape(256, HEADS * 64)
    a_in, kv = a["a_w_in"][0], a["w_kv"]
    parts = [_by_columns(a_in[:, D:]), _by_columns(a_in[:, :D]), _by_columns(a["a_w_out"][0]),
             _paired(a["f_w_in"][0]), _by_rows(a["f_w_down"][0]),
             _by_columns(kv[:, :D]), _by_columns(kv[:, D:]), _by_columns(a["b_w_q"][0]), _by_columns(a["b_w_o"][0]),
             _paired(a["f_w_in"][1]), _by_rows(a["f_w_down"][1]),
             _by_columns(hyb), _by_columns(a["hyb_w_out_2"][0]),
             _paired(a["ffn_w_in_2"][0]), _by_rows(a["ffn_w_out_2"][0]),
             _by_rows(a["ple_w_proj_2"][0]), _by_columns(a["ple_w_gate_2"][0]),
             _by_columns(down), _by_heads(uq), _by_heads(uk), _by_rows(uv), _by_columns(a["mla_w_o_2"][0]),
             _paired(a["ffn_w_in_2"][1]), _by_rows(a["ffn_w_out_2"][1]),
             _by_rows(a["ple_w_proj_2"][1]), _by_columns(a["ple_w_gate_2"][1])]
    stream = np.concatenate(parts, 0)

    half_freq = (f32(10000.0) ** (-np.arange(16, dtype=f32) / f32(16))).astype(f32)
    freq, phase = zeros(P), zeros(P)
    freq[64:128] = np.tile(half_freq, 4)
    phase[64:96], phase[96:112] = np.pi / 2, np.pi
    mu = a["rw_mu_2"][0]
    vecs = {
        "a_norm": a["a_norm_g"][0], "a_vnorm": a["a_v_norm_g"][0], "kv_norm": a["kv_norm_g"], "b_norm": a["b_norm_g"][0],
        "f_norm0": a["f_norm_g"][0], "f_norm1": a["f_norm_g"][1], "cw0": a["f_conv_w"][0], "cw1": a["f_conv_w"][1],
        "cb0": a["f_conv_b"][0], "cb1": a["f_conv_b"][1], "fin1": a["final_norm_g"],
        "at_norm0": a["attn_norm_2"][0], "at_norm1": a["attn_norm_2"][1], "ff_norm0": a["ffn_norm_2"][0],
        "ff_norm1": a["ffn_norm_2"][1], "cw2": a["ffn_conv_w_2"][0], "cw3": a["ffn_conv_w_2"][1],
        "cb2": a["ffn_conv_b_2"][0], "cb3": a["ffn_conv_b_2"][1], "pl_norm0": a["ple_norm_2"][0],
        "pl_norm1": a["ple_norm_2"][1], "pl_gnorm0": a["ple_gate_norm_2"][0], "pl_gnorm1": a["ple_gate_norm_2"][1],
        "rw_mu": np.concatenate([mu[1536:], zeros(96), mu[512:1024], mu[:512], mu[1024:1536]]), "rw_a0": a["rw_a0_2"][0], "rw_kk": a["rw_k_k_2"][0],
        "rw_ka": a["rw_k_a_2"][0], "rw_rk": a["rw_r_k_2"][0], "rw_lnw": a["rw_ln_w_2"][0], "rw_lnb": a["rw_ln_b_2"][0],
        "q_norm": a["mla_q_norm_2"][0], "c_norm": a["mla_kv_norm_2"][0], "fin2": a["final_norm_2"],
        "eps": zeros(P) + f32(EPS), "gn_eps": zeros(P) + f32(GN_EPS), "freq": freq, "turn": phase / f32(2 * np.pi),
        "phase": phase, "ln256": zeros(P) + f32(8 * np.log(2.0)),
    }
    packed = np.concatenate([_cols(vecs[name]) for name, _ in _VECS], 1).astype(f32)
    hyc, mlc = _constants()
    rel = a["b_rel_bias"][0][:, ::-1]
    ext = np.concatenate([np.repeat(rel[:, :1], P, 1), rel[:, :256]], 1)
    rel = np.lib.stride_tricks.sliding_window_view(ext, T, 1)[:, P:0:-1].transpose(1, 0, 2)
    lora = np.concatenate([a["rw_w2_2"][0], zeros(64, 512), zeros(64, 512), a["rw_a2_2"][0], a["rw_g2_2"][0],
                           zeros(96, 512)], 0).reshape(4, P, 512).transpose(1, 0, 2)
    arrays = {
        "stream": stream,
        "x_t": a["x"][0].T.reshape(KD, P, T).transpose(1, 0, 2),
        "vecs": packed,
        "wst": a["a_w_s"][0].transpose(2, 0, 1),
        "bsp": a["a_b_s"][0],
        "rel": rel, "hyc": hyc, "w0": a["rw_w0_2"], "lora": lora, "mlc": mlc, "pos": a["positions_2"],
        "p_t": a["p_2"][:, 0].transpose(0, 2, 1).reshape(2, 2, P, T).transpose(0, 2, 1, 3),
    }
    nc = bacc.Bacc("TRN2", target_bir_lowering=False, num_devices=1)
    args = []
    for name in arrays:
        arrays[name] = np.ascontiguousarray(arrays[name])
        args.append(nc.dram_tensor(name, arrays[name].shape, mybir.dt.from_np(arrays[name].dtype),
                                   kind="ExternalInput").ap())
    args.append(nc.dram_tensor("out_t", (P, KD, T), F32, kind="ExternalOutput").ap())
    build(nc, *args)
    r = run_bass_kernel_spmd(nc, [arrays], core_ids=[0])
    got = r.results[0]["out_t"]
    return np.ascontiguousarray(got.transpose(2, 1, 0).reshape(1, T, D))
```
